# Optimizing a Trainium2 kernel written in Bass

```python
import jax
import jax.numpy as jnp
from jax import lax
import numpy as np

D_MODEL = 1024
BATCH = 1
SEQ = 128
DEPTH = 2
DEC_BATCH = 1
DEC_SEQ = 1024
PAST_LEN = 128

GRID_W = 64
CHUNK = 64
N_EVEN = (DEPTH + 1) // 2
N_ODD = DEPTH // 2
H_M = 4
DK_M = 128
DV_M = 128
H_R = 4
DK_R = 128
DV_R = 128
H_G = 4
DK_G = 128
DV_G = 256
GLA_RANK = 16
GLA_TAU = 16.0
D_FF = 2816
EPS = 1e-6

MIX_EVEN = H_M * DV_M + H_R * DV_R
MIX_ODD = H_G * DV_G
EVEN_SIZES = (H_M * DK_M, H_M * DK_M, H_M * DV_M, H_M * DV_M, 4 * H_M,
              H_R * DK_R, H_R * DK_R, H_R * DV_R, H_R * DV_R)
ODD_SIZES = (H_G * DK_G, H_G * DK_G, H_G * DV_G, H_G * DV_G, 2 * GLA_RANK)
P_EVEN = sum(EVEN_SIZES)
P_ODD = sum(ODD_SIZES)

kernel_name = 'bidir_mlstm_retention_gla_diffusion_step'

def _split(x, sizes):
    out, off = [], 0
    for s in sizes:
        out.append(x[..., off:off + s])
        off += s
    return out

def rmsnorm(x, g):
    xf = x.astype(jnp.float32)
    y = xf * lax.rsqrt(jnp.mean(xf * xf, axis=-1, keepdims=True) + EPS)
    return (y * g.astype(jnp.float32)).astype(x.dtype)

def headnorm(h):
    return h * lax.rsqrt(jnp.mean(h * h, axis=-1, keepdims=True) + EPS)

def to_heads(t, n_heads):
    b, t_len, _ = t.shape
    return t.reshape(b, t_len, n_heads, -1).transpose(0, 2, 1, 3).astype(jnp.float32)

def from_heads(h):
    b, nh, t_len, d = h.shape
    return h.transpose(0, 2, 1, 3).reshape(b, t_len, nh * d)

def chunked(t):
    return t.reshape(t.shape[:2] + (t.shape[2] // CHUNK, CHUNK) + t.shape[3:])

def unchunk(t):
    return t.reshape(t.shape[:2] + (-1, t.shape[-1]))

def flip_t(t):
    return jnp.flip(t, axis=2)

def linear_state_scan(decay, update, s0):
    def step(s, du):
        d, u = du
        return d * s + u, s
    final, starts = lax.scan(step, s0, (decay, update))
    return starts, final

def retention_dir(q, k, v, log_gamma, s0):
    qc, kc, vc = chunked(q), chunked(k), chunked(v)
    nc = qc.shape[2]
    pos = jnp.arange(CHUNK, dtype=jnp.float32)
    lg = log_gamma.astype(jnp.float32)[:, None]
    diff = pos[:, None] - pos[None, :]
    dmat = jnp.where(diff >= 0, jnp.exp(lg[:, :, None] * jnp.maximum(diff, 0.0)), 0.0)
    scores = jnp.einsum('bhcid,bhcjd->bhcij', qc, kc) * dmat[None, :, None]
    intra = jnp.einsum('bhcij,bhcjv->bhciv', scores, vc)
    w_upd = jnp.exp(lg * (CHUNK - 1.0 - pos))
    upd = jnp.einsum('bhcjd,hj,bhcjv->cbhdv', kc, w_upd, vc)
    decay = jnp.broadcast_to(jnp.exp(lg * CHUNK)[None, None, :, :, None], (nc, 1, q.shape[1], 1, 1))
    starts, final = linear_state_scan(decay, upd, s0.astype(jnp.float32))
    q_in = qc * jnp.exp(lg * (pos + 1.0))[None, :, None, :, None]
    cross = jnp.einsum('bhcid,cbhdv->bhciv', q_in, starts)
    return unchunk(intra + cross), final

def gla_dir(q, k, v, log_alpha, s0):
    qc, kc, vc, lac = chunked(q), chunked(k), chunked(v), chunked(log_alpha)
    b = jnp.cumsum(lac, axis=3)
    b_last = b[:, :, :, -1:, :]
    qe = qc * jnp.exp(b)
    ke = kc * jnp.exp(-b)
    lower = jnp.tril(jnp.ones((CHUNK, CHUNK), dtype=bool))
    att = jnp.where(lower, jnp.einsum('bhcid,bhcjd->bhcij', qe, ke), 0.0)
    intra = jnp.einsum('bhcij,bhcjv->bhciv', att, vc)
    upd = jnp.einsum('bhcjd,bhcjv->cbhdv', kc * jnp.exp(b_last - b), vc)
    decay = jnp.exp(b_last[:, :, :, 0, :]).transpose(2, 0, 1, 3)[..., None]
    starts, final = linear_state_scan(decay, upd, s0.astype(jnp.float32))
    cross = jnp.einsum('bhcid,cbhdv->bhciv', qe, starts)
    return unchunk(intra + cross), final

def mlstm_dir(q, k, v, i_pre, f_pre, state0):
    c0, n0, m0 = (s.astype(jnp.float32) for s in state0)
    qc, kc, vc = chunked(q), chunked(k), chunked(v)
    ic = chunked(i_pre)
    fcum = jnp.cumsum(chunked(jax.nn.log_sigmoid(f_pre)), axis=3)
    lower = jnp.tril(jnp.ones((CHUNK, CHUNK), dtype=bool))
    dlog = jnp.where(lower, fcum[..., :, None] - fcum[..., None, :] + ic[..., None, :], -jnp.inf)
    mloc = jnp.max(dlog, axis=-1)
    w_last = jnp.exp(dlog[..., -1, :] - mloc[..., -1:])
    upd_c = jnp.einsum('bhcj,bhcjd,bhcjv->cbhdv', w_last, kc, vc)
    upd_n = jnp.einsum('bhcj,bhcjd->cbhd', w_last, kc)
    f_last = fcum[..., -1].transpose(2, 0, 1)
    m_last = mloc[..., -1].transpose(2, 0, 1)

    def step(carry, xs):
        cm, nm, mm = carry
        fl, ml, uc, un = xs
        m_new = jnp.maximum(fl + mm, ml)
        a = jnp.exp(fl + mm - m_new)
        bb = jnp.exp(ml - m_new)
        c_new = a[..., None, None] * cm + bb[..., None, None] * uc
        n_new = a[..., None] * nm + bb[..., None] * un
        return (c_new, n_new, m_new), (cm, nm, mm)

    final, (c_st, n_st, m_st) = lax.scan(step, (c0, n0, m0), (f_last, m_last, upd_c, upd_n))
    a_i = fcum + m_st.transpose(1, 2, 0)[..., None]
    m_i = jnp.maximum(a_i, mloc)
    w_inter = jnp.exp(a_i - m_i)
    pw = jnp.exp(dlog - m_i[..., None]) * jnp.einsum('bhcid,bhcjd->bhcij', qc, kc)
    num = (jnp.einsum('bhcij,bhcjv->bhciv', pw, vc)
           + w_inter[..., None] * jnp.einsum('bhcid,cbhdv->bhciv', qc, c_st))
    den = pw.sum(-1) + w_inter * jnp.einsum('bhcid,cbhd->bhci', qc, n_st)
    h = num / jnp.maximum(jnp.abs(den), jnp.exp(-m_i))[..., None]
    return unchunk(h), final

def even_mixer(xn, w_in, w_out, ig_b, fg_b, ret_logit, init):
    b, t_len, _ = xn.shape
    mq, mk, mv, mo, mg, rq, rk, rv, rg = _split(xn @ w_in, EVEN_SIZES)
    m_c0, m_n0, m_m0, r_s0 = init
    mq = to_heads(mq, H_M)
    mk = to_heads(mk, H_M) * DK_M ** -0.5
    mv = to_heads(mv, H_M)
    gates = mg.astype(jnp.float32).reshape(b, t_len, 2, 2, H_M).transpose(2, 3, 0, 4, 1)
    i_pre = gates[:, 0] + ig_b.astype(jnp.float32)[:, None, :, None]
    f_pre = gates[:, 1] + fg_b.astype(jnp.float32)[:, None, :, None]
    hf, (cf, nf, mf) = mlstm_dir(mq, mk, mv, i_pre[0], f_pre[0], (m_c0[:, 0], m_n0[:, 0], m_m0[:, 0]))
    hb, (cb, nb, mb) = mlstm_dir(flip_t(mq), flip_t(mk), flip_t(mv), flip_t(i_pre[1]), flip_t(f_pre[1]),
                                 (m_c0[:, 1], m_n0[:, 1], m_m0[:, 1]))
    h_m = from_heads(headnorm(hf + flip_t(hb))) * jax.nn.sigmoid(mo.astype(jnp.float32))
    rq = to_heads(rq, H_R)
    rk = to_heads(rk, H_R) * DK_R ** -0.5
    rv = to_heads(rv, H_R)
    log_gamma = jax.nn.log_sigmoid(ret_logit.astype(jnp.float32))
    of, sf = retention_dir(rq, rk, rv, log_gamma[0], r_s0[:, 0])
    ob, sb = retention_dir(flip_t(rq), flip_t(rk), flip_t(rv), log_gamma[1], r_s0[:, 1])
    h_r = from_heads(headnorm(of + flip_t(ob))) * jax.nn.silu(rg.astype(jnp.float32))
    y = jnp.concatenate([h_m, h_r], axis=-1).astype(xn.dtype) @ w_out
    new = (jnp.stack([cf, cb], axis=1), jnp.stack([nf, nb], axis=1),
           jnp.stack([mf, mb], axis=1), jnp.stack([sf, sb], axis=1))
    return y, new

def odd_mixer(xn, w_in, w2, b2, w_out, init):
    b, t_len, _ = xn.shape
    gq, gk, gv, gr, glr = _split(xn @ w_in, ODD_SIZES)
    gq = to_heads(gq, H_G) * DK_G ** -0.5
    gk = to_heads(gk, H_G)
    gv = to_heads(gv, H_G)
    glr = glr.reshape(b, t_len, 2, GLA_RANK)
    z = jnp.einsum('btdr,drk->dbtk', glr, w2) + b2[:, None, None, :]
    log_alpha = jax.nn.log_sigmoid(z.astype(jnp.float32)) / GLA_TAU
    la_f = to_heads(log_alpha[0], H_G)
    la_b = to_heads(log_alpha[1], H_G)
    of, sf = gla_dir(gq, gk, gv, la_f, init[:, 0])
    ob, sb = gla_dir(flip_t(gq), flip_t(gk), flip_t(gv), flip_t(la_b), init[:, 1])
    h = from_heads(headnorm(of + flip_t(ob))) * jax.nn.silu(gr.astype(jnp.float32))
    return h.astype(xn.dtype) @ w_out, jnp.stack([sf, sb], axis=1)

def dwconv_seq(a, w):
    f = a.shape[-1]
    return lax.conv_general_dilated(a, w[:, None, :].astype(a.dtype), (1,), 'SAME',
                                    dimension_numbers=('NWC', 'WIO', 'NWC'), feature_group_count=f)

def dwconv_grid(a, w, rows):
    b, t_len, f = a.shape
    a4 = a.reshape(b, rows, t_len // rows, f)
    out = lax.conv_general_dilated(a4, w[:, :, None, :].astype(a.dtype), (1, 1), 'SAME',
                                   dimension_numbers=('NHWC', 'HWIO', 'NHWC'), feature_group_count=f)
    return out.reshape(b, t_len, f)

def conv_ffn(xn, w_in, conv_w, conv_b, w_out, rows):
    a, v = _split(xn @ w_in, (D_FF, D_FF))
    if rows is None:
        a = dwconv_seq(a, conv_w[1])
    else:
        a = dwconv_grid(a, conv_w, rows)
    h = jax.nn.gelu(a + conv_b) * v
    return h @ w_out

def trunk_layer(x, mod, l, p, init, rows):
    shift1, scale1, gate1, shift2, scale2, gate2 = jnp.split(mod[:, None, :], 6, axis=-1)
    xn = rmsnorm(x, p['norm_mix_pre'][l]) * (1.0 + scale1) + shift1
    if l % 2 == 0:
        e = l // 2
        y, new = even_mixer(xn, p['w_in_even'][e], p['w_out_even'][e], p['mlstm_igate_b'][e],
                            p['mlstm_fgate_b'][e], p['ret_decay_logit'][e], init)
    else:
        o = l // 2
        y, new = odd_mixer(xn, p['w_in_odd'][o], p['gla_gate_w2'][o], p['gla_gate_b'][o],
                           p['w_out_odd'][o], init)
    x = x + gate1 * rmsnorm(y, p['norm_mix_post'][l])
    xn = rmsnorm(x, p['norm_ffn_pre'][l]) * (1.0 + scale2) + shift2
    y = conv_ffn(xn, p['ffn_w_in'][l], p['ffn_conv_w'][l], p['ffn_conv_b'][l], p['ffn_w_out'][l], rows)
    x = x + gate2 * rmsnorm(y, p['norm_ffn_post'][l])
    return x, new

def setup_inputs(seed: int = 0) -> dict:
    key = jax.random.key(seed)
    ks = jax.random.split(key, 32)
    f32 = jnp.float32

    def nrm(k, shape, scale):
        return jax.random.normal(k, shape, f32) * scale

    inp = {}
    inp['x_prompt'] = nrm(ks[0], (BATCH, SEQ, D_MODEL), 1.0)
    inp['x_sample'] = nrm(ks[1], (DEC_BATCH, DEC_SEQ, D_MODEL), 1.0)
    inp['c'] = nrm(ks[2], (DEC_BATCH, D_MODEL), 1.0)
    inp['c_ctx'] = nrm(ks[3], (D_MODEL,), 1.0)
    inp['state_mlstm_C'] = nrm(ks[4], (DEC_BATCH, N_EVEN, 2, H_M, DK_M, DV_M), 0.1)
    inp['state_mlstm_n'] = nrm(ks[5], (DEC_BATCH, N_EVEN, 2, H_M, DK_M), 0.1)
    inp['state_mlstm_m'] = nrm(ks[6], (DEC_BATCH, N_EVEN, 2, H_M), 1.0)
    inp['state_ret'] = nrm(ks[7], (DEC_BATCH, N_EVEN, 2, H_R, DK_R, DV_R), 0.3)
    inp['state_gla'] = nrm(ks[8], (DEC_BATCH, N_ODD, 2, H_G, DK_G, DV_G), 0.3)
    inp['ada_w'] = nrm(ks[9], (DEPTH, D_MODEL, 6 * D_MODEL), 0.5 * D_MODEL ** -0.5)
    inp['ada_b'] = nrm(ks[10], (DEPTH, 6 * D_MODEL), 0.02)
    inp['norm_mix_pre'] = 1.0 + nrm(ks[11], (DEPTH, D_MODEL), 0.02)
    inp['norm_mix_post'] = 1.0 + nrm(ks[12], (DEPTH, D_MODEL), 0.02)
    inp['norm_ffn_pre'] = 1.0 + nrm(ks[13], (DEPTH, D_MODEL), 0.02)
    inp['norm_ffn_post'] = 1.0 + nrm(ks[14], (DEPTH, D_MODEL), 0.02)
    inp['w_in_even'] = nrm(ks[15], (N_EVEN, D_MODEL, P_EVEN), D_MODEL ** -0.5)
    inp['w_out_even'] = nrm(ks[16], (N_EVEN, MIX_EVEN, D_MODEL), MIX_EVEN ** -0.5)
    inp['mlstm_igate_b'] = nrm(ks[17], (N_EVEN, 2, H_M), 0.1)
    inp['mlstm_fgate_b'] = jnp.linspace(3.0, 6.0, H_M, dtype=f32) + nrm(ks[18], (N_EVEN, 2, H_M), 0.1)
    base_logit = jnp.log(2.0 ** (5.0 + jnp.arange(H_R, dtype=f32)) - 1.0)
    inp['ret_decay_logit'] = base_logit + nrm(ks[19], (N_EVEN, 2, H_R), 0.1)
    inp['w_in_odd'] = nrm(ks[20], (N_ODD, D_MODEL, P_ODD), D_MODEL ** -0.5)
    inp['gla_gate_w2'] = nrm(ks[21], (N_ODD, 2, GLA_RANK, H_G * DK_G), GLA_RANK ** -0.5)
    inp['gla_gate_b'] = nrm(ks[22], (N_ODD, 2, H_G * DK_G), 0.1)
    inp['w_out_odd'] = nrm(ks[23], (N_ODD, MIX_ODD, D_MODEL), MIX_ODD ** -0.5)
    inp['ffn_w_in'] = nrm(ks[24], (DEPTH, D_MODEL, 2 * D_FF), D_MODEL ** -0.5)
    inp['ffn_conv_w'] = nrm(ks[25], (DEPTH, 3, 3, D_FF), 1.0 / 3.0)
    inp['ffn_conv_b'] = nrm(ks[26], (DEPTH, D_FF), 0.02)
    inp['ffn_w_out'] = nrm(ks[27], (DEPTH, D_FF, D_MODEL), D_FF ** -0.5)
    return inp

def reference(x_prompt, x_sample, c, c_ctx, state_mlstm_C, state_mlstm_n, state_mlstm_m, state_ret,
              state_gla, ada_w, ada_b, norm_mix_pre, norm_mix_post, norm_ffn_pre, norm_ffn_post,
              w_in_even, w_out_even, mlstm_igate_b, mlstm_fgate_b, ret_decay_logit,
              w_in_odd, gla_gate_w2, gla_gate_b, w_out_odd,
              ffn_w_in, ffn_conv_w, ffn_conv_b, ffn_w_out):
    p = dict(norm_mix_pre=norm_mix_pre, norm_mix_post=norm_mix_post, norm_ffn_pre=norm_ffn_pre,
             norm_ffn_post=norm_ffn_post, w_in_even=w_in_even, w_out_even=w_out_even,
             mlstm_igate_b=mlstm_igate_b, mlstm_fgate_b=mlstm_fgate_b, ret_decay_logit=ret_decay_logit,
             w_in_odd=w_in_odd, gla_gate_w2=gla_gate_w2, gla_gate_b=gla_gate_b, w_out_odd=w_out_odd,
             ffn_w_in=ffn_w_in, ffn_conv_w=ffn_conv_w, ffn_conv_b=ffn_conv_b, ffn_w_out=ffn_w_out)
    f32 = jnp.float32

    bp = x_prompt.shape[0]
    cond_ctx = jax.nn.silu(c_ctx)[None, :]
    h = x_prompt
    new_c, new_n, new_m, new_r, new_g = [], [], [], [], []
    for l in range(DEPTH):
        mod = cond_ctx @ ada_w[l] + ada_b[l]
        if l % 2 == 0:
            init = (jnp.zeros((bp, 2, H_M, DK_M, DV_M), f32), jnp.zeros((bp, 2, H_M, DK_M), f32),
                    jnp.zeros((bp, 2, H_M), f32), jnp.zeros((bp, 2, H_R, DK_R, DV_R), f32))
            h, (sc, sn, sm, sr) = trunk_layer(h, mod, l, p, init, None)
            new_c.append(sc)
            new_n.append(sn)
            new_m.append(sm)
            new_r.append(sr)
        else:
            init = jnp.zeros((bp, 2, H_G, DK_G, DV_G), f32)
            h, sg = trunk_layer(h, mod, l, p, init, None)
            new_g.append(sg)
    y_prompt = h

    rows = x_sample.shape[1] // GRID_W
    cond = jax.nn.silu(c)
    g = x_sample
    for l in range(DEPTH):
        mod = cond @ ada_w[l] + ada_b[l]
        if l % 2 == 0:
            e = l // 2
            init = (state_mlstm_C[:, e], state_mlstm_n[:, e], state_mlstm_m[:, e], state_ret[:, e])
        else:
            init = state_gla[:, l // 2]
        g, _ = trunk_layer(g, mod, l, p, init, rows)
    y_sample = g

    return (y_prompt, y_sample, jnp.stack(new_c, axis=1), jnp.stack(new_n, axis=1),
            jnp.stack(new_m, axis=1), jnp.stack(new_r, axis=1), jnp.stack(new_g, axis=1))


_drawn_inputs = setup_inputs


def setup_inputs(seed=0):
    import zlib

    import numpy as np

    out = dict(_drawn_inputs(seed))
    spreads = {}
    factors = {'state_mlstm_C': 4.36,
     'state_mlstm_n': 8.0,
     'state_mlstm_m': 6.062,
     'state_ret': 2.997,
     'state_gla': 8.0,
     'norm_mix_post': 6.415,
     'norm_ffn_pre': 4.97,
     'norm_ffn_post': 6.977,
     'ffn_conv_b': 4.711}
    for name, (base, spread) in spreads.items():
        noise = np.random.default_rng([zlib.crc32(name.encode()), seed]).standard_normal(out[name].shape)
        drawn = base * np.exp(spread * noise) if base else spread * noise
        out[name] = jnp.asarray(drawn.astype(out[name].dtype))
    for name, factor in factors.items():
        out[name] = (out[name] * factor).astype(out[name].dtype)
    return out
```

```python
import numpy as np
import concourse.bass as bass
from concourse import mybir
from contextlib import ExitStack, contextmanager

D = 1024
KT = D // 128
CTX, LAT = 128, 1024
T = CTX + LAT
CH = 128
NC = T // CH
TG = 384
NG = T // TG
GRID_W = 64
ROWS = LAT // GRID_W
DK = 128
DVG = 256
D_FF = 2816
FT = D_FF // 128
FP = FT // 2
EPS = 1e-6
FAR = 1.0e30
NBLK = 206
ADA_FRONT = 20
RANK = 16
GLA_TAU = 16.0

PER = {'act.ffn0': {'a_padded': 2,
              'act_order': 2,
              'conv_done': 2,
              'pj_free0': 4,
              'pj_free1': 4,
              'pj_free2': 4,
              'pj_full0': 4,
              'pj_full1': 4,
              'w_used0': 3,
              'w_used1': 3},
 'act.ffn1': {'a_padded': 2,
              'act_order': 2,
              'conv_done': 2,
              'pj_free0': 4,
              'pj_free1': 4,
              'pj_free2': 4,
              'pj_full0': 4,
              'pj_full1': 4,
              'w_used0': 3,
              'w_used1': 3},
 'act.mlstm': {'act_order': 3,
               'e_masked': 6,
               'front_done': 3,
               'h_stored0': 16,
               'h_stored1': 16,
               'h_stored2': 16,
               'head_set': 1,
               'hout_ready': 3,
               'mb_full0': 7,
               'mb_full1': 7,
               'mb_full2': 8,
               'mb_full3': 7,
               'mb_full4': 6,
               'pj_free0': 4,
               'pj_free1': 4,
               'pj_free2': 4,
               'pj_full0': 4,
               'pj_full1': 4,
               'so_ready': 2,
               'ss_ready': 1,
               'w_used0': 2,
               'w_used1': 2},
 'act.odd': {'act_order': 6,
             'bb_ready': 2,
             'dc_ready': 1,
             'front_done': 3,
             'h_stored0': 32,
             'h_stored1': 32,
             'h_stored2': 32,
             'hout_ready': 6,
             'mb_full0': 14,
             'mb_full1': 11,
             'mb_full2': 12,
             'mb_full3': 11,
             'mb_full4': 15,
             'pj_free0': 6,
             'pj_free1': 6,
             'pj_free2': 6,
             'pj_full0': 6,
             'pj_full1': 6,
             'sg_new': 8,
             'so_ready': 2,
             'ss_ready': 1,
             'w2_set': 1,
             'w_used0': 3,
             'w_used1': 3,
             'z_logs': 2},
 'act.out': {'pj_free0': 2,
             'pj_free1': 2,
             'pj_free2': 2,
             'pj_full0': 2,
             'pj_full1': 2,
             'sq_added0': 3,
             'sq_added1': 3,
             'w_used0': 1,
             'w_used1': 1},
 'act.post': {'sq_added0': 1, 'sq_added1': 1, 'y_new': 2},
 'act.post_last': {'y_new': 2},
 'act.pre': {'act_order': 4, 't_ready': 2},
 'act.ret': {'act_order': 6,
             'front_done': 3,
             'h_stored0': 16,
             'h_stored1': 16,
             'h_stored2': 16,
             'head_set': 1,
             'hout_ready': 3,
             'mb_full0': 7,
             'mb_full1': 7,
             'mb_full2': 8,
             'mb_full3': 4,
             'mb_full4': 3,
             'pj_free0': 4,
             'pj_free1': 4,
             'pj_free2': 4,
             'pj_full0': 4,
             'pj_full1': 4,
             'so_ready': 2,
             'ss_ready': 1,
             'w_used0': 2,
             'w_used1': 2},
 'act.squares': {'sq_added0': 1, 'sq_added1': 1},
 'dve.ffn0': {'a_padded': 2,
              'ada_used': 4,
              'conv_done': 2,
              'dve_order': 23,
              'gelu_done': 2,
              'hh_ready': 2,
              'hl_ready': 2,
              'mb_free0': 6,
              'mb_free1': 6,
              'mb_free2': 6,
              'mb_free3': 6,
              'mb_free4': 1,
              'mb_full0': 6,
              'mb_full1': 6,
              'mb_full2': 6,
              'mb_full3': 4,
              'pj_free0': 2,
              'pj_free1': 2,
              'pj_free2': 2,
              'pj_full0': 4,
              'pj_full1': 4,
              'w_used0': 3,
              'w_used1': 3},
 'dve.ffn1': {'a_padded': 2,
              'conv_done': 2,
              'dve_order': 23,
              'gelu_done': 2,
              'hh_ready': 2,
              'hl_ready': 2,
              'mb_free0': 6,
              'mb_free1': 6,
              'mb_free2': 6,
              'mb_free3': 6,
              'mb_full0': 6,
              'mb_full1': 6,
              'mb_full2': 6,
              'mb_full3': 4,
              'pj_free0': 2,
              'pj_free1': 2,
              'pj_free2': 2,
              'pj_full0': 4,
              'pj_full1': 4,
              'w_used0': 3,
              'w_used1': 3},
 'dve.mlstm': {'ada_used': 4,
               'dve_order': 32,
               'e_masked': 6,
               'e_ready': 18,
               'front_done': 3,
               'gate_ready': 1,
               'h_stored0': 16,
               'h_stored1': 16,
               'h_stored2': 16,
               'head_set': 1,
               'hout_ready': 3,
               'hstd_ready': 1,
               'mb_free0': 7,
               'mb_free1': 4,
               'mb_free2': 8,
               'mb_free4': 1,
               'mb_full0': 7,
               'mb_full1': 7,
               'mb_full2': 8,
               'mb_full3': 7,
               'mb_full4': 6,
               'o_ready': 1,
               'q_decay': 18,
               'so_ready': 2,
               'so_stored': 32,
               'ss_ready': 1,
               'st_loaded': 32},
 'dve.odd': {'bb_ready': 2,
             'dc_ready': 1,
             'dve_order': 40,
             'eg_ready': 12,
             'front_done': 3,
             'gate_ready': 1,
             'h_stored0': 32,
             'h_stored1': 32,
             'h_stored2': 32,
             'hout_ready': 6,
             'hstd_ready': 1,
             'ke_ready': 3,
             'mb_free0': 11,
             'mb_free1': 8,
             'mb_free2': 7,
             'mb_free3': 7,
             'mb_free4': 3,
             'mb_full0': 14,
             'mb_full1': 11,
             'mb_full2': 12,
             'mb_full3': 11,
             'mb_full4': 15,
             'o_ready': 1,
             'sd_ready': 16,
             'sg_new': 8,
             'so_ready': 2,
             'so_stored': 32,
             'ss_ready': 1,
             'st_loaded': 32,
             'w2_set': 1,
             'z_logs': 2},
 'dve.out': {'pj_full0': 2,
             'pj_full1': 2,
             'sq_added0': 3,
             'sq_added1': 3,
             'sq_ready0': 3,
             'sq_ready1': 3,
             'w_used0': 1,
             'w_used1': 1},
 'dve.post': {'dve_order': 4,
              'sq_added0': 1,
              'sq_added1': 1,
              'sq_ready0': 1,
              'sq_ready1': 1,
              'xr_loaded0': 16,
              'xr_loaded1': 16,
              'y_new': 2},
 'dve.post_last': {'dve_order': 4, 'xr_loaded0': 16, 'xr_loaded1': 16, 'y_new': 2},
 'dve.pre': {'t_ready': 2, 'xh_ready': 2, 'xl_ready': 2},
 'dve.ret': {'ada_used': 4,
             'dve_order': 18,
             'front_done': 3,
             'gate_ready': 1,
             'h_stored0': 16,
             'h_stored1': 16,
             'h_stored2': 16,
             'head_set': 1,
             'hout_ready': 3,
             'hstd_ready': 1,
             'mb_free0': 7,
             'mb_free1': 4,
             'mb_free2': 8,
             'mb_free4': 1,
             'mb_full0': 7,
             'mb_full1': 7,
             'mb_full2': 8,
             'mb_full3': 4,
             'mb_full4': 3,
             'o_ready': 1,
             'ret_rows': 1,
             'so_ready': 2,
             'so_stored': 32,
             'ss_ready': 1,
             'st_loaded': 32},
 'dve.squares': {'sq_added0': 1, 'sq_added1': 1, 'sq_ready0': 1, 'sq_ready1': 1},
 'pe.ffn0': {'ada_loaded': 64,
             'hl_ready': 2,
             'mb_free0': 6,
             'mb_free1': 6,
             'mb_free2': 6,
             'mb_free3': 6,
             'mb_free4': 1,
             'pj_free0': 4,
             'pj_free1': 4,
             'pj_free2': 4,
             'w_ready0': 3,
             'w_ready1': 3},
 'pe.ffn1': {'hl_ready': 2,
             'mb_free0': 6,
             'mb_free1': 6,
             'mb_free2': 6,
             'mb_free3': 6,
             'pj_free0': 4,
             'pj_free1': 4,
             'pj_free2': 4,
             'w_ready0': 3,
             'w_ready1': 3},
 'pe.mlstm': {'ada_loaded': 64,
              'front_done': 3,
              'head_set': 1,
              'hout_ready': 3,
              'mb_free0': 7,
              'mb_free1': 7,
              'mb_free2': 8,
              'mb_free3': 7,
              'mb_free4': 4,
              'o_ready': 1,
              'pj_free0': 4,
              'pj_free1': 4,
              'pj_free2': 4,
              'w_ready0': 2,
              'w_ready1': 2},
 'pe.odd': {'front_done': 3,
            'hout_ready': 6,
            'ke_ready': 3,
            'mb_free0': 14,
            'mb_free1': 11,
            'mb_free2': 12,
            'mb_free3': 11,
            'mb_free4': 9,
            'o_ready': 1,
            'pj_free0': 6,
            'pj_free1': 6,
            'pj_free2': 6,
            'sd_ready': 16,
            'w2_set': 1,
            'w_ready0': 3,
            'w_ready1': 3},
 'pe.out': {'pj_free0': 2, 'pj_free1': 2, 'pj_free2': 2, 'w_ready0': 1, 'w_ready1': 1},
 'pe.ret': {'ada_loaded': 64,
            'front_done': 3,
            'hout_ready': 3,
            'mb_free0': 7,
            'mb_free1': 7,
            'mb_free2': 8,
            'mb_free3': 4,
            'mb_free4': 1,
            'o_ready': 1,
            'pj_free0': 4,
            'pj_free1': 4,
            'pj_free2': 4,
            'w_ready0': 2,
            'w_ready1': 2},
 'pool.split': {'raw_loaded0': 16, 'raw_loaded1': 16, 'w_hi0': 1, 'w_hi1': 1, 'w_used0': 1, 'w_used1': 1},
 'sp.ffn1': {'w_ready0': 3, 'w_ready1': 3},
 'sp.ffn_b': {'ada_used': 4, 'w_ready0': 3, 'w_ready1': 3},
 'sp.heads': {'ada_used': 4, 'w_ready0': 2, 'w_ready1': 2},
 'sp.odd': {'w_ready0': 3, 'w_ready1': 3},
 'sp.out0': {'w_ready0': 1, 'w_ready1': 1},
 'sp.out1': {'w_ready0': 1, 'w_ready1': 1}}


class Tally:

    def __init__(self):
        self.count, self.turn, self.per = {}, None, {}

    def before(self, sem):
        at = self.count.get(sem.name, 0)
        if self.turn is not None and self.per.get(sem.name, 0):
            return self.turn * self.per[sem.name] + at
        return at

    def next(self, sem, by=1):
        self.count[sem.name] = self.count.get(sem.name, 0) + by
        return self.before(sem)

    @contextmanager
    def loop(self, engine, name, turns):
        start = dict(self.count)
        self.per = PER.get(name, {})
        with engine.Fori(0, turns) as turn:
            self.turn = turn
            yield turn
        found = {k: v - start.get(k, 0) for k, v in self.count.items() if v != start.get(k, 0)}
        assert found == self.per, (name, found)
        for k, v in found.items():
            self.count[k] += v * (turns - 1)
        self.turn, self.per = None, {}


def mod_column(layer, part, k):
    j = 8 * part + k
    if layer == 0:
        return j if j < 16 else j + 4
    return j + 52 if j < 44 else j - 28


def build(nc, a):
    f32, f32r = mybir.dt.float32, mybir.dt.float32r
    u8 = mybir.dt.uint8
    ALU = mybir.AluOpType
    ACT = mybir.ActivationFunctionType
    AX = mybir.AxisListType

    x_saved_dram = nc.dram_tensor("residual_scratch", [128, KT, T], f32, kind="Internal").ap()
    h_dram = nc.dram_tensor("mixer_scratch", [KT, 128, T], f32, kind="Internal").ap()

    ctx = ExitStack()
    with ctx:
        def sem(name):
            return ctx.enter_context(nc.semaphore(name))

        def sb(name, shape, dt=f32, scope=ctx):
            return scope.enter_context(nc.sbuf_tensor(name, shape, dt))

        xh = sb("xh", [128, KT, T], f32r)
        xl = sb("xl", [128, KT, T], f32r)
        wh = [sb(f"wh{s}", [128, 1024], f32r) for s in range(2)]
        wl = [sb(f"wl{s}", [128, 1024], f32r) for s in range(2)]
        raw = [sb(f"raw{s}", [128, 1024]) for s in range(2)]
        ada_w = sb("ada_w", [128, 1024])
        ident = sb("ident", [128, 128])
        ones = sb("ones", [128, 1])
        after = sb("after", [128, 2])
        tickp = sb("tickp", [128, 1])
        eps = sb("eps", [128, 1])
        tick = sb("tick", [128, 1])
        tickv = sb("tickv", [128, 1])
        cond = sb("cond", [128, KT, 2])
        mod = sb("mod", [128, 96, 2])
        ada_b = sb("ada_b", [128, 96])
        gains = sb("gains", [128, 4, 2, KT])
        coef = sb("coef", [128, KT, 2])
        std = sb("std", [128, NC])
        rstd = sb("rstd", [128, NC])
        cw = sb("cw", [128, 2, 10])
        rst = sb("rst", [128, T + 1])
        far = sb("far", [128, 2, CH])
        m01 = sb("m01", [128, 2, CH])
        m8 = sb("m8", [128, 2, CH], u8)
        pos = sb("pos", [128, 4, CH])
        pcol = sb("pcol", [128, 2])
        hss = sb("hss", [128, NC])
        hstd = sb("hstd", [128, NC])
        hrs = sb("hrs", [128, NC])

        rows_scope = ExitStack()
        y = sb("y", [128, KT, T], scope=rows_scope)
        norm_scope = ExitStack()
        rb = sb("rb", [128, T], scope=norm_scope)
        ss = sb("ss", [128, T], scope=norm_scope)
        sq = [sb(f"sq{s}", [128, T], scope=norm_scope) for s in range(2)]
        xr = [sb(f"xr{s}", [128, T], scope=norm_scope) for s in range(2)]
        front = sb("front", [128, 8, 1024], scope=norm_scope)
        norm_scope.close()
        ffn_scope = ExitStack()
        sb("under_norm", [128, 4 * T], scope=ffn_scope)
        hh = sb("hh", [128, 2, T], f32r, scope=ffn_scope)
        hl = sb("hl", [128, 2, T], f32r, scope=ffn_scope)
        pad = [sb(f"pad{t}", [128, ROWS + 2, GRID_W + 2], scope=ffn_scope) for t in range(2)]
        padc = [sb(f"padc{t}", [128, CTX + 2], scope=ffn_scope) for t in range(2)]
        cc = [sb(f"cc{t}", [128, T], scope=ffn_scope) for t in range(2)]
        conv = sb("conv", [128, FT, 10], scope=ffn_scope)
        ffn_scope.close()
        rows_scope.close()

        even = ExitStack()
        qT = sb("qT", [128, T], scope=even)
        kT = sb("kT", [128, T], scope=even)
        vT = sb("vT", [128, T], scope=even)
        gT = sb("gT", [128, T], scope=even)
        hout = [sb(f"hout{s}", [128, TG], scope=even) for s in range(3)]
        kw = [sb(f"kw{d}", [128, NC, CH], scope=even) for d in range(2)]
        v1 = sb("v1", [128, NC, 129], scope=even)
        pr = [sb(f"pr{d}", [128, NC, CH], scope=even) for d in range(2)]
        qw = [sb(f"qw{d}", [128, NC, CH], scope=even) for d in range(2)]
        st = [sb(f"st{d}", [128, NC, 129], scope=even) for d in range(2)]
        num = sb("num", [128, NC, 2, 129], scope=even)
        cb = [sb(f"cb{d}", [128, 3, CH], scope=even) for d in range(2)]
        tm = [sb(f"tm{d}", [128, 3, CH], scope=even) for d in range(2)]
        crow = sb("crow", [36, T], scope=even)
        cols = [sb(f"cols{n}", [128, NC, 36], scope=even) for n in range(3)]
        hcol = sb("hcol", [128, 3, 2, NC], scope=even)
        scb = sb("scb", [128, 8, 2, NC], scope=even)
        hsc = sb("hsc", [128, 2, 2, NC], scope=even)
        sel = sb("sel", [36, 2, 128], scope=even)
        den = sb("den", [128, NC, 2], scope=even)
        rr = sb("rr", [128, NC, 2], scope=even)
        gbias = sb("gbias", [128, 2], scope=even)
        m0 = sb("m0", [36, 1], scope=even)
        ms = sb("ms", [36, 2, NC], scope=even)
        cl = sb("cl", [36, NC], scope=even)
        lg = sb("lg", [128, 8], scope=even)
        lgt = sb("lgt", [128, 8], scope=even)
        rt = sb("rt", [128, 4, CH], scope=even)
        rlg = sb("rlg", [128, 2], scope=even)
        rw = sb("rw", [128, 2, 2], scope=even)
        ig = qw[0][:, :, :].rearrange("p c n -> p (c n)")[0:36, :]
        lf = qw[1][:, :, :].rearrange("p c n -> p (c n)")[0:36, :]
        fz = kw[0][:, :, :].rearrange("p c n -> p (c n)")
        fa = kw[1][:, :, :].rearrange("p c n -> p (c n)")
        fc = pr[0][:, :, :].rearrange("p c n -> p (c n)")[0:36, :]
        jr = pr[1][:, :, :].rearrange("p c n -> p (c n)")[0:36, :]
        mr = st[0][:, :, :].rearrange("p c n -> p (c n)")[0:36, 0:T]
        ur = st[1][:, :, :].rearrange("p c n -> p (c n)")[0:36, 0:T]
        gr = num[:, :, :, :].rearrange("p c d n -> p (c d n)")[0:36, 0:T]
        even.close()

        odd = ExitStack()
        oq = sb("oq", [128, T], scope=odd)
        ok = sb("ok", [128, T], scope=odd)
        ov = sb("ov", [128, 2, T], scope=odd)
        ogate = sb("ogate", [128, 2, T], scope=odd)
        bb = [sb(f"bb{d}", [128, T], scope=odd) for d in range(2)]
        qe = [sb(f"qe{d}", [128, NC, CH], scope=odd) for d in range(2)]
        kt = sb("kt", [128, 2, NC, CH], scope=odd)
        og = sb("og", [128, NC, DVG], scope=odd)
        tp = [sb(f"tp{d}", [128, 3, CH], scope=odd) for d in range(2)]
        sg = [[sb(f"sg{d}{s}", [128, DVG], scope=odd) for s in range(2)] for d in range(2)]
        sgo = [sb(f"sgo{d}", [128, DVG], scope=odd) for d in range(2)]
        dc = sb("dc", [128, 2, 3, NC], scope=odd)
        bm = sb("bm", [128, 2, 3, NC], scope=odd)
        glr = sb("glr", [48, T], scope=odd)
        w2 = ada_w[0:48, 0:4 * DK]
        w2s = ada_w[0:48, 4 * DK:5 * DK]
        b2 = sb("b2", [128, 2, 4], scope=odd)
        b2s = sb("b2s", [128, 2], scope=odd)
        own = ExitStack()
        la = sb("la", [128, T], scope=own)
        own.close()
        own = ExitStack()
        pg = sb("pg", [128, NC, CH], scope=own)
        own.close()
        sb("under_pg", [128, T], scope=odd)
        own = ExitStack()
        ke = [sb(f"ke{d}", [128, 3, CH], scope=own) for d in range(2)]
        own.close()
        own = ExitStack()
        sgs = [sb(f"sgs{d}", [128, DVG], scope=own) for d in range(2)]
        sgt = [sb(f"sgt{d}", [128, DVG], scope=own) for d in range(2)]
        own.close()
        sb("under_sgs", [128, 4 * DVG], scope=odd)
        own = ExitStack()
        vt = sb("vt", [128, NC, DVG], scope=own)
        own.close()
        own = ExitStack()
        oh = [sb(f"oh{s}", [128, TG], scope=own) for s in range(3)]
        own.close()
        sb("under_vt", [128, NC * DVG], scope=odd)
        odd.close()

        bank = [ctx.enter_context(nc.psum_tensor(f"bank{i}", [128, 512], f32)) for i in range(8)]
        pj, mb = bank[0:3], bank[3:8]

        def sems(names):
            return [sem(x) for x in names.split()]

        consts_made, small_loaded, x_loaded, cond_ready = sems("consts_made small_loaded x_loaded cond_ready")
        front_loaded = [sem(f"front_loaded{s}") for s in range(8)]
        front_used = sem("front_used")
        mod_ready = sem("mod_ready")
        raw_loaded = [sem(f"raw_loaded{s}") for s in range(2)]
        w_hi = [sem(f"w_hi{s}") for s in range(2)]
        w_ready = [sem(f"w_ready{s}") for s in range(2)]
        w_used = [sem(f"w_used{s}") for s in range(2)]
        ada_loaded, ada_used = sems("ada_loaded ada_used")
        pj_full = [sem(f"pj_full{c}") for c in range(2)]
        pj_free = [sem(f"pj_free{c}") for c in range(3)]
        mb_full = [sem(f"mb_full{i}") for i in range(5)]
        mb_free = [sem(f"mb_free{i}") for i in range(5)]
        act_order, dve_order, pool_order = sems("act_order dve_order pool_order")
        sq_ready = [sem(f"sq_ready{s}") for s in range(2)]
        sq_added = [sem(f"sq_added{s}") for s in range(2)]
        stat_full, std_ready, rstd_ready, rb_full, rb_ready = sems("stat_full std_ready rstd_ready rb_full rb_ready")
        coef_ready, t_ready, xh_ready, xl_ready, x_saved = sems("coef_ready t_ready xh_ready xl_ready x_saved")
        xr_loaded = [sem(f"xr_loaded{s}") for s in range(2)]
        y_new, out_stored = sems("y_new out_stored")
        conv_loaded, a_padded, conv_done, gelu_done, hh_ready, hl_ready, pads_clear = sems(
            "conv_loaded a_padded conv_done gelu_done hh_ready hl_ready pads_clear")
        mix_loaded, gates_logs, gates_rows, gates_exp, m_stored, cols_ready = sems(
            "mix_loaded gates_logs gates_rows gates_exp m_stored cols_ready")
        head_set, q_decay, e_masked, e_ready, front_done, ret_rows = sems(
            "head_set q_decay e_masked e_ready front_done ret_rows")
        st_loaded, so_ready, so_stored = sems("st_loaded so_ready so_stored")
        ss_ready, hstd_ready, o_ready, gate_ready, hout_ready = sems("ss_ready hstd_ready o_ready gate_ready hout_ready")
        h_stored = [sem(f"h_stored{g}") for g in range(3)]
        z_logs, bb_ready, w2_set, eg_ready, ke_ready, sd_ready, sg_new, dc_ready = sems(
            "z_logs bb_ready w2_set eg_ready ke_ready sd_ready sg_new dc_ready")

        block = ctx.enter_context(nc.Block())

        def b3(ap, n):
            return ap.rearrange("p (c o) -> p c o", o=1).broadcast_to([ap.shape[0], ap.shape[1], n])

        def g3(ap):
            return ap.rearrange("p (c n) -> p c n", n=CH)

        def chunk_row(ap, n):
            return ap.rearrange("p (o i) -> p o i", o=1).broadcast_to([ap.shape[0], n, CH])

        @block.sync
        def _(sp):
            seen = Tally()
            state = {"n": 0, "ada": ADA_FRONT}

            def weights(n, s):
                sp.wait_ge(w_ready[s], seen.before(w_ready[s]))
                seen.next(w_ready[s])
                sp.dma_start(raw[s][:, :], a["w"][n]).then_inc(raw_loaded[s], 16)

            def ada(n):
                sp.wait_ge(ada_used, seen.before(ada_used))
                seen.next(ada_used)
                sp.dma_start(ada_w[:, :], a["ada"][n]).then_inc(ada_loaded, 16)

            def stream(name, turns, pattern):
                nw, na, n0, a0 = pattern.count("w"), pattern.count("a"), state["n"], state["ada"]

                def once(turn):
                    w, c = 0, 0
                    for what in pattern:
                        if what == "w":
                            weights(turn * nw + (n0 + w), (n0 + w) % 2)
                            w += 1
                        else:
                            ada(turn * na + (a0 + c))
                            c += 1
                if turns == 1:
                    once(0)
                else:
                    with seen.loop(sp, "sp." + name, turns) as turn:
                        once(turn)
                state["n"] += turns * nw
                state["ada"] += turns * na

            sp.dma_start(cond[:, :, :], a["cond"]).then_inc(small_loaded, 16)
            sp.dma_start(ada_b[:, :], a["ada_b"]).then_inc(small_loaded, 16)
            sp.dma_start(gains[:, :, :, :], a["gains"]).then_inc(small_loaded, 16)
            for n in range(8):
                sp.dma_start(front[:, n, :], a["ada"][n]).then_inc(front_loaded[n], 16)
            sp.dma_start(y[:, :, :], a["x"]).then_inc(x_loaded, 16)
            for n in range(8, ADA_FRONT):
                sp.wait_ge(front_used, n - 7)
                sp.dma_start(front[:, n % 8, :], a["ada"][n]).then_inc(front_loaded[n % 8], 16)
            stream("first", 1, "wwww")
            stream("head0", 1, "wawawawa")
            stream("heads", 6, "wawawawa")
            stream("last", 1, "waaaa")
            stream("out0", 4, "ww")
            stream("ffn_a", 1, "wawawawa")
            stream("ffn_b", FP - 1, "wawwwawawa")
            stream("ffn_c", 1, "ww")
            stream("odd_first", 1, "wwwww")
            stream("odd", 3, "wwwwww")
            stream("odd_last", 1, "ww")
            stream("out1", 4, "ww")
            stream("ffn1", FP, "wwwwww")
            assert state["n"] == NBLK and state["ada"] == 96, state

        @block.gpsimd
        def _(pool):
            made = Tally()

            def link(ins):
                ins.then_inc(pool_order, 1)
                pool.wait_ge(pool_order, made.next(pool_order))

            link(nc.gpsimd.memset(ident[:, :], 0.0))
            link(nc.gpsimd.affine_select(out=ident[:, :], in_=ident[:, :], compare_op=ALU.not_equal, fill=1.0,
                                         base=0, pattern=[[-1, 128]], channel_multiplier=1))
            link(nc.gpsimd.memset(eps[:, :], EPS))
            link(nc.gpsimd.memset(far[:, :, :], 0.0))
            link(nc.gpsimd.memset(m01[:, :, :], 1.0))
            for d, (cm, step) in enumerate(((-1, 1), (1, -1))):
                for tile, fill in ((far, FAR), (m01, 0.0)):
                    link(nc.gpsimd.affine_select(out=tile[:, d, :], in_=tile[:, d, :], compare_op=ALU.is_ge, fill=fill,
                                                 base=0, pattern=[[step, CH]], channel_multiplier=cm))
            for n, (step, base, cm) in enumerate(((1, 1, 0), (-1, CH, 0), (1, 0, -1), (-1, 0, 1))):
                link(nc.gpsimd.iota(pos[:, n, :], [[step, CH]], base=base, channel_multiplier=cm,
                                    allow_small_or_imprecise_dtypes=True))
            for n, (base, cm) in enumerate(((CH - 1, -1), (0, 1))):
                link(nc.gpsimd.iota(pcol[:, n:n + 1], [[0, 1]], base=base, channel_multiplier=cm,
                                    allow_small_or_imprecise_dtypes=True))
            link(nc.gpsimd.memset(rst[:, :], 1.0))
            link(nc.gpsimd.memset(rst[:, 0:T + 1:CH], 0.0))
            link(nc.gpsimd.memset(ones[:, :], 1.0))
            nc.gpsimd.memset(tickp[:, :], 0.0).then_inc(consts_made, 1)

            def split(s):
                pool.wait_ge(raw_loaded[s], made.next(raw_loaded[s], 16))
                pool.wait_ge(w_used[s], made.before(w_used[s]))
                made.next(w_used[s])
                nc.gpsimd.tensor_tensor(wh[s][:, :], raw[s][:, :], ones[:, 0:1].broadcast_to([128, 1024]), ALU.mult).then_inc(w_hi[s], 1)
                pool.wait_ge(w_hi[s], made.next(w_hi[s]))
                nc.gpsimd.tensor_tensor(wl[s][:, :], raw[s][:, :], wh[s][:, :].bitcast(f32), ALU.subtract).then_inc(w_ready[s], 1)

            split(0)
            split(1)
            with made.loop(pool, "pool.split", NBLK // 2 - 1):
                for s in range(2):
                    split(s)

        @block.tensor
        def _(pe):
            n = Tally()
            blocks = {"n": 0}

            def mm(out, lhsT, rhs, start=True, stop=True):
                return nc.tensor.matmul(out, lhsT, rhs, start=start, stop=stop)

            def exact(out, w_hi_, w_lo_, x_hi_, x_lo_, start, stop):
                mm(out, w_hi_, x_hi_, start, False)
                mm(out, w_hi_, x_lo_, False, False)
                return mm(out, w_lo_, x_hi_, False, stop)

            def slot():
                blocks["n"] += 1
                return (blocks["n"] - 1) % 2

            def project(s, c):
                if c == 0:
                    pe.wait_ge(w_ready[s], n.next(w_ready[s]))
                pe.wait_ge(pj_free[c], n.before(pj_free[c]))
                n.next(pj_free[c])
                g = slice(c * TG, (c + 1) * TG)
                for k in range(KT):
                    w = slice(k * 128, (k + 1) * 128)
                    last = exact(pj[c][:, 0:TG], wh[s][:, w], wl[s][:, w], xh[:, k, g], xl[:, k, g], k == 0, k == KT - 1)
                last.then_inc(w_used[s] if c == 2 else pj_full[c], 1)

            def project_first(s):
                pe.wait_ge(w_ready[s], n.next(w_ready[s]))
                for c in range(3):
                    pe.wait_ge(pj_free[c], n.before(pj_free[c]))
                    n.next(pj_free[c])
                for k in range(KT):
                    pe.wait_ge(xl_ready, n.next(xl_ready))
                    w = slice(k * 128, (k + 1) * 128)
                    for c in range(3):
                        g = slice(c * TG, (c + 1) * TG)
                        last = exact(pj[c][:, 0:TG], wh[s][:, w], wl[s][:, w], xh[:, k, g], xl[:, k, g], k == 0, k == KT - 1)
                        if k == KT - 1:
                            last.then_inc(w_used[s] if c == 2 else pj_full[c], 1)

            def project_all(s):
                for c in range(3):
                    project(s, c)

            def claim(i):
                pe.wait_ge(mb_free[i], n.before(mb_free[i]))
                if i == 4:
                    pe.wait_ge(hout_ready, n.before(hout_ready))
                n.next(mb_free[i])

            def ada(j):
                if j == 0:
                    claim(4)
                pe.wait_ge(ada_loaded, n.next(ada_loaded, 16))
                for k in range(KT):
                    last = mm(mb[4][:, 2 * j:2 * j + 2], ada_w[:, k * 128:(k + 1) * 128], cond[:, k, :], k == 0, k == KT - 1)
                last.then_inc(ada_used, 1)

            def stats(adds):
                for s in range(2):
                    pe.wait_ge(sq_added[s], n.next(sq_added[s], adds))
                pe.wait_ge(mb_free[3], n.before(mb_free[3]))
                for c in range(NC):
                    last = mm(mb[3][:, c:c + 1], ss[:, c * CH:(c + 1) * CH], ones[:, :])
                last.then_inc(stat_full, 1)
                pe.wait_ge(rstd_ready, n.next(rstd_ready))
                for c in range(3):
                    pe.wait_ge(pj_free[c], n.before(pj_free[c]))
                for c in range(NC):
                    last = mm(pj[c // 3][:, (c % 3) * CH:(c % 3 + 1) * CH], rstd[:, c:c + 1].broadcast_to([128, 128]), ident[:, :])
                last.then_inc(rb_full, 1)

            def chunk(g, j):
                return slice((3 * g + j) * CH, (3 * g + j + 1) * CH)

            def third(j):
                return slice(j * CH, (j + 1) * CH)

            def front_even(g, mlstm):
                if g == 0:
                    for c in range(3):
                        pe.wait_ge(pj_free[c], n.before(pj_free[c]))
                claim(0)
                for j in range(3):
                    last = nc.tensor.transpose(mb[0][:, third(j)], kT[:, chunk(g, j)], ident[:, :])
                last.then_inc(mb_full[0], 1)
                claim(1)
                for j in range(3):
                    last = nc.tensor.transpose(mb[1][:, third(j)], vT[:, chunk(g, j)], ident[:, :])
                last.then_inc(mb_full[1], 1)
                claim(2)
                for j in range(3):
                    last = mm(mb[2][:, third(j)], kT[:, chunk(g, j)], qT[:, chunk(g, j)])
                last.then_inc(mb_full[2], 1)
                if mlstm:
                    if g == 0:
                        pe.wait_ge(head_set, n.next(head_set))
                    for d in range(2):
                        claim(3 + d)
                        mm(mb[3 + d][:, 0:TG], sel[:, d, :], crow[:, g * TG:(g + 1) * TG]).then_inc(mb_full[3 + d], 1)

            def update_even(t, w):
                i = t % 2
                if t == 0:
                    pe.wait_ge(front_done, n.next(front_done, 3))
                    pe.wait_ge(mb_free[1], n.before(mb_free[1]))
                claim(i)
                for d, c in enumerate((t, NC - t if t else 0)):
                    last = mm(mb[i][:, 129 * d:129 * d + w], kw[d][:, c, :], v1[:, c, 0:w])
                last.then_inc(mb_full[i], 1)

            def read_mlstm(c):
                if c == 0:
                    for i in range(2):
                        pe.wait_ge(mb_free[i], n.before(mb_free[i]))
                i = 2 + c % 2
                claim(i)
                for d in range(2):
                    out = mb[i][:, 129 * d:129 * d + 129]
                    last = mm(out, pr[d][:, c, :], v1[:, c, :], True, c == 0)
                    if c:
                        last = mm(out, qw[d][:, c, :], st[d][:, c, :], False, True)
                last.then_inc(mb_full[i], 1)

            def read_ret(c):
                if c == 0:
                    for i in range(2):
                        pe.wait_ge(mb_free[i], n.before(mb_free[i]))
                i = 2 + c % 2
                claim(i)
                out = mb[i][:, 0:128]
                last = mm(out, pr[0][:, c, :], v1[:, c, 0:128], True, c == 0)
                if c:
                    mm(out, qw[0][:, c, :], st[0][:, c, 0:128], False, False)
                    last = mm(out, qw[1][:, c, :], st[1][:, c, 0:128], False, True)
                last.then_inc(mb_full[i], 1)

            def out_even():
                pe.wait_ge(o_ready, n.next(o_ready))
                for g in range(3):
                    pe.wait_ge(mb_free[4], n.before(mb_free[4]))
                    pe.wait_ge(hout_ready, n.before(hout_ready))
                    n.next(hout_ready)
                    for j in range(3):
                        last = nc.tensor.transpose(mb[4][:, third(j)], num[:, 3 * g + j, 0, 0:128], ident[:, :])
                    last.then_inc(mb_full[4], 1)

            def head_even(mlstm, follows):
                read = read_mlstm if mlstm else read_ret
                w = 129 if mlstm else 128
                s = slot()
                for g in range(3):
                    project(s, g)
                    front_even(g, mlstm)
                ada(0)
                if not follows:
                    for j in range(1, 4):
                        ada(j)
                    for t in range(8):
                        update_even(t, w)
                    for c in range(NC):
                        read(c)
                else:
                    s = slot()
                    for c in range(3):
                        project(s, c)
                        update_even(2 * c, w)
                        update_even(2 * c + 1, w)
                    ada(1)
                    s = slot()
                    project(s, 0)
                    update_even(6, w)
                    update_even(7, w)
                    project(s, 1)
                    for c in range(3):
                        read(c)
                    project(s, 2)
                    for c in range(3, 6):
                        read(c)
                    ada(2)
                    s = slot()
                    project(s, 0)
                    for c in range(6, 9):
                        read(c)
                    project(s, 1)
                    project(s, 2)
                    ada(3)
                out_even()

            def gate_logits(d):
                if d == 0:
                    pe.wait_ge(w2_set, n.next(w2_set))
                for g in range(3):
                    claim(4)
                    mm(mb[4][:, 0:TG], w2s[32 * d:32 * d + RANK, :], glr[32 * d:32 * d + RANK, g * TG:(g + 1) * TG])\
                        .then_inc(mb_full[4], 1)

            def front_odd(g):
                if g == 0:
                    for c in range(3):
                        pe.wait_ge(pj_free[c], n.before(pj_free[c]))
                for i in range(2):
                    claim(2 + i)
                    for j in range(3):
                        last = nc.tensor.transpose(mb[2 + i][:, third(j)], ov[:, i, chunk(g, j)], ident[:, :])
                    last.then_inc(mb_full[2 + i], 1)
                pe.wait_ge(ke_ready, n.next(ke_ready))
                for d in range(2):
                    claim(d)
                    for j in range(3):
                        last = nc.tensor.transpose(mb[d][:, third(j)], ke[d][:, j, :], ident[:, :])
                    last.then_inc(mb_full[d], 1)
                for d in range(2):
                    i = 4 if d == 0 else 0
                    claim(i)
                    for j in range(3):
                        last = mm(mb[i][:, third(j)], ke[d][:, j, :], qe[d][:, 3 * g + j, :])
                    last.then_inc(mb_full[i], 1)

            def step_odd(t):
                if t == 0:
                    pe.wait_ge(front_done, n.next(front_done, 3))
                    for i in range(4):
                        pe.wait_ge(mb_free[i], n.before(mb_free[i]))
                back = NC - t if t else 0
                if t < 8:
                    for d, c in enumerate((t, back)):
                        claim(d)
                        mm(mb[d][:, 0:DVG], kt[:, d, c, :], vt[:, c, :]).then_inc(mb_full[d], 1)
                claim(2)
                last = mm(mb[2][:, 0:DVG], pg[:, t, :], vt[:, t, :], True, t == 0)
                if t:
                    pe.wait_ge(sd_ready, n.next(sd_ready, 2))
                    last = mm(mb[2][:, 0:DVG], qe[0][:, t, :], sgs[0][:, :], False, True)
                last.then_inc(mb_full[2], 1)
                if t:
                    claim(3)
                    mm(mb[3][:, 0:DVG], qe[1][:, back, :], sgs[1][:, :]).then_inc(mb_full[3], 1)

            def out_odd():
                pe.wait_ge(o_ready, n.next(o_ready))
                for i in range(2):
                    for g in range(3):
                        pe.wait_ge(mb_free[4], n.before(mb_free[4]))
                        pe.wait_ge(hout_ready, n.before(hout_ready))
                        n.next(hout_ready)
                        for j in range(3):
                            last = nc.tensor.transpose(mb[4][:, third(j)], og[:, 3 * g + j, 128 * i:128 * i + 128], ident[:, :])
                        last.then_inc(mb_full[4], 1)

            def head_odd(follows):
                s = slot()
                project(s, 0)
                front_odd(0)
                project(s, 1)
                project(s, 2)
                front_odd(1)
                s = slot()
                project(s, 0)
                project(s, 1)
                front_odd(2)
                project(s, 2)
                if not follows:
                    for t in range(NC):
                        step_odd(t)
                else:
                    for b in range(4):
                        s = slot()
                        for c in range(3):
                            project(s, c)
                            t = 3 * b + c
                            if t < NC:
                                step_odd(t)
                            elif t < NC + 2:
                                gate_logits(t - NC)
                out_odd()

            def project_out():
                project_first(slot())
                project_all(slot())
                with n.loop(pe, "pe.out", 3):
                    project_all(slot())
                    project_all(slot())

            def down(last):
                pe.wait_ge(hl_ready, n.next(hl_ready, 2))
                for half in range(2):
                    s = slot()
                    pe.wait_ge(w_ready[s], n.next(w_ready[s]))
                    for m in range(4):
                        for c in range(3):
                            j = 12 * half + 3 * m + c
                            i = j % 4
                            if last and j >= 4:
                                pe.wait_ge(y_new, n.next(y_new))
                            else:
                                pe.wait_ge(mb_free[i], n.before(mb_free[i]))
                            if not last:
                                n.next(mb_free[i])
                            g = slice(c * TG, (c + 1) * TG)
                            for t in range(2):
                                w = slice(t * 512 + m * 128, t * 512 + m * 128 + 128)
                                ins = exact(mb[i][:, 0:TG], wh[s][:, w], wl[s][:, w], hh[:, t, g], hl[:, t, g], t == 0, t == 1)
                            ins.then_inc(w_used[s] if m == 3 and c == 2 else mb_full[i], 1)
                if last:
                    n.next(y_new, 4)

            def ffn(layer):
                with_ada = layer == 0
                project_first(slot())
                if with_ada:
                    ada(0)
                for j in range(1, 4):
                    project_all(slot())
                    if with_ada:
                        ada(j)
                with n.loop(pe, f"pe.ffn{layer}", FP - 1):
                    project_all(slot())
                    if with_ada:
                        ada(0)
                    down(False)
                    for j in range(1, 4):
                        project_all(slot())
                        if with_ada:
                            ada(j)
                down(True)

            pe.wait_ge(cond_ready, 1)
            pe.wait_ge(consts_made, 1)
            for b in range(ADA_FRONT):
                s = b % 8
                pe.wait_ge(front_loaded[s], n.next(front_loaded[s], 16))
                for k in range(KT):
                    last = mm(mb[4][:, 2 * b:2 * b + 2], front[:, s, k * 128:(k + 1) * 128], cond[:, k, :], k == 0, k == KT - 1)
                last.then_inc(front_used, 1)
            n.next(mb_free[4])
            stats(4)
            project_first(slot())
            for _ in range(3):
                project_all(slot())
            pe.wait_ge(gates_exp, 1)
            for i, rows in enumerate((gr, ur, lf)):
                claim(i)
                for c in range(NC):
                    last = nc.tensor.transpose(mb[i][:, 36 * c:36 * c + 36], rows[:, c * CH:(c + 1) * CH], ident[0:36, 0:36])
                last.then_inc(mb_full[i], 1)
            claim(3)
            for r in range(8):
                row = 32 * (r // 4) + r % 4
                last = mm(mb[3][:, 18 * r:18 * r + 18], ident[0:36, row:row + 1].broadcast_to([36, 128]),
                          ms[:, :, :].rearrange("p a c -> p (a c)"))
            last.then_inc(mb_full[3], 1)
            head_even(True, True)
            with n.loop(pe, "pe.mlstm", 3):
                head_even(True, True)
            with n.loop(pe, "pe.ret", 3):
                head_even(False, True)
            head_even(False, False)
            project_out()
            stats(12)
            n.next(y_new, 8)
            stats(4)
            ffn(0)
            stats(12)
            n.next(y_new, 8)
            stats(4)
            project_first(slot())
            for b in range(4):
                project_all(slot())
                if b < 2:
                    gate_logits(b)
            with n.loop(pe, "pe.odd", 3):
                head_odd(True)
            head_odd(False)
            project_out()
            stats(12)
            n.next(y_new, 8)
            stats(4)
            ffn(1)
            stats(12)

        @block.scalar
        def _(act):
            n = Tally()
            blocks = {"n": 0}
            COPY, EXP, IDENT = ACT.Copy, ACT.Exp, ACT.Identity
            fn = nc.scalar.activation

            def link(ins, done=act_order):
                ins.then_inc(done, 1)
                act.wait_ge(done, n.next(done))

            def settle():
                link(fn(tick[:, :], eps[:, :], COPY))

            def slot():
                blocks["n"] += 1
                return (blocks["n"] - 1) % 2

            def full(i):
                act.wait_ge(mb_full[i], n.next(mb_full[i]))

            def dves(i, uses):
                n.next(mb_full[i], uses)

            def job(s, c):
                full_ = w_used[s] if c == 2 else pj_full[c]
                act.wait_ge(full_, n.next(full_))

            def evacuate(s, c, out, scale=1.0):
                job(s, c)
                fn(out, pj[c][0:out.shape[0], 0:TG], COPY, scale=scale).then_inc(pj_free[c], 1)
                n.next(pj_free[c])

            def tg(c):
                return slice(c * TG, (c + 1) * TG)

            def square(source, s, width=T):
                act.wait_ge(sq_added[s], n.before(sq_added[s]))
                n.next(sq_added[s])
                fn(sq[s][:, 0:width], source, ACT.Square).then_inc(sq_ready[s], 1)

            def stats():
                act.wait_ge(stat_full, n.next(stat_full))
                fn(std[:, :], mb[3][:, 0:NC], ACT.Sqrt, bias=eps[:, :], scale=1.0 / D).then_inc(std_ready, 1)
                act.wait_ge(rb_full, n.next(rb_full))
                for c in range(3):
                    fn(rb[:, tg(c)], pj[c][:, 0:TG], COPY).then_inc(rb_ready, 1)

            def pre(layer, part, save):
                if save:
                    act.wait_ge(y_new, n.before(y_new))
                    act.dma_start(x_saved_dram, y[:, :, :]).then_inc(x_saved, 16)
                    n.next(x_saved, 16)
                act.wait_ge(coef_ready, n.next(coef_ready))
                shift = mod_column(layer, 3 * part, 0)

                def tile(k, s):
                    act.wait_ge(t_ready, n.next(t_ready))
                    fn(sq[s][:, 0:CTX], sq[s][:, 0:CTX], IDENT, bias=mod[:, k + shift, 0:1], scale=coef[:, k, 0:1]).then_inc(act_order, 1)
                    fn(sq[s][:, CTX:T], sq[s][:, CTX:T], IDENT, bias=mod[:, k + shift, 1:2], scale=coef[:, k, 1:2]).then_inc(act_order, 1)
                    act.wait_ge(act_order, n.next(act_order, 2))
                    fn(xh[:, k, :], sq[s][:, :], COPY).then_inc(xh_ready, 1)
                with n.loop(act, "act.pre", KT // 2) as turn:
                    tile(turn * 2, 0)
                    tile(turn * 2 + 1, 1)
                n.next(xl_ready, KT)

            def post(first, squares):
                source = a["x"] if first else x_saved_dram

                def load(k, s):
                    act.dma_start(xr[s][:, :], source[:, k, :]).then_inc(xr_loaded[s], 16)

                def tile(k, s, more):
                    act.wait_ge(y_new, n.next(y_new))
                    if more:
                        load(k + 2, s)
                    if squares:
                        square(y[:, k, :], s)
                act.wait_ge(x_saved, n.before(x_saved))
                load(0, 0)
                load(1, 1)
                with n.loop(act, "act.post" if squares else "act.post_last", KT // 2 - 1) as turn:
                    tile(turn * 2, 0, True)
                    tile(turn * 2 + 1, 1, True)
                tile(6, 0, False)
                tile(7, 1, False)
                for s in range(2):
                    n.next(xr_loaded[s], 16 * KT // 2)

            def load_states_even(mlstm, h):
                for d in range(2):
                    c = 1 if d == 0 else NC - 1
                    source = a["st_mlstm"][d] if mlstm else a["st_ret"][d]
                    act.dma_start(st[d][:, c, 0:(129 if mlstm else 128)], source[h]).then_inc(st_loaded, 16)

            def store_states_even(mlstm, h):
                act.wait_ge(so_ready, n.next(so_ready, 2))
                for d in range(2):
                    dest = a["new_mlstm"][d] if mlstm else a["new_ret"][d]
                    act.dma_start(dest[h], st[d][:, 0, 0:(129 if mlstm else 128)]).then_inc(so_stored, 16)

            def front_even(g, mlstm):
                full(1)
                fn(v1[:, 3 * g:3 * g + 3, 0:CH], g3(mb[1][:, 0:TG]), COPY).then_inc(mb_free[1], 1)
                if not mlstm:
                    return
                for d in range(2):
                    full(3 + d)
                    fn(cb[d][:, :, :], g3(mb[3 + d][:, 0:TG]), COPY).then_inc(mb_free[3 + d], 1)
                settle()
                if g == 0:
                    act.wait_ge(head_set, n.next(head_set))
                for d in range(2):
                    for j in range(3):
                        c = 3 * g + j
                        fn(qw[d][:, c, :], cb[d][:, j, :], EXP, bias=hsc[:, d, 0, c:c + 1], scale=-1.0).then_inc(q_decay, 1)
                act.wait_ge(e_masked, n.next(e_masked, 2))
                for d in range(2):
                    for j in range(3):
                        c = 3 * g + j
                        fn(pr[d][:, c, :], tm[d][:, j, :], EXP, bias=hcol[:, 0, d, c:c + 1], scale=-1.0).then_inc(e_ready, 1)

            def read_even(mlstm, c):
                i = 2 + c % 2
                full(i)
                if mlstm:
                    fn(num[:, c, :, :], mb[i][:, 0:258].rearrange("p (d n) -> p d n", d=2), COPY).then_inc(mb_free[i], 1)
                else:
                    fn(num[:, c, 0, 0:CH], mb[i][:, 0:CH], COPY).then_inc(mb_free[i], 1)

            def tail_even(mlstm, h):
                act.wait_ge(pj_free[2], n.before(pj_free[2]))
                fn(gT[:, :], gT[:, :], ACT.Sigmoid if mlstm else ACT.Silu).then_inc(gate_ready, 1)
                act.wait_ge(ss_ready, n.next(ss_ready))
                fn(hstd[:, :], hss[:, :], ACT.Sqrt, bias=eps[:, :], scale=1.0 / CH).then_inc(hstd_ready, 1)
                for g in range(3):
                    act.wait_ge(hout_ready, n.next(hout_ready))
                    act.dma_start(h_dram[h + (0 if mlstm else 4)][:, tg(g)], hout[g][:, :]).then_inc(h_stored[g], 16)
                    n.next(h_stored[g], 16)

            def head_even(mlstm, h, follows):
                load_states_even(mlstm, h)
                if not mlstm:
                    act.wait_ge(head_set, n.next(head_set))
                    for i in range(4):
                        fn(rt[:, i, :], pos[:, i, :], EXP, scale=rlg[:, i % 2:i % 2 + 1]).then_inc(act_order, 1)
                    for d in range(2):
                        fn(rw[:, 0, d:d + 1], pcol[:, d:d + 1], EXP, scale=rlg[:, d:d + 1]).then_inc(act_order, 1)
                    n.next(act_order, 6)
                    fn(rw[:, 1, :], rlg[:, :], EXP, scale=float(CH)).then_inc(ret_rows, 1)
                s = slot()
                for g in range(3):
                    evacuate(s, g, gT[:, tg(g)])
                    front_even(g, mlstm)
                dves(0, 3)
                dves(2, 3)
                dves(0, 4)
                dves(1, 4)
                if not follows:
                    n.next(front_done, 3)
                    store_states_even(mlstm, h)
                    for c in range(NC):
                        read_even(mlstm, c)
                else:
                    s = slot()
                    act.wait_ge(front_done, n.next(front_done, 3))
                    evacuate(s, 0, qT[:, tg(0)])
                    store_states_even(mlstm, h)
                    evacuate(s, 1, qT[:, tg(1)])
                    evacuate(s, 2, qT[:, tg(2)])
                    s = slot()
                    evacuate(s, 0, kT[:, tg(0)], DK ** -0.5)
                    evacuate(s, 1, kT[:, tg(1)], DK ** -0.5)
                    for c in range(3):
                        read_even(mlstm, c)
                    evacuate(s, 2, kT[:, tg(2)], DK ** -0.5)
                    for c in range(3, 6):
                        read_even(mlstm, c)
                    s = slot()
                    evacuate(s, 0, vT[:, tg(0)])
                    for c in range(6, 9):
                        read_even(mlstm, c)
                    evacuate(s, 1, vT[:, tg(1)])
                    evacuate(s, 2, vT[:, tg(2)])
                dves(4, 3)
                tail_even(mlstm, h)

            def gate_logits(d):
                if d == 0:
                    act.wait_ge(w2_set, n.next(w2_set))
                for g in range(3):
                    full(4)
                    fn(bb[d][:, tg(g)], mb[4][:, 0:TG], IDENT, bias=b2s[:, d:d + 1]).then_inc(mb_free[4], 1)
                settle()

            def gate_logs(d):
                if d == 1:
                    act.wait_ge(bb_ready, n.next(bb_ready))
                link(fn(la[:, :], bb[d][:, :], ACT.Abs))
                link(fn(la[:, :], la[:, :], EXP, scale=-1.0))
                link(fn(la[:, :], la[:, :], ACT.Ln, bias=1.0), z_logs)
                if d == 1:
                    act.wait_ge(bb_ready, n.next(bb_ready))

            def front_odd(g):
                dves(2, 1)
                dves(3, 1)
                for d in range(2):
                    fn(qe[d][:, 3 * g:3 * g + 3, :], g3(bb[d][:, tg(g)]), EXP, scale=1.0 / GLA_TAU).then_inc(eg_ready, 1)
                    fn(ke[d][:, :, :], g3(bb[d][:, tg(g)]), EXP, scale=-1.0 / GLA_TAU).then_inc(eg_ready, 1)
                for d in range(2):
                    full(d)
                    fn(kt[:, d, 3 * g:3 * g + 3, :], g3(mb[d][:, 0:TG]), COPY).then_inc(mb_free[d], 1)
                dves(4, 1)
                dves(0, 1)
                act.wait_ge(front_done, n.next(front_done))

            def step_odd(t):
                if t:
                    act.wait_ge(sg_new, n.next(sg_new))
                    for d, c in enumerate((t, NC - t)):
                        fn(sgs[d][:, :], sg[d][t % 2][:, :], COPY, scale=dc[:, d, 2, c:c + 1]).then_inc(sd_ready, 1)
                if t < 8:
                    dves(0, 1)
                    dves(1, 1)
                full(2)
                if t <= 4:
                    fn(og[:, t, :], mb[2][:, 0:DVG], COPY).then_inc(mb_free[2], 1)
                if t:
                    full(3)
                    if t <= 4:
                        fn(og[:, NC - t, :], mb[3][:, 0:DVG], COPY).then_inc(mb_free[3], 1)

            def tail_odd_std():
                act.wait_ge(ss_ready, n.next(ss_ready))
                fn(hstd[:, :], hss[:, :], ACT.Sqrt, bias=eps[:, :], scale=1.0 / DVG).then_inc(hstd_ready, 1)

            def tail_odd(h):
                act.wait_ge(pj_free[2], n.before(pj_free[2]))
                fn(ogate[:, :, :].rearrange("p i n -> p (i n)"), ogate[:, :, :].rearrange("p i n -> p (i n)"), ACT.Silu).then_inc(gate_ready, 1)
                for i in range(2):
                    for g in range(3):
                        act.wait_ge(hout_ready, n.next(hout_ready))
                        act.dma_start(h_dram[2 * h + i][:, tg(g)], oh[g][:, :]).then_inc(h_stored[g], 16)
                        n.next(h_stored[g], 16)

            def head_odd(h, follows):
                for d in range(2):
                    act.dma_start(sg[d][1][:, :], a["st_gla"][d][h]).then_inc(st_loaded, 16)
                link(fn(dc[:, :, :, :].rearrange("p d i c -> p (d i c)"), bm[:, :, :, :].rearrange("p d i c -> p (d i c)"),
                        EXP, scale=1.0 / GLA_TAU), dc_ready)
                s = slot()
                evacuate(s, 0, ogate[:, 0, tg(0)])
                front_odd(0)
                evacuate(s, 1, ogate[:, 0, tg(1)])
                evacuate(s, 2, ogate[:, 0, tg(2)])
                front_odd(1)
                s = slot()
                evacuate(s, 0, ogate[:, 1, tg(0)])
                evacuate(s, 1, ogate[:, 1, tg(1)])
                front_odd(2)
                evacuate(s, 2, ogate[:, 1, tg(2)])

                def store():
                    act.wait_ge(so_ready, n.next(so_ready, 2))
                    for d in range(2):
                        act.dma_start(a["new_gla"][d][h], sgo[d][:, :]).then_inc(so_stored, 16)
                if not follows:
                    for t in range(NC):
                        step_odd(t)
                        if t == 1:
                            store()
                    tail_odd_std()
                else:
                    for b in range(4):
                        s = slot()
                        for c in range(3):
                            out, scale = ((oq[:, tg(c)], DK ** -0.5), (ok[:, tg(c)], 1.0),
                                          (ov[:, 0, tg(c)], 1.0), (ov[:, 1, tg(c)], 1.0))[b]
                            evacuate(s, c, out, scale)
                            t = 3 * b + c
                            if t < NC:
                                step_odd(t)
                                if t == 1:
                                    store()
                            elif t == NC:
                                gate_logits(0)
                                tail_odd_std()
                            elif t == NC + 1:
                                gate_logs(0)
                                gate_logits(1)
                dves(4, 6)
                if follows:
                    gate_logs(1)
                tail_odd(h)

            def project_out():
                for g in range(3):
                    act.wait_ge(h_stored[g], n.before(h_stored[g]))

                def load(k):
                    act.dma_start(xr[k % 2][:, :], h_dram[k]).then_inc(xr_loaded[k % 2], 16)
                load(0)
                load(1)
                for k in range(KT):
                    act.wait_ge(xr_loaded[k % 2], n.next(xr_loaded[k % 2], 16))
                    fn(xh[:, k, :], xr[k % 2][:, :], COPY).then_inc(xh_ready, 1)
                    act.wait_ge(xl_ready, n.next(xl_ready))
                    if k + 2 < KT:
                        load(k + 2)

                def block_(m, s, odd_):
                    for c in range(3):
                        job(s, c)
                        p = (c + odd_) % 2
                        square(pj[c][:, 0:TG], p, TG)
                        fn(y[:, m, tg(c)], pj[c][:, 0:TG], COPY).then_inc(pj_free[c], 1)
                        n.next(pj_free[c])
                block_(0, slot(), 0)
                block_(1, slot(), 1)
                with n.loop(act, "act.out", 3) as turn:
                    block_(turn * 2 + 2, slot(), 0)
                    block_(turn * 2 + 3, slot(), 1)

            def pads(t, s):
                for c in range(3):
                    job(s, c)
                    if c == 0:
                        fn(padc[t][:, 1:1 + CTX], pj[0][:, 0:CTX], COPY).then_inc(act_order, 1)
                        n.next(act_order)
                    lo = 0 if c == 0 else (c * TG - CTX) // GRID_W
                    hi = ((c + 1) * TG - CTX) // GRID_W
                    off = CTX if c == 0 else 0
                    fn(pad[t][:, 1 + lo:1 + hi, 1:1 + GRID_W],
                       pj[c][:, off:TG].rearrange("p (r w) -> p r w", w=GRID_W), COPY).then_inc(pj_free[c], 1)
                    n.next(pj_free[c])
                fn(tick[:, :], eps[:, :], COPY).then_inc(a_padded, 1)
                act.wait_ge(a_padded, n.next(a_padded))

            def dve_takes(s):
                for c in range(2):
                    n.next(pj_full[c])
                    n.next(pj_free[c])
                n.next(w_used[s])
                n.next(pj_free[2])

            def gelu(t):
                act.wait_ge(conv_done, n.next(conv_done))
                fn(cc[t][:, :], cc[t][:, :], ACT.Gelu_apprx_tanh, bias=cw[:, t, 9:10]).then_inc(gelu_done, 1)

            def upper(t):
                act.wait_ge(pj_free[2], n.before(pj_free[2]))
                fn(hh[:, t, :], cc[t][:, :], COPY).then_inc(hh_ready, 1)

            def pair(with_down):
                pads(0, slot())
                if with_down:
                    for _ in range(2):
                        n.next(w_used[slot()])
                gelu(0)
                dve_takes(slot())
                upper(0)
                pads(1, slot())
                gelu(1)
                dve_takes(slot())
                upper(1)

            def ffn(layer):
                act.dma_start(conv[:, :, :], a["conv"][layer]).then_inc(conv_loaded, 16)
                act.wait_ge(pads_clear, n.next(pads_clear))
                pair(False)
                with n.loop(act, f"act.ffn{layer}", FP - 1):
                    pair(True)
                for half in range(2):
                    n.next(w_used[slot()])
                    for m in range(4):
                        for c in range(3):
                            act.wait_ge(y_new, n.next(y_new))
                            square(y[:, 4 * half + m, tg(c)], (3 * m + c) % 2, TG)
                for i in range(4):
                    dves(i, FP * (6 if i < 3 else 4))

            act.wait_ge(small_loaded, 48)
            link(fn(cond[:, :, :], cond[:, :, :], ACT.Silu), cond_ready)
            act.wait_ge(x_loaded, 16)
            act.wait_ge(consts_made, 1)
            square(y[:, 0, :], 0)
            square(y[:, 1, :], 1)
            with n.loop(act, "act.squares", KT // 2 - 1) as turn:
                square(y[:, turn * 2 + 2, :], 0)
                square(y[:, turn * 2 + 3, :], 1)
            stats()
            pre(0, 0, False)

            act.dma_start(gbias[:, :], a["gbias"]).then_inc(mix_loaded, 16)
            act.dma_start(m0[:, :], a["m0"]).then_inc(mix_loaded, 16)
            act.dma_start(lg[:, :], a["ret_logit"]).then_inc(mix_loaded, 16)
            act.wait_ge(mix_loaded, n.next(mix_loaded, 48))
            s = slot()
            for c in range(3):
                job(s, c)
                link(fn(ig[:, tg(c)], pj[c][0:36, 0:TG], IDENT, bias=gbias[0:36, 0:1]))
                fn(fz[64:100, tg(c)], pj[c][64:100, 0:TG], IDENT, bias=gbias[64:100, 1:2]).then_inc(pj_free[c], 1)
                n.next(pj_free[c])
            act.wait_ge(pj_free[2], n.before(pj_free[2]))
            link(fn(fa[64:100, :], fz[64:100, :], ACT.Abs))
            link(fn(fa[64:100, :], fa[64:100, :], EXP, scale=-1.0))
            link(fn(lgt[:, :], lg[:, :], ACT.Abs))
            link(fn(lgt[:, :], lgt[:, :], EXP, scale=-1.0))
            link(fn(lgt[:, :], lgt[:, :], ACT.Ln, bias=1.0))
            link(fn(fa[64:100, :], fa[64:100, :], ACT.Ln, bias=1.0), gates_logs)
            s = slot()
            for c in range(3):
                evacuate(s, c, qT[:, tg(c)])
            act.wait_ge(gates_rows, 1)
            act.dma_start(a["new_m"][0], mr[0:4, CTX - 1:CTX]).then_inc(m_stored, 16)
            act.dma_start(a["new_m"][1], mr[32:36, 0:1]).then_inc(m_stored, 16)
            link(fn(ur, ur, EXP))
            link(fn(lf, mr, EXP, scale=-1.0))
            link(fn(ms[:, 1, :], ms[:, 1, :], EXP), gates_exp)
            for dest, scale in ((kT, DK ** -0.5), (vT, 1.0)):
                s = slot()
                for c in range(3):
                    evacuate(s, c, dest[:, tg(c)], scale)
            for i in range(3):
                full(i)
                fn(cols[i][:, :, :].rearrange("p c r -> p (c r)"), mb[i][:, 0:36 * NC], COPY).then_inc(mb_free[i], 1)
            full(3)
            fn(scb[:, :, :, :].rearrange("p r a c -> p (r a c)"), mb[3][:, 0:8 * 18], COPY).then_inc(mb_free[3], 1)
            act.wait_ge(m_stored, 32)
            link(fn(tick[:, :], eps[:, :], COPY), cols_ready)
            head_even(True, 0, True)
            with n.loop(act, "act.mlstm", 3) as turn:
                head_even(True, turn + 1, True)
            with n.loop(act, "act.ret", 3) as turn:
                head_even(False, turn, True)
            head_even(False, 3, False)
            project_out()
            stats()
            post(True, True)
            stats()
            pre(0, 1, True)
            ffn(0)
            stats()
            post(False, True)
            stats()
            pre(1, 0, True)
            act.dma_start(w2, a["w2"]).then_inc(mix_loaded, 16)
            act.dma_start(b2[:, :, :], a["b2"]).then_inc(mix_loaded, 16)
            act.wait_ge(x_saved, n.before(x_saved))
            s = slot()
            for c in range(3):
                evacuate(s, c, glr[:, tg(c)])
            for b in range(4):
                s = slot()
                for c in range(3):
                    out, scale = ((oq[:, tg(c)], DK ** -0.5), (ok[:, tg(c)], 1.0),
                                  (ov[:, 0, tg(c)], 1.0), (ov[:, 1, tg(c)], 1.0))[b]
                    evacuate(s, c, out, scale)
                if b < 2:
                    gate_logits(b)
                    gate_logs(b)
            with n.loop(act, "act.odd", 3) as turn:
                head_odd(turn, True)
            head_odd(3, False)
            project_out()
            stats()
            post(False, True)
            stats()
            pre(1, 1, True)
            ffn(1)
            stats()
            post(False, False)
            act.dma_start(a["out_x"], y[:, :, :]).then_inc(out_stored, 16)
            act.wait_ge(out_stored, 16)
            act.wait_ge(so_stored, 16 * 2 * 12)
            for g in range(3):
                act.wait_ge(h_stored[g], n.before(h_stored[g]))
            act.wait_ge(x_saved, n.before(x_saved))

        @block.vector
        def _(dve):
            n = Tally()
            blocks = {"n": 0}
            v = nc.vector

            def link(ins, done=dve_order):
                ins.then_inc(done, 1)
                dve.wait_ge(done, n.next(done))

            def give(ins, free):
                ins.then_inc(free, 1)
                n.next(free)

            def settle(done=dve_order):
                link(v.tensor_copy(tickv[:, :], eps[:, :]), done)

            def slot():
                blocks["n"] += 1
                return (blocks["n"] - 1) % 2

            def passes(count):
                for _ in range(count):
                    n.next(w_used[slot()])
                    n.next(pj_full[0])
                    n.next(pj_full[1])

            def full(i):
                dve.wait_ge(mb_full[i], n.next(mb_full[i]))

            def acts(i, uses=1):
                n.next(mb_full[i], uses)

            def tg(c):
                return slice(c * TG, (c + 1) * TG)

            def add_squares(s, g, width):
                dve.wait_ge(sq_ready[s], n.next(sq_ready[s]))
                link(v.tensor_tensor(ss[:, g], ss[:, g], sq[s][:, 0:width], ALU.add), sq_added[s])

            def stats():
                dve.wait_ge(std_ready, n.next(std_ready))
                link(v.reciprocal(rstd[:, :], std[:, :]), rstd_ready)

            def pre(layer, part):
                g = gains[:, 2 * part, layer, :]
                c0 = mod_column(layer, 3 * part + 1, 0)
                link(v.scalar_tensor_tensor(coef[:, :, :], mod[:, c0:c0 + KT, :], 1.0, b3(g, 2), ALU.add, ALU.mult), coef_ready)
                dve.wait_ge(rb_ready, n.next(rb_ready, 3))

                def scaled(k, s):
                    link(v.tensor_tensor(sq[s][:, :], y[:, k, :], rb[:, :], ALU.mult), t_ready)

                def lower(k, s):
                    dve.wait_ge(xh_ready, n.next(xh_ready))
                    link(v.tensor_tensor(xl[:, k, :], sq[s][:, :], xh[:, k, :].bitcast(f32), ALU.subtract), xl_ready)
                scaled(0, 0)
                scaled(1, 1)
                with n.loop(dve, "dve.pre", KT // 2 - 1) as turn:
                    for s in range(2):
                        lower(turn * 2 + s, s)
                        scaled(turn * 2 + (s + 2), s)
                lower(6, 0)
                lower(7, 1)

            def post(layer, part, squares):
                g = gains[:, 2 * part + 1, layer, :]
                for k0, k1 in ((0, 4), (4, 8)):
                    c0 = mod_column(layer, 3 * part + 2, k0)
                    link(v.tensor_tensor(coef[:, k0:k1, :], mod[:, c0:c0 + 4, :], b3(g[:, k0:k1], 2), ALU.mult))
                link(v.memset(ss[:, :], 0.0))
                dve.wait_ge(rb_ready, n.next(rb_ready, 3))

                def tile(k, s):
                    link(v.tensor_tensor(y[:, k, :], y[:, k, :], rb[:, :], ALU.mult))
                    dve.wait_ge(xr_loaded[s], n.next(xr_loaded[s], 16))
                    link(v.scalar_tensor_tensor(y[:, k, 0:CTX], y[:, k, 0:CTX], coef[:, k, 0:1], xr[s][:, 0:CTX], ALU.mult, ALU.add))
                    link(v.scalar_tensor_tensor(y[:, k, CTX:T], y[:, k, CTX:T], coef[:, k, 1:2], xr[s][:, CTX:T], ALU.mult, ALU.add), y_new)

                with n.loop(dve, "dve.post" if squares else "dve.post_last", KT // 2) as turn:
                    for s in range(2):
                        tile(turn * 2 + s, s)
                        if squares:
                            add_squares(s, slice(0, T), T)

            def conditioning(column):
                dve.wait_ge(ada_used, n.next(ada_used, 4))
                give(v.tensor_tensor(mod[:, bass.ds(column, 4), :], mb[4][:, 0:8].rearrange("p (c g) -> p c g", g=2),
                                     b3(ada_b[:, bass.ds(column, 4)], 2), ALU.add), mb_free[4])

            def bcast(col, g):
                return b3(col[:, 3 * g:3 * g + 3], CH)

            def set_head_mlstm(h):
                for d in range(2):
                    for i in range(3):
                        link(v.tensor_copy(hcol[:, i, d, :], cols[i][:, :, h + 32 * d]))
                    link(v.tensor_copy(hsc[:, d, :, :], scb[:, h + 4 * d, :, :]))
                    link(v.tensor_copy(sel[:, d, :], ident[0:36, bass.ds(h + 32 * d, 1)].broadcast_to([36, 128])),
                         head_set if d else dve_order)

            def set_head_ret(h):
                for d in range(2):
                    link(v.tensor_copy(rlg[:, d:d + 1], lg[:, bass.ds(h + 4 * d, 1)]), head_set if d else dve_order)
                dve.wait_ge(ret_rows, n.next(ret_rows))
                for d in range(2):
                    link(v.tensor_tensor(rt[:, 2 + d, :], rt[:, 2 + d, :], m01[:, d, :], ALU.mult))
                link(v.tensor_tensor(rt[:, 2, :], rt[:, 2, :], rt[:, 3, :], ALU.add))

            def front_mlstm(g):
                r = slice(3 * g, 3 * g + 3)
                full(0)
                for d, done in ((0, link), (1, give)):
                    done(v.tensor_tensor(kw[d][:, r, :], g3(mb[0][:, 0:TG]), bcast(hcol[:, 1, d, :], g), ALU.mult),
                         mb_free[0] if d else dve_order)
                acts(1)
                acts(3)
                acts(4)
                dve.wait_ge(q_decay, n.next(q_decay, 6))
                for d in range(2):
                    link(v.tensor_tensor(tm[d][:, :, :], cb[d][:, :, :], chunk_row(far[:, d, :], 3), ALU.add), e_masked)
                full(2)
                dve.wait_ge(e_ready, n.next(e_ready, 6))
                for d, done in ((0, link), (1, give)):
                    done(v.tensor_tensor(pr[d][:, r, :], pr[d][:, r, :], g3(mb[2][:, 0:TG]), ALU.mult), mb_free[2] if d else dve_order)
                for d in range(2):
                    link(v.tensor_tensor(qw[d][:, r, :], qw[d][:, r, :], g3(qT[:, tg(g)]), ALU.mult), front_done if d else dve_order)

            def front_ret(g):
                r = slice(3 * g, 3 * g + 3)
                full(0)
                for d, done in ((0, link), (1, give)):
                    done(v.tensor_scalar(kw[d][:, r, :], g3(mb[0][:, 0:TG]), rw[:, 0, d:d + 1], None, ALU.mult),
                         mb_free[0] if d else dve_order)
                acts(1)
                full(2)
                give(v.tensor_tensor(pr[0][:, r, :], chunk_row(rt[:, 2, :], 3), g3(mb[2][:, 0:TG]), ALU.mult), mb_free[2])
                for d in range(2):
                    link(v.tensor_tensor(qw[d][:, r, :], chunk_row(rt[:, d, :], 3), g3(qT[:, tg(g)]), ALU.mult), front_done if d else dve_order)

            def states_even(mlstm):
                w = 129 if mlstm else 128
                for t in range(8):
                    i = t % 2
                    full(i)
                    if t == 0:
                        dve.wait_ge(so_stored, n.before(so_stored))
                        n.next(so_stored, 32)
                        link(v.tensor_copy(st[0][:, 0, 0:w], mb[0][:, 0:w]), so_ready)
                        give(v.tensor_copy(st[1][:, 0, 0:w], mb[0][:, 129:129 + w]), mb_free[0])
                        continue
                    if t == 1:
                        dve.wait_ge(st_loaded, n.next(st_loaded, 32))
                    for d, (c, to) in enumerate(((t, t + 1), (NC - t, NC - t - 1))):
                        decay = hsc[:, d, 1, c:c + 1] if mlstm else rw[:, 1, d:d + 1]
                        done = mb_free[i] if d else so_ready if t == 1 else dve_order
                        (give if d else link)(v.scalar_tensor_tensor(st[d][:, to, 0:w], st[d][:, c, 0:w], decay, mb[i][:, 129 * d:129 * d + w],
                                                    ALU.mult, ALU.add), done)

            def head_norm(o, square, width):
                link(v.tensor_tensor(square, o, o, ALU.mult))
                link(v.tensor_reduce(hss[:, :], square, AX.X, ALU.add), ss_ready)
                dve.wait_ge(hstd_ready, n.next(hstd_ready))
                link(v.reciprocal(hrs[:, :], hstd[:, :]))
                link(v.tensor_tensor(o, o, b3(hrs[:, :], width), ALU.mult), o_ready)

            def gated(g, gate, dest):
                full(4)
                dve.wait_ge(h_stored[g], n.before(h_stored[g]))
                n.next(h_stored[g], 16)
                link(v.tensor_tensor(dest[g][:, :], mb[4][:, 0:TG], gate, ALU.mult), hout_ready)

            def head_even(mlstm, h, ada_turn):
                if mlstm:
                    set_head_mlstm(h)
                else:
                    set_head_ret(h)
                for g in range(3):
                    (front_mlstm if mlstm else front_ret)(g)
                states_even(mlstm)
                acts(2, 5)
                acts(3, 4)
                n.next(mb_free[2], 5)
                dve.wait_ge(mb_free[2], n.before(mb_free[2]))
                o = num[:, :, 0, 0:CH]
                if mlstm:
                    link(v.scalar_tensor_tensor(den[:, :, :], num[:, :, :, 128], -1.0, num[:, :, :, 128], ALU.mult, ALU.max))
                    link(v.tensor_tensor(den[:, :, :], den[:, :, :], hcol[:, 2, :, :].rearrange("p d c -> p c d"), ALU.max))
                    link(v.reciprocal(rr[:, :, :], den[:, :, :]))
                    for d in range(2):
                        link(v.tensor_tensor(num[:, :, d, 0:CH], num[:, :, d, 0:CH], b3(rr[:, :, d], CH), ALU.mult))
                    link(v.tensor_tensor(o, o, num[:, :, 1, 0:CH], ALU.add))
                head_norm(o, num[:, :, 1, 0:CH], CH)
                conditioning(ada_turn)
                dve.wait_ge(gate_ready, n.next(gate_ready))
                for g in range(3):
                    gated(g, gT[:, tg(g)], hout)

            def set_gates_odd(h):
                link(v.tensor_copy(b2s[:, :], b2[:, :, h]))
                link(v.tensor_copy(w2s, ada_w[0:48, bass.ds(h * 128, 128)]), w2_set)

            def log_decay(d):
                dve.wait_ge(z_logs, n.next(z_logs))
                link(v.scalar_tensor_tensor(la[:, :], bb[d][:, :], 0.0, la[:, :], ALU.min, ALU.subtract))
                if d == 0:
                    link(v.tensor_tensor_scan(bb[0][:, :], rst[:, 0:T], la[:, :], 0.0, ALU.mult, ALU.add))
                else:
                    link(v.tensor_tensor_scan(bb[1][:, T - 1::-1], rst[:, T:0:-1], la[:, T - 1::-1], 0.0, ALU.mult, ALU.add))
                last, mid = (CH - 1, CH // 2 - 1) if d == 0 else (0, CH // 2)
                link(v.tensor_copy(bm[:, d, 0, :], bb[d][:, last::CH]))
                link(v.tensor_copy(bm[:, d, 2, :], bb[d][:, mid::CH]))
                link(v.tensor_tensor(bm[:, d, 1, :], bm[:, d, 0, :], bm[:, d, 2, :], ALU.subtract))
                link(v.tensor_tensor(g3(bb[d][:, :]), g3(bb[d][:, :]), b3(bm[:, d, 2, :], CH), ALU.subtract), bb_ready)

            def front_odd(g):
                r = slice(3 * g, 3 * g + 3)
                for i in range(2):
                    full(2 + i)
                    if g == 0 and i == 0:
                        for x in range(3):
                            dve.wait_ge(h_stored[x], n.before(h_stored[x]))
                    give(v.tensor_copy(vt[:, r, 128 * i:128 * i + 128], g3(mb[2 + i][:, 0:TG])), mb_free[2 + i])
                dve.wait_ge(eg_ready, n.next(eg_ready, 4))
                for d in range(2):
                    link(v.tensor_tensor(qe[d][:, r, :], qe[d][:, r, :], g3(oq[:, tg(g)]), ALU.mult))
                    link(v.tensor_tensor(ke[d][:, :, :], ke[d][:, :, :], g3(ok[:, tg(g)]), ALU.mult), ke_ready if d else dve_order)
                acts(0)
                acts(1)
                for d in range(2):
                    i = 4 if d == 0 else 0
                    full(i)
                    v.memset(after[:, d:d + 1], 0.0)
                    give(v.copy_predicated(tp[d][:, :, :], chunk_row(m8[:, d, :], 3), g3(mb[i][:, 0:TG])), mb_free[i])
                settle()
                link(v.tensor_tensor(pg[:, r, :], tp[0][:, :, :], tp[1][:, :, :], ALU.add), front_done)

            def step_odd(t):
                if t == 0:
                    dve.wait_ge(so_stored, n.before(so_stored))
                    n.next(so_stored, 32)
                    dve.wait_ge(dc_ready, n.next(dc_ready))
                    for d in range(2):
                        full(d)
                        give(v.tensor_scalar(sgo[d][:, :], mb[d][:, 0:DVG], dc[:, d, 1, 0:1], None, ALU.mult), mb_free[d])
                    acts(2)
                    return
                now, then = t % 2, (t + 1) % 2
                if t == 1:
                    dve.wait_ge(st_loaded, n.next(st_loaded, 32))
                settle(sg_new)
                if t == 1:
                    settle(so_ready)
                    settle(so_ready)
                if t < 8:
                    for d, c in enumerate((t, NC - t)):
                        link(v.tensor_scalar(sgt[d][:, :], sg[d][now][:, :], dc[:, d, 0, c:c + 1], None, ALU.mult))
                    if t > 1:
                        dve.wait_ge(sd_ready, n.next(sd_ready, 2))
                    for d, c in enumerate((t, NC - t)):
                        full(d)
                        give(v.scalar_tensor_tensor(sg[d][then][:, :], mb[d][:, 0:DVG], dc[:, d, 1, c:c + 1], sgt[d][:, :],
                                                    ALU.mult, ALU.add), mb_free[d])
                else:
                    n.next(sd_ready, 4)
                for i, c in ((2, t), (3, NC - t)):
                    if t <= 4:
                        acts(i)
                    else:
                        full(i)
                        give(v.tensor_tensor(og[:, c, :], og[:, c, :], mb[i][:, 0:DVG], ALU.add), mb_free[i])

            def head_odd(h, follows):
                for g in range(3):
                    front_odd(g)
                if follows:
                    set_gates_odd(h + 1)
                for t in range(NC):
                    step_odd(t)
                settle()
                head_norm(og[:, :, :], kt[:, :, :, :].rearrange("p d c n -> p (d c n)").rearrange("p (c n) -> p c n", n=DVG), DVG)
                if follows:
                    acts(4, 6)
                    log_decay(0)
                    log_decay(1)
                dve.wait_ge(gate_ready, n.next(gate_ready))
                for i in range(2):
                    for g in range(3):
                        gated(g, ogate[:, i, tg(g)], oh)

            def project_out():
                for g in range(3):
                    dve.wait_ge(h_stored[g], n.before(h_stored[g]))
                link(v.memset(ss[:, :], 0.0))
                for k in range(KT):
                    s = k % 2
                    dve.wait_ge(xr_loaded[s], n.next(xr_loaded[s], 16))
                    dve.wait_ge(xh_ready, n.next(xh_ready))
                    link(v.tensor_tensor(xl[:, k, :], xr[s][:, :], xh[:, k, :].bitcast(f32), ALU.subtract), xl_ready)
                with n.loop(dve, "dve.out", 4):
                    for j in range(6):
                        add_squares(j % 2, tg(j % 3), TG)
                    for _ in range(2):
                        s = slot()
                        n.next(w_used[s])
                        n.next(pj_full[0])
                        n.next(pj_full[1])

            def conv_tap(t, tap):
                grid = tap < 9
                i, j = (tap // 3, tap % 3) if grid else (1, tap - 9)
                first = tap in (0, 9)
                if grid:
                    src = pad[t][:, i:i + ROWS, j:j + GRID_W]
                    dst = cc[t][:, CTX:T].rearrange("p (r w) -> p r w", w=GRID_W)
                else:
                    src, dst = padc[t][:, j:j + CTX], cc[t][:, 0:CTX]
                w = cw[:, t, 3 * i + j:3 * i + j + 1]
                done = conv_done if tap == 11 else dve_order
                if tap == 0:
                    dve.wait_ge(a_padded, n.next(a_padded))
                if first:
                    link(v.tensor_scalar(dst, src, w, None, ALU.mult), done)
                else:
                    link(v.scalar_tensor_tensor(dst, src, w, dst, ALU.mult, ALU.add), done)

            def value(t, s):
                dve.wait_ge(gelu_done, n.next(gelu_done))
                for c in range(3):
                    full_ = w_used[s] if c == 2 else pj_full[c]
                    dve.wait_ge(full_, n.next(full_))
                    give(v.tensor_tensor(cc[t][:, tg(c)], cc[t][:, tg(c)], pj[c][:, 0:TG], ALU.mult), pj_free[c])
                dve.wait_ge(hh_ready, n.next(hh_ready))
                link(v.tensor_tensor(hl[:, t, :], cc[t][:, :], hh[:, t, :].bitcast(f32), ALU.subtract), hl_ready)

            def act_takes(s):
                n.next(w_used[s])
                for c in range(2):
                    n.next(pj_full[c])

            def down(last):
                for half in range(2):
                    s = slot()
                    for m in range(4):
                        for c in range(3):
                            j = 12 * half + 3 * m + c
                            i = j % 4
                            if m == 3 and c == 2:
                                dve.wait_ge(w_used[s], n.next(w_used[s]))
                            else:
                                full(i)
                            dst = y[:, 4 * half + m, tg(c)]
                            if last:
                                link(v.tensor_tensor(dst, dst, mb[i][:, 0:TG], ALU.add), y_new)
                                if j:
                                    add_squares((j - 1) % 2, tg((j - 1) % 3), TG)
                            else:
                                give(v.tensor_tensor(dst, dst, mb[i][:, 0:TG], ALU.add), mb_free[i])
                                if j % 2:
                                    conv_tap(0, j // 2)
                if last:
                    add_squares(1, tg(2), TG)

            def set_taps(p):
                link(v.tensor_copy(cw[:, :, :], conv[:, bass.ds(p * 2, 2), :]))

            def pair(turn, with_down, column):
                set_taps(turn)
                act_takes(slot())
                if with_down:
                    down(False)
                else:
                    for tap in range(12):
                        conv_tap(0, tap)
                    dve.wait_ge(x_saved, n.next(x_saved, 16))
                    link(v.memset(y[:, :, :], 0.0))
                    link(v.memset(ss[:, :], 0.0))
                value(0, slot())
                act_takes(slot())
                for tap in range(12):
                    conv_tap(1, tap)
                value(1, slot())
                if column is not None:
                    conditioning(column)

            def ffn(layer):
                for t in range(2):
                    link(v.memset(pad[t][:, :, :], 0.0))
                    link(v.memset(padc[t][:, :], 0.0), pads_clear if t else dve_order)
                dve.wait_ge(conv_loaded, n.next(conv_loaded, 16))
                column = 52 if layer == 0 else None
                pair(0, False, column)
                with n.loop(dve, f"dve.ffn{layer}", FP - 1) as turn:
                    pair(turn + 1, True, None if column is None else turn * 4 + 56)
                down(True)

            dve.wait_ge(consts_made, 1)
            link(v.tensor_copy(m8[:, :, :], m01[:, :, :]))
            link(v.memset(ss[:, :], 0.0))
            with n.loop(dve, "dve.squares", KT // 2):
                for s in range(2):
                    add_squares(s, slice(0, T), T)
            dve.wait_ge(small_loaded, 48)
            dve.wait_ge(front_used, ADA_FRONT)
            give(v.tensor_tensor(mod[:, 0:ADA_FRONT, :], mb[4][:, 0:2 * ADA_FRONT].rearrange("p (c g) -> p c g", g=2),
                                 b3(ada_b[:, 0:ADA_FRONT], 2), ALU.add), mb_free[4])
            stats()
            pre(0, 0)

            dve.wait_ge(gates_logs, 1)
            link(v.scalar_tensor_tensor(lf, fz[64:100, :], 0.0, fa[64:100, :], ALU.min, ALU.subtract))
            link(v.scalar_tensor_tensor(lg[:, :], lg[:, :], 0.0, lgt[:, :], ALU.min, ALU.subtract))
            link(v.memset(jr, 0.0))
            link(v.tensor_tensor_scan(fc[0:32, :], rst[0:32, 0:T], lf[0:32, :], 0.0, ALU.mult, ALU.add))
            link(v.tensor_tensor_scan(fc[32:36, T - 1::-1], rst[32:36, T:0:-1], lf[32:36, T - 1::-1], 0.0, ALU.mult, ALU.add))
            link(v.tensor_tensor(gr, ig, fc, ALU.subtract))
            link(v.tensor_copy(jr[0:32, 2 * CH:T:CH], fc[0:32, 2 * CH - 1:T - 1:CH]))
            link(v.tensor_copy(jr[32:36, 2 * CH - 1:T - 1:CH], fc[32:36, 2 * CH:T:CH]))
            link(v.tensor_tensor_scan(crow[0:32, 0:CTX], jr[0:32, 0:CTX], gr[0:32, 0:CTX], 0.0, ALU.add, ALU.max))
            link(v.tensor_tensor_scan(crow[0:32, CTX:T], jr[0:32, CTX:T], gr[0:32, CTX:T], m0[0:32, :], ALU.add, ALU.max))
            link(v.tensor_tensor_scan(crow[32:36, CTX - 1::-1], jr[32:36, CTX - 1::-1], gr[32:36, CTX - 1::-1], 0.0, ALU.add, ALU.max))
            link(v.tensor_tensor_scan(crow[32:36, T - 1:CTX - 1:-1], jr[32:36, T - 1:CTX - 1:-1], gr[32:36, T - 1:CTX - 1:-1],
                                      m0[32:36, :], ALU.add, ALU.max))
            link(v.tensor_tensor(mr, fc, crow[:, :], ALU.add))
            link(v.memset(ms[:, :, :], 0.0))
            link(v.tensor_copy(ms[0:32, 0, 1:2], m0[0:32, :]))
            link(v.tensor_copy(ms[0:32, 0, 2:NC], mr[0:32, 2 * CH - 1:T - 1:CH]))
            link(v.tensor_copy(ms[32:36, 0, NC - 1:NC], m0[32:36, :]))
            link(v.tensor_copy(ms[32:36, 0, 1:NC - 1], mr[32:36, 2 * CH:T:CH]))
            link(v.tensor_copy(cl[0:32, :], crow[0:32, CH - 1:T:CH]))
            link(v.tensor_copy(cl[32:36, :], crow[32:36, 0:T:CH]))
            link(v.tensor_tensor(ms[:, 1, :], ms[:, 0, :], cl[:, :], ALU.subtract))
            link(v.tensor_tensor(g3(ur), g3(gr), b3(cl[:, :], CH), ALU.subtract), gates_rows)
            dve.wait_ge(cols_ready, 1)
            link(v.memset(v1[:, :, 128:129], 1.0))
            for i in range(4):
                acts(i)
            n.next(mb_free[2])
            head_even(True, 0, ADA_FRONT)
            with n.loop(dve, "dve.mlstm", 3) as turn:
                head_even(True, turn + 1, turn * 4 + (ADA_FRONT + 4))
            with n.loop(dve, "dve.ret", 3) as turn:
                head_even(False, turn, turn * 4 + 36)
            head_even(False, 3, 48)
            passes(4 + 7 * 4 + 1)
            project_out()
            stats()
            post(0, 0, True)
            stats()
            pre(0, 1)
            ffn(0)
            stats()
            post(0, 1, True)
            stats()
            pre(1, 0)
            dve.wait_ge(mix_loaded, 48 + 32)
            set_gates_odd(0)
            for d in range(2):
                link(v.memset(tp[d][:, :, :], 0.0))
            acts(4, 6)
            log_decay(0)
            log_decay(1)
            with n.loop(dve, "dve.odd", 3) as turn:
                head_odd(turn, True)
            head_odd(3, False)
            passes(5 + 3 * 6 + 2)
            project_out()
            stats()
            post(1, 0, True)
            stats()
            pre(1, 1)
            ffn(1)
            stats()
            post(1, 1, False)

def even_blocks(w_in):
    gates = np.zeros((D, 128), w_in.dtype)
    for to, off in ((0, 0), (32, 8), (64, 4), (96, 12)):
        gates[:, to:to + 4] = w_in[:, 2048 + off:2052 + off]

    def head(h, part):
        base = 512 * part + (0 if h < 4 else 2064)
        return w_in[:, base + 128 * (h % 4):base + 128 * (h % 4) + 128]
    blocks = [gates] + [head(0, p) for p in range(3)]
    for h in range(8):
        blocks.append(head(h, 3))
        if h < 7:
            blocks += [head(h + 1, p) for p in range(3)]
    return blocks


def odd_blocks(w_in):
    low = np.zeros((D, 128), w_in.dtype)
    low[:, 0:RANK] = w_in[:, 3072:3072 + RANK]
    low[:, 32:32 + RANK] = w_in[:, 3072 + RANK:3072 + 2 * RANK]

    def cols(at):
        return w_in[:, at:at + 128]

    def qkv(h):
        return [cols(128 * h), cols(512 + 128 * h), cols(1024 + 256 * h), cols(1024 + 256 * h + 128)]
    blocks = [low] + qkv(0)
    for h in range(4):
        blocks += [cols(2048 + 256 * h), cols(2048 + 256 * h + 128)]
        if h < 3:
            blocks += qkv(h + 1)
    return blocks


def by_features(w):
    return w.reshape(KT, 128, 128).transpose(1, 0, 2).reshape(128, 1024)


def ffn_blocks(w_in, w_out):
    def a_(t):
        return by_features(w_in[:, 128 * t:128 * t + 128])

    def v_(t):
        return by_features(w_in[:, D_FF + 128 * t:D_FF + 128 * t + 128])

    def down(p):
        pair = w_out[256 * p:256 * p + 256].reshape(2, 128, 2, 512)
        return [pair[:, :, half].transpose(1, 0, 2).reshape(128, 1024) for half in range(2)]
    blocks = []
    for p in range(FP):
        blocks.append(a_(2 * p))
        if p:
            blocks += down(p - 1)
        blocks += [v_(2 * p), a_(2 * p + 1), v_(2 * p + 1)]
    return blocks + down(FP - 1)


_OUTS = {"out_x": (128, KT, T), "new_mlstm": (2, 4, 128, 129), "new_m": (2, 4, 1),
         "new_ret": (2, 4, 128, 128), "new_gla": (2, 4, 128, DVG)}


def kernel(x_prompt, x_sample, c, c_ctx, state_mlstm_C, state_mlstm_n, state_mlstm_m, state_ret,
           state_gla, ada_w, ada_b, norm_mix_pre, norm_mix_post, norm_ffn_pre, norm_ffn_post,
           w_in_even, w_out_even, mlstm_igate_b, mlstm_fgate_b, ret_decay_logit,
           w_in_odd, gla_gate_w2, gla_gate_b, w_out_odd,
           ffn_w_in, ffn_conv_w, ffn_conv_b, ffn_w_out):
    import concourse.bacc as bacc
    from concourse.bass_utils import run_bass_kernel_spmd

    f = np.float32
    tokens = np.concatenate([np.asarray(x_prompt)[0], np.asarray(x_sample)[0]], 0)
    arrays = {"x": tokens.T.reshape(KT, 128, T).transpose(1, 0, 2)}
    arrays["cond"] = np.stack([np.asarray(c_ctx), np.asarray(c)[0]], 1).reshape(KT, 128, 2).transpose(1, 0, 2)
    ada_w, ada_b = np.asarray(ada_w), np.asarray(ada_b)
    ada = np.zeros((96, 128, 1024), ada_w.dtype)
    bias = np.zeros((128, 96), ada_b.dtype)
    for layer in range(2):
        for part in range(6):
            for k in range(KT):
                at, j = mod_column(layer, part, k), 8 * part + k
                ada[at] = by_features(ada_w[layer][:, 128 * j:128 * j + 128])
                bias[:, at] = ada_b[layer][128 * j:128 * j + 128]
    arrays["ada"], arrays["ada_b"] = ada, bias
    arrays["gains"] = np.stack([np.asarray(g).reshape(2, KT, 128) for g in
                                (norm_mix_pre, norm_mix_post, norm_ffn_pre, norm_ffn_post)]).transpose(3, 0, 1, 2)
    w_in, w_out = np.asarray(ffn_w_in), np.asarray(ffn_w_out)
    blocks = [by_features(w) for w in even_blocks(np.asarray(w_in_even)[0])]
    blocks += [by_features(np.asarray(w_out_even)[0][:, 128 * m:128 * m + 128]) for m in range(KT)]
    blocks += ffn_blocks(w_in[0], w_out[0])
    blocks += [by_features(w) for w in odd_blocks(np.asarray(w_in_odd)[0])]
    blocks += [by_features(np.asarray(w_out_odd)[0][:, 128 * m:128 * m + 128]) for m in range(KT)]
    blocks += ffn_blocks(w_in[1], w_out[1])
    arrays["w"] = np.stack(blocks)
    gbias = np.zeros((128, 2), f)
    m0 = np.zeros((36, 1), f)
    for d in range(2):
        gbias[32 * d:32 * d + 4, 0] = np.asarray(mlstm_igate_b)[0, d]
        gbias[64 + 32 * d:68 + 32 * d, 1] = np.asarray(mlstm_fgate_b)[0, d]
        m0[32 * d:32 * d + 4, 0] = np.asarray(state_mlstm_m)[0, 0, d]
    arrays["gbias"], arrays["m0"] = gbias, m0
    arrays["ret_logit"] = np.broadcast_to(np.asarray(ret_decay_logit)[0].reshape(1, 8), (128, 8))
    arrays["st_mlstm"] = np.concatenate([np.asarray(state_mlstm_C)[0, 0], np.asarray(state_mlstm_n)[0, 0][..., None]], -1)
    arrays["st_ret"] = np.asarray(state_ret)[0, 0]
    arrays["st_gla"] = np.asarray(state_gla)[0, 0]
    w2 = np.zeros((48, 512), f)
    w2[0:RANK], w2[32:32 + RANK] = np.asarray(gla_gate_w2)[0, 0], np.asarray(gla_gate_w2)[0, 1]
    arrays["w2"] = w2
    arrays["b2"] = np.asarray(gla_gate_b)[0].reshape(2, 4, 128).transpose(2, 0, 1)
    taps = np.concatenate([np.asarray(ffn_conv_w).reshape(2, 9, D_FF), np.asarray(ffn_conv_b)[:, None]], 1)
    arrays["conv"] = taps.reshape(2, 10, FT, 128).transpose(0, 3, 2, 1)

    nc = bacc.Bacc("TRN2", target_bir_lowering=False, num_devices=1)
    args, feed = {}, {}
    for name, array in arrays.items():
        array = np.ascontiguousarray(array)
        feed[f"in_{name}"] = array
        args[name] = nc.dram_tensor(f"in_{name}", array.shape, mybir.dt.from_np(array.dtype), kind="ExternalInput").ap()
    for name, shape in _OUTS.items():
        args[name] = nc.dram_tensor(f"res_{name}", shape, mybir.dt.float32, kind="ExternalOutput").ap()
    build(nc, args)
    r = run_bass_kernel_spmd(nc, [feed], core_ids=[0])
    got = {name: r.results[0][f"res_{name}"] for name in _OUTS}
    y = got["out_x"].transpose(1, 0, 2).reshape(D, T).T
    states = got["new_mlstm"]
    return (np.ascontiguousarray(y[None, 0:CTX]), np.ascontiguousarray(y[None, CTX:T]),
            np.ascontiguousarray(states[None, None, ..., 0:128]), np.ascontiguousarray(states[None, None, ..., 128]),
            np.ascontiguousarray(got["new_m"][None, None, ..., 0]), got["new_ret"][None, None], got["new_gla"][None, None])
```

```python
import numpy as np
import concourse.bass as bass
from concourse import mybir
from contextlib import ExitStack, contextmanager

D = 1024
KT = D // 128
CTX, LAT = 128, 1024
T = CTX + LAT
CH = 128
NC = T // CH
TG = 384
NG = T // TG
GRID_W = 64
ROWS = LAT // GRID_W
DK = 128
DVG = 256
D_FF = 2816
FT = D_FF // 128
FP = FT // 2
EPS = 1e-6
FAR = 1.0e30
NBLK = 206
ADA_FRONT = 16
RANK = 16
GLA_TAU = 16.0

PER = {'act.ffn0': {'a_padded': 2,
              'act_order': 2,
              'conv_done': 2,
              'pj_free0': 4,
              'pj_free1': 4,
              'pj_free2': 4,
              'pj_full0': 4,
              'pj_full1': 4,
              'w_used0': 3,
              'w_used1': 3},
 'act.ffn1': {'a_padded': 2,
              'act_order': 2,
              'conv_done': 2,
              'pj_free0': 4,
              'pj_free1': 4,
              'pj_free2': 4,
              'pj_full0': 4,
              'pj_full1': 4,
              'w_used0': 3,
              'w_used1': 3},
 'act.mlstm': {'act_order': 3,
               'e_masked': 6,
               'front_done': 3,
               'h_stored0': 16,
               'h_stored1': 16,
               'h_stored2': 16,
               'head_set': 1,
               'hout_ready': 3,
               'mb_full0': 8,
               'mb_full1': 8,
               'mb_full2': 8,
               'mb_full3': 7,
               'mb_full4': 4,
               'pj_free0': 4,
               'pj_free1': 4,
               'pj_free2': 4,
               'pj_full0': 4,
               'pj_full1': 4,
               'so_ready': 2,
               'ss_ready': 1,
               'w_used0': 2,
               'w_used1': 2},
 'act.odd': {'act_order': 6,
             'bb_ready': 2,
             'dc_ready': 1,
             'front_done': 3,
             'h_stored0': 32,
             'h_stored1': 32,
             'h_stored2': 32,
             'hout_ready': 6,
             'la_free': 2,
             'mb_full0': 15,
             'mb_full1': 12,
             'mb_full2': 13,
             'mb_full3': 12,
             'mb_full4': 11,
             'pj_free0': 6,
             'pj_free1': 6,
             'pj_free2': 6,
             'pj_full0': 6,
             'pj_full1': 6,
             'sg_new': 8,
             'so_ready': 2,
             'ss_ready': 1,
             'w2_set': 1,
             'w_used0': 3,
             'w_used1': 3,
             'z_logs': 2},
 'act.out': {'pj_free0': 2, 'pj_free1': 2, 'pj_free2': 2, 'pj_full0': 2, 'pj_full1': 2, 'w_used0': 1, 'w_used1': 1},
 'act.ret': {'act_order': 6,
             'front_done': 3,
             'h_stored0': 16,
             'h_stored1': 16,
             'h_stored2': 16,
             'head_set': 1,
             'hout_ready': 3,
             'mb_full0': 8,
             'mb_full1': 8,
             'mb_full2': 8,
             'mb_full3': 4,
             'mb_full4': 1,
             'pj_free0': 4,
             'pj_free1': 4,
             'pj_free2': 4,
             'pj_full0': 4,
             'pj_full1': 4,
             'so_ready': 2,
             'ss_ready': 1,
             'w_used0': 2,
             'w_used1': 2},
 'dve.ffn0': {'a_padded': 2,
              'ada_used': 4,
              'conv_done': 2,
              'dve_order': 23,
              'gelu_done': 2,
              'hh_ready': 2,
              'hl_ready': 2,
              'mb_free0': 6,
              'mb_free1': 6,
              'mb_free2': 6,
              'mb_free3': 6,
              'mb_free4': 1,
              'mb_full0': 6,
              'mb_full1': 6,
              'mb_full2': 6,
              'mb_full3': 4,
              'pj_free0': 2,
              'pj_free1': 2,
              'pj_free2': 2,
              'pj_full0': 4,
              'pj_full1': 4,
              'w_used0': 3,
              'w_used1': 3},
 'dve.ffn1': {'a_padded': 2,
              'conv_done': 2,
              'dve_order': 23,
              'gelu_done': 2,
              'hh_ready': 2,
              'hl_ready': 2,
              'mb_free0': 6,
              'mb_free1': 6,
              'mb_free2': 6,
              'mb_free3': 6,
              'mb_full0': 6,
              'mb_full1': 6,
              'mb_full2': 6,
              'mb_full3': 4,
              'pj_free0': 2,
              'pj_free1': 2,
              'pj_free2': 2,
              'pj_full0': 4,
              'pj_full1': 4,
              'w_used0': 3,
              'w_used1': 3},
 'dve.mlstm': {'ada_used': 4,
               'dve_order': 32,
               'e_masked': 6,
               'e_ready': 18,
               'front_done': 3,
               'gate_ready': 1,
               'h_stored0': 16,
               'h_stored1': 16,
               'h_stored2': 16,
               'head_set': 1,
               'hout_ready': 3,
               'hstd_ready': 1,
               'mb_free0': 7,
               'mb_free1': 4,
               'mb_free2': 8,
               'mb_free4': 1,
               'mb_full0': 8,
               'mb_full1': 8,
               'mb_full2': 8,
               'mb_full3': 7,
               'mb_full4': 4,
               'o_ready': 1,
               'q_decay': 18,
               'so_ready': 2,
               'so_stored': 32,
               'ss_ready': 1,
               'st_loaded': 32},
 'dve.odd': {'bb_ready': 2,
             'dc_ready': 1,
             'dve_order': 38,
             'eg_ready': 12,
             'front_done': 3,
             'gate_ready': 1,
             'h_stored0': 32,
             'h_stored1': 32,
             'h_stored2': 32,
             'hout_ready': 6,
             'hstd_ready': 1,
             'ke_ready': 3,
             'la_free': 2,
             'mb_free0': 11,
             'mb_free1': 8,
             'mb_free2': 7,
             'mb_free3': 7,
             'mb_free4': 3,
             'mb_full0': 15,
             'mb_full1': 12,
             'mb_full2': 13,
             'mb_full3': 12,
             'mb_full4': 11,
             'o_ready': 1,
             'sd_ready': 16,
             'sg_new': 8,
             'so_ready': 2,
             'so_stored': 32,
             'ss_ready': 1,
             'st_loaded': 32,
             'w2_set': 1,
             'z_logs': 2},
 'dve.ret': {'ada_used': 4,
             'dve_order': 18,
             'front_done': 3,
             'gate_ready': 1,
             'h_stored0': 16,
             'h_stored1': 16,
             'h_stored2': 16,
             'head_set': 1,
             'hout_ready': 3,
             'hstd_ready': 1,
             'mb_free0': 7,
             'mb_free1': 4,
             'mb_free2': 8,
             'mb_free4': 1,
             'mb_full0': 8,
             'mb_full1': 8,
             'mb_full2': 8,
             'mb_full3': 4,
             'mb_full4': 1,
             'o_ready': 1,
             'ret_rows': 1,
             'so_ready': 2,
             'so_stored': 32,
             'ss_ready': 1,
             'st_loaded': 32},
 'pe.ffn0': {'ada_loaded': 64,
             'hl_ready': 2,
             'mb_free0': 6,
             'mb_free1': 6,
             'mb_free2': 6,
             'mb_free3': 6,
             'mb_free4': 1,
             'pj_free0': 4,
             'pj_free1': 4,
             'pj_free2': 4,
             'w_ready0': 3,
             'w_ready1': 3},
 'pe.ffn1': {'hl_ready': 2,
             'mb_free0': 6,
             'mb_free1': 6,
             'mb_free2': 6,
             'mb_free3': 6,
             'pj_free0': 4,
             'pj_free1': 4,
             'pj_free2': 4,
             'w_ready0': 3,
             'w_ready1': 3},
 'pe.mlstm': {'ada_loaded': 64,
              'front_done': 3,
              'head_set': 1,
              'hout_ready': 3,
              'mb_free0': 7,
              'mb_free1': 7,
              'mb_free2': 8,
              'mb_free3': 7,
              'mb_free4': 4,
              'o_ready': 1,
              'pj_free0': 4,
              'pj_free1': 4,
              'pj_free2': 4,
              'w_ready0': 2,
              'w_ready1': 2},
 'pe.odd': {'front_done': 3,
            'hout_ready': 6,
            'ke_ready': 3,
            'mb_free0': 14,
            'mb_free1': 11,
            'mb_free2': 12,
            'mb_free3': 11,
            'mb_free4': 9,
            'o_ready': 1,
            'pj_free0': 6,
            'pj_free1': 6,
            'pj_free2': 6,
            'sd_ready': 16,
            'w2_set': 1,
            'w_ready0': 3,
            'w_ready1': 3},
 'pe.out': {'pj_free0': 2, 'pj_free1': 2, 'pj_free2': 2, 'w_ready0': 1, 'w_ready1': 1},
 'pe.ret': {'ada_loaded': 64,
            'front_done': 3,
            'hout_ready': 3,
            'mb_free0': 7,
            'mb_free1': 7,
            'mb_free2': 8,
            'mb_free3': 4,
            'mb_free4': 1,
            'o_ready': 1,
            'pj_free0': 4,
            'pj_free1': 4,
            'pj_free2': 4,
            'w_ready0': 2,
            'w_ready1': 2},
 'pool.split': {'raw_loaded0': 16, 'raw_loaded1': 16, 'w_hi0': 1, 'w_hi1': 1, 'w_used0': 1, 'w_used1': 1},
 'sp.ffn1': {'w_ready0': 3, 'w_ready1': 3},
 'sp.ffn_b': {'ada_used': 4, 'w_ready0': 3, 'w_ready1': 3},
 'sp.heads': {'ada_used': 4, 'w_ready0': 2, 'w_ready1': 2},
 'sp.odd': {'w_ready0': 3, 'w_ready1': 3},
 'sp.out0': {'w_ready0': 1, 'w_ready1': 1},
 'sp.out1': {'w_ready0': 1, 'w_ready1': 1}}


class Tally:

    def __init__(self):
        self.count, self.turn, self.per = {}, None, {}

    def before(self, sem):
        at = self.count.get(sem.name, 0)
        if self.turn is not None and self.per.get(sem.name, 0):
            return self.turn * self.per[sem.name] + at
        return at

    def next(self, sem, by=1):
        self.count[sem.name] = self.count.get(sem.name, 0) + by
        return self.before(sem)

    @contextmanager
    def loop(self, engine, name, turns):
        start = dict(self.count)
        self.per = PER.get(name, {})
        with engine.Fori(0, turns) as turn:
            self.turn = turn
            yield turn
        found = {k: v - start.get(k, 0) for k, v in self.count.items() if v != start.get(k, 0)}
        assert found == self.per, (name, found)
        for k, v in found.items():
            self.count[k] += v * (turns - 1)
        self.turn, self.per = None, {}


def mod_column(layer, part, k):
    j = 8 * part + k
    if layer == 0:
        return j if j < 16 else j + 4
    return j + 52 if j < 44 else j - 28


def build(nc, a):
    f32, f32r = mybir.dt.float32, mybir.dt.float32r
    u8 = mybir.dt.uint8
    ALU = mybir.AluOpType
    ACT = mybir.ActivationFunctionType
    AX = mybir.AxisListType

    x_saved_dram = nc.dram_tensor("residual_scratch", [128, KT, T], f32, kind="Internal").ap()
    h_dram = nc.dram_tensor("mixer_scratch", [KT, 128, T], f32, kind="Internal").ap()

    ctx = ExitStack()
    with ctx:
        def sem(name):
            return ctx.enter_context(nc.semaphore(name))

        def sb(name, shape, dt=f32, scope=ctx):
            return scope.enter_context(nc.sbuf_tensor(name, shape, dt))

        xh = sb("xh", [128, KT, T], f32r)
        same = ExitStack()
        xt = sb("xt", [128, KT, T], scope=same)
        same.close()
        xl = sb("xl", [128, KT, T], f32r)
        wh = [sb(f"wh{s}", [128, 1024], f32r) for s in range(2)]
        wl = [sb(f"wl{s}", [128, 1024], f32r) for s in range(2)]
        raw = [sb(f"raw{s}", [128, 1024]) for s in range(2)]
        ada_w = sb("ada_w", [128, 1024])
        ident = sb("ident", [128, 128])
        ones = sb("ones", [128, 1])
        after = sb("after", [128, 2])
        tickp = sb("tickp", [128, 1])
        eps = sb("eps", [128, 1])
        tick = sb("tick", [128, 1])
        tickv = sb("tickv", [128, 1])
        cond = sb("cond", [128, KT, 2])
        mod = sb("mod", [128, 96, 2])
        ada_b = sb("ada_b", [128, 96])
        gains = sb("gains", [128, 4, 2, KT])
        sumsq = sb("sumsq", [128, 6, 3])
        std = sb("std", [128, 6, 3])
        rstd = sb("rstd", [128, 6, 3])
        coef_in = sb("coef_in", [128, KT, 2])
        coef_out = sb("coef_out", [128, KT, 2])
        cw = sb("cw", [128, 2, 10])
        rst = sb("rst", [128, T + 1])
        far = sb("far", [128, 2, CH])
        m01 = sb("m01", [128, 2, CH])
        m8 = sb("m8", [128, 2, CH], u8)
        pos = sb("pos", [128, 4, CH])
        pcol = sb("pcol", [128, 2])
        hss = sb("hss", [128, NC])
        hstd = sb("hstd", [128, NC])
        hrs = sb("hrs", [128, NC])

        rows_scope = ExitStack()
        y = sb("y", [128, KT, T], scope=rows_scope)
        norm_scope = ExitStack()
        diag = sb("diag", [128, 3, CH], scope=norm_scope)
        xg0 = sb("xg0", [128, KT, TG], scope=norm_scope)
        front = sb("front", [128, 8, 1024], scope=norm_scope)
        norm_scope.close()
        ffn_scope = ExitStack()
        sb("under_norm", [128, TG + KT * TG], scope=ffn_scope)
        heads_scope = ExitStack()
        xr = [sb(f"xr{s}", [128, T], scope=heads_scope) for s in range(2)]
        heads_scope.close()
        hh = sb("hh", [128, 2, T], f32r, scope=ffn_scope)
        hl = sb("hl", [128, 2, T], f32r, scope=ffn_scope)
        group_scope = ExitStack()
        xg1 = sb("xg1", [128, KT, TG], scope=group_scope)
        group_scope.close()
        pad = [sb(f"pad{t}", [128, ROWS + 2, GRID_W + 2], scope=ffn_scope) for t in range(2)]
        padc = [sb(f"padc{t}", [128, CTX + 2], scope=ffn_scope) for t in range(2)]
        cc = [sb(f"cc{t}", [128, T], scope=ffn_scope) for t in range(2)]
        conv = pos[:, :, :].rearrange("p n i -> p (n i)")[:, 0:FT * 10].rearrange("p (f n) -> p f n", n=10)
        ffn_scope.close()
        rows_scope.close()
        xg = [xg0, xg1, xg0]

        even = ExitStack()
        qT = sb("qT", [128, T], scope=even)
        kT = sb("kT", [128, T], scope=even)
        vT = sb("vT", [128, T], scope=even)
        gT = sb("gT", [128, T], scope=even)
        hout = [sb(f"hout{s}", [128, TG], scope=even) for s in range(3)]
        kw = [sb(f"kw{d}", [128, NC, CH], scope=even) for d in range(2)]
        v1 = sb("v1", [128, NC, 129], scope=even)
        pr = [sb(f"pr{d}", [128, NC, CH], scope=even) for d in range(2)]
        qw = [sb(f"qw{d}", [128, NC, CH], scope=even) for d in range(2)]
        st = [sb(f"st{d}", [128, NC, 129], scope=even) for d in range(2)]
        num = sb("num", [128, NC, 2, 129], scope=even)
        cb = [sb(f"cb{d}", [128, 3, CH], scope=even) for d in range(2)]
        tm = [sb(f"tm{d}", [128, 3, CH], scope=even) for d in range(2)]
        crow = sb("crow", [36, T], scope=even)
        cols = [sb(f"cols{n}", [128, NC, 36], scope=even) for n in range(3)]
        hcol = sb("hcol", [128, 3, 2, NC], scope=even)
        scb = sb("scb", [128, 8, 2, NC], scope=even)
        hsc = sb("hsc", [128, 2, 2, NC], scope=even)
        sel = sb("sel", [36, 2, 128], scope=even)
        den = sb("den", [128, NC, 2], scope=even)
        rr = sb("rr", [128, NC, 2], scope=even)
        gbias = sb("gbias", [128, 2], scope=even)
        m0 = sb("m0", [36, 1], scope=even)
        ms = sb("ms", [36, 2, NC], scope=even)
        cl = sb("cl", [36, NC], scope=even)
        lg = sb("lg", [128, 8], scope=even)
        lgt = sb("lgt", [128, 8], scope=even)
        rt = sb("rt", [128, 4, CH], scope=even)
        rlg = sb("rlg", [128, 2], scope=even)
        rw = sb("rw", [128, 2, 2], scope=even)
        ig = qw[0][:, :, :].rearrange("p c n -> p (c n)")[0:36, :]
        lf = qw[1][:, :, :].rearrange("p c n -> p (c n)")[0:36, :]
        fz = kw[0][:, :, :].rearrange("p c n -> p (c n)")
        fa = kw[1][:, :, :].rearrange("p c n -> p (c n)")
        fc = pr[0][:, :, :].rearrange("p c n -> p (c n)")[0:36, :]
        jr = pr[1][:, :, :].rearrange("p c n -> p (c n)")[0:36, :]
        mr = st[0][:, :, :].rearrange("p c n -> p (c n)")[0:36, 0:T]
        ur = st[1][:, :, :].rearrange("p c n -> p (c n)")[0:36, 0:T]
        gr = num[:, :, :, :].rearrange("p c d n -> p (c d n)")[0:36, 0:T]
        even.close()

        odd = ExitStack()
        oq = sb("oq", [128, T], scope=odd)
        ok = sb("ok", [128, T], scope=odd)
        ov = sb("ov", [128, 2, T], scope=odd)
        ogate = sb("ogate", [128, 2, T], scope=odd)
        bb = [sb(f"bb{d}", [128, T], scope=odd) for d in range(2)]
        qe = [sb(f"qe{d}", [128, NC, CH], scope=odd) for d in range(2)]
        kt = sb("kt", [128, 2, NC, CH], scope=odd)
        og = sb("og", [128, NC, DVG], scope=odd)
        tp = [sb(f"tp{d}", [128, 3, CH], scope=odd) for d in range(2)]
        sg = [[sb(f"sg{d}{s}", [128, DVG], scope=odd) for s in range(2)] for d in range(2)]
        sgo = [sb(f"sgo{d}", [128, DVG], scope=odd) for d in range(2)]
        dc = sb("dc", [128, 2, 3, NC], scope=odd)
        bm = sb("bm", [128, 2, 3, NC], scope=odd)
        glr = sb("glr", [48, T], scope=odd)
        w2 = ada_w[0:48, 0:4 * DK]
        w2s = ada_w[0:48, 4 * DK:5 * DK]
        b2 = sb("b2", [128, 2, 4], scope=odd)
        b2s = sb("b2s", [128, 2], scope=odd)
        la = [ov[:, d, :] for d in range(2)]
        pg = sb("pg", [128, NC, CH], scope=odd)
        own = ExitStack()
        ke = [sb(f"ke{d}", [128, 3, CH], scope=own) for d in range(2)]
        own.close()
        own = ExitStack()
        sgs = [sb(f"sgs{d}", [128, DVG], scope=own) for d in range(2)]
        sgt = [sb(f"sgt{d}", [128, DVG], scope=own) for d in range(2)]
        own.close()
        sb("under_sgs", [128, 4 * DVG], scope=odd)
        own = ExitStack()
        vt = sb("vt", [128, NC, DVG], scope=own)
        own.close()
        own = ExitStack()
        oh = [sb(f"oh{s}", [128, TG], scope=own) for s in range(3)]
        own.close()
        sb("under_vt", [128, NC * DVG], scope=odd)
        odd.close()

        bank = [ctx.enter_context(nc.psum_tensor(f"bank{i}", [128, 512], f32)) for i in range(8)]
        pj, mb = bank[0:3], bank[3:8]

        def sems(names):
            return [sem(x) for x in names.split()]

        consts_made, small_loaded, x_loaded, cond_ready = sems("consts_made small_loaded x_loaded cond_ready")
        front_loaded = [sem(f"front_loaded{s}") for s in range(8)]
        front_used = sem("front_used")
        raw_loaded = [sem(f"raw_loaded{s}") for s in range(2)]
        w_hi = [sem(f"w_hi{s}") for s in range(2)]
        w_ready = [sem(f"w_ready{s}") for s in range(2)]
        w_used = [sem(f"w_used{s}") for s in range(2)]
        ada_loaded, ada_used = sems("ada_loaded ada_used")
        la_free = sem("la_free")
        pj_full = [sem(f"pj_full{c}") for c in range(2)]
        pj_free = [sem(f"pj_free{c}") for c in range(3)]
        mb_full = [sem(f"mb_full{i}") for i in range(5)]
        mb_free = [sem(f"mb_free{i}") for i in range(5)]
        act_order, dve_order, pool_order = sems("act_order dve_order pool_order")
        gram_full, sum_ready = sems("gram_full sum_ready")
        std_ready, rstd_ready, rb_full, x_new = sems("std_ready rstd_ready rb_full x_new")
        coef_ready, t_ready, xh_ready, xl_ready, x_saved = sems("coef_ready t_ready xh_ready xl_ready x_saved")
        xr_loaded = [sem(f"xr_loaded{s}") for s in range(2)]
        xg_loaded = [sem(f"xg_loaded{g}") for g in range(3)]
        y_new, out_stored = sems("y_new out_stored")
        conv_loaded, a_padded, conv_done, gelu_done, hh_ready, hl_ready, pads_clear = sems(
            "conv_loaded a_padded conv_done gelu_done hh_ready hl_ready pads_clear")
        mix_loaded, gates_logs, gates_rows, gates_exp, m_stored, cols_ready = sems(
            "mix_loaded gates_logs gates_rows gates_exp m_stored cols_ready")
        head_set, q_decay, e_masked, e_ready, front_done, ret_rows = sems(
            "head_set q_decay e_masked e_ready front_done ret_rows")
        st_loaded, so_ready, so_stored = sems("st_loaded so_ready so_stored")
        ss_ready, hstd_ready, o_ready, gate_ready, hout_ready = sems("ss_ready hstd_ready o_ready gate_ready hout_ready")
        h_stored = [sem(f"h_stored{g}") for g in range(3)]
        z_logs, bb_ready, w2_set, eg_ready, ke_ready, sd_ready, sg_new, dc_ready = sems(
            "z_logs bb_ready w2_set eg_ready ke_ready sd_ready sg_new dc_ready")

        block = ctx.enter_context(nc.Block())

        def b3(ap, n):
            return ap.rearrange("p (c o) -> p c o", o=1).broadcast_to([ap.shape[0], ap.shape[1], n])

        def g3(ap):
            return ap.rearrange("p (c n) -> p c n", n=CH)

        def chunk_row(ap, n):
            return ap.rearrange("p (o i) -> p o i", o=1).broadcast_to([ap.shape[0], n, CH])

        GRAM_BANK = {0: 2, 1: 2, 2: 1, 3: 2, 4: 1, 5: 2}
        NORM_BANK = {0: 4, 1: 4, 2: 3, 3: 4, 4: 0, 5: 3}

        @block.sync
        def _(sp):
            seen = Tally()
            state = {"n": 0, "ada": ADA_FRONT}

            def weights(n, s):
                sp.wait_ge(w_ready[s], seen.before(w_ready[s]))
                seen.next(w_ready[s])
                sp.dma_start(raw[s][:, :], a["w"][n]).then_inc(raw_loaded[s], 16)

            def ada(n):
                if seen.count.get(ada_used.name, 0):
                    sp.wait_ge(ada_used, seen.before(ada_used))
                seen.next(ada_used)
                sp.dma_start(ada_w[:, :], a["ada"][n]).then_inc(ada_loaded, 16)

            def stream(name, turns, pattern):
                nw, na, n0, a0 = pattern.count("w"), pattern.count("a"), state["n"], state["ada"]

                def once(turn):
                    w, c = 0, 0
                    for what in pattern:
                        if what == "w":
                            weights(turn * nw + (n0 + w), (n0 + w) % 2)
                            w += 1
                        else:
                            ada(turn * na + (a0 + c))
                            c += 1
                if turns == 1:
                    once(0)
                else:
                    with seen.loop(sp, "sp." + name, turns) as turn:
                        once(turn)
                state["n"] += turns * nw
                state["ada"] += turns * na

            sp.dma_start(cond[:, :, :], a["cond"]).then_inc(small_loaded, 16)
            sp.dma_start(ada_b[:, :], a["ada_b"]).then_inc(small_loaded, 16)
            sp.dma_start(gains[:, :, :, :], a["gains"]).then_inc(small_loaded, 16)
            for n in range(8):
                sp.dma_start(front[:, n, :], a["ada"][n]).then_inc(front_loaded[n], 16)
            sp.dma_start(y[:, :, :], a["x"]).then_inc(x_loaded, 16)
            for n in range(8, ADA_FRONT):
                sp.wait_ge(front_used, n - 7)
                sp.dma_start(front[:, n % 8, :], a["ada"][n]).then_inc(front_loaded[n % 8], 16)
            stream("first", 1, "wwawawaa")
            stream("head0", 1, "wawawawa")
            stream("heads", 6, "wawawawa")
            stream("last", 1, "waaaa")
            stream("out0", 4, "ww")
            stream("ffn_a", 1, "wawawawa")
            stream("ffn_b", FP - 1, "wawwwawawa")
            stream("ffn_c", 1, "ww")
            stream("odd_first", 1, "wwwww")
            stream("odd", 3, "wwwwww")
            stream("odd_last", 1, "ww")
            stream("out1", 4, "ww")
            stream("ffn1", FP, "wwwwww")
            assert state["n"] == NBLK and state["ada"] == 96, state

        @block.gpsimd
        def _(pool):
            made = Tally()

            def link(ins):
                ins.then_inc(pool_order, 1)
                pool.wait_ge(pool_order, made.next(pool_order))

            link(nc.gpsimd.memset(ident[:, :], 0.0))
            link(nc.gpsimd.affine_select(out=ident[:, :], in_=ident[:, :], compare_op=ALU.not_equal, fill=1.0,
                                         base=0, pattern=[[-1, 128]], channel_multiplier=1))
            link(nc.gpsimd.memset(eps[:, :], EPS))
            link(nc.gpsimd.memset(far[:, :, :], 0.0))
            link(nc.gpsimd.memset(m01[:, :, :], 1.0))
            for d, (cm, step) in enumerate(((-1, 1), (1, -1))):
                for tile, fill in ((far, FAR), (m01, 0.0)):
                    link(nc.gpsimd.affine_select(out=tile[:, d, :], in_=tile[:, d, :], compare_op=ALU.is_ge, fill=fill,
                                                 base=0, pattern=[[step, CH]], channel_multiplier=cm))
            for n, (step, base, cm) in enumerate(((1, 1, 0), (-1, CH, 0), (1, 0, -1), (-1, 0, 1))):
                link(nc.gpsimd.iota(pos[:, n, :], [[step, CH]], base=base, channel_multiplier=cm,
                                    allow_small_or_imprecise_dtypes=True))
            for n, (base, cm) in enumerate(((CH - 1, -1), (0, 1))):
                link(nc.gpsimd.iota(pcol[:, n:n + 1], [[0, 1]], base=base, channel_multiplier=cm,
                                    allow_small_or_imprecise_dtypes=True))
            link(nc.gpsimd.memset(rst[:, :], 1.0))
            link(nc.gpsimd.memset(rst[:, 0:T + 1:CH], 0.0))
            link(nc.gpsimd.memset(ones[:, :], 1.0))
            nc.gpsimd.memset(tickp[:, :], 0.0).then_inc(consts_made, 1)

            def split(s):
                pool.wait_ge(raw_loaded[s], made.next(raw_loaded[s], 16))
                pool.wait_ge(w_used[s], made.before(w_used[s]))
                made.next(w_used[s])
                nc.gpsimd.tensor_tensor(wh[s][:, :], raw[s][:, :], ones[:, 0:1].broadcast_to([128, 1024]), ALU.mult).then_inc(w_hi[s], 1)
                pool.wait_ge(w_hi[s], made.next(w_hi[s]))
                nc.gpsimd.tensor_tensor(wl[s][:, :], raw[s][:, :], wh[s][:, :].bitcast(f32), ALU.subtract).then_inc(w_ready[s], 1)

            split(0)
            split(1)
            with made.loop(pool, "pool.split", NBLK // 2 - 1):
                for s in range(2):
                    split(s)

        @block.tensor
        def _(pe):
            n = Tally()
            blocks = {"n": 0}

            def mm(out, lhsT, rhs, start=True, stop=True):
                return nc.tensor.matmul(out, lhsT, rhs, start=start, stop=stop)

            def exact(out, w_hi_, w_lo_, x_hi_, x_lo_, start, stop):
                mm(out, w_hi_, x_hi_, start, False)
                mm(out, w_hi_, x_lo_, False, False)
                return mm(out, w_lo_, x_hi_, False, stop)

            def slot():
                blocks["n"] += 1
                return (blocks["n"] - 1) % 2

            def project(s, c):
                if c == 0:
                    pe.wait_ge(w_ready[s], n.next(w_ready[s]))
                pe.wait_ge(pj_free[c], n.before(pj_free[c]))
                n.next(pj_free[c])
                g = slice(c * TG, (c + 1) * TG)
                for k in range(KT):
                    w = slice(k * 128, (k + 1) * 128)
                    last = exact(pj[c][:, 0:TG], wh[s][:, w], wl[s][:, w], xh[:, k, g], xl[:, k, g], k == 0, k == KT - 1)
                last.then_inc(w_used[s] if c == 2 else pj_full[c], 1)

            def project_first(s):
                def part(c):
                    if c == 0:
                        pe.wait_ge(w_ready[s], n.next(w_ready[s]))
                    pe.wait_ge(pj_free[c], n.before(pj_free[c]))
                    n.next(pj_free[c])
                    g = slice(c * TG, (c + 1) * TG)
                    for k in range(KT):
                        if k % 2 == 0:
                            pe.wait_ge(xl_ready, n.next(xl_ready))
                        w = slice(k * 128, (k + 1) * 128)
                        last = exact(pj[c][:, 0:TG], wh[s][:, w], wl[s][:, w], xh[:, k, g], xl[:, k, g], k == 0, k == KT - 1)
                    last.then_inc(w_used[s] if c == 2 else pj_full[c], 1)
                return part

            def project_heads(s):
                pe.wait_ge(w_ready[s], n.next(w_ready[s]))
                for c in range(3):
                    pe.wait_ge(pj_free[c], n.before(pj_free[c]))
                    n.next(pj_free[c])
                for k in range(KT):
                    pe.wait_ge(xl_ready, n.next(xl_ready))
                    w = slice(k * 128, (k + 1) * 128)
                    for c in range(3):
                        g = slice(c * TG, (c + 1) * TG)
                        last = exact(pj[c][:, 0:TG], wh[s][:, w], wl[s][:, w], xh[:, k, g], xl[:, k, g], k == 0, k == KT - 1)
                        if k == KT - 1:
                            last.then_inc(w_used[s] if c == 2 else pj_full[c], 1)

            def project_all(s):
                for c in range(3):
                    project(s, c)

            def claim(i):
                pe.wait_ge(mb_free[i], n.before(mb_free[i]))
                n.next(mb_free[i])

            def outputs_taken():
                pe.wait_ge(hout_ready, n.before(hout_ready))

            def ada(j):
                if j == 0:
                    claim(4)
                pe.wait_ge(ada_loaded, n.next(ada_loaded, 16))
                for k in range(KT):
                    last = mm(mb[4][:, 2 * j:2 * j + 2], ada_w[:, k * 128:(k + 1) * 128], cond[:, k, :], k == 0, k == KT - 1)
                last.then_inc(ada_used, 1)

            def gram(norm, g):
                i = GRAM_BANK[norm]
                pe.wait_ge(mb_free[i], n.before(mb_free[i]))
                for c in range(3):
                    at = g * TG + c * CH
                    for k in range(KT):
                        last = mm(mb[i][:, c * CH:(c + 1) * CH], y[:, k, at:at + CH], y[:, k, at:at + CH], k == 0, k == KT - 1)
                last.then_inc(gram_full, 1)

            def gram_new(norm, g):
                pe.wait_ge(x_new, n.next(x_new))
                gram(norm, g)

            def spread(norm):
                i = NORM_BANK[norm]
                pe.wait_ge(mb_free[i], n.before(mb_free[i]))
                pe.wait_ge(rstd_ready, n.next(rstd_ready))
                for c in range(3):
                    last = mm(mb[i][:, c * CH:(c + 1) * CH], rstd[:, norm, c:c + 1].broadcast_to([128, 128]), ident[:, :])
                last.then_inc(rb_full, 1)

            def boundary(last_part, first_part):
                part, part_ready = last_part
                part(0)
                part(1)
                part_ready(0)
                gram(0, 0)
                spread(0)
                part(2)
                part_ready(1)
                gram(1, 1)
                spread(1)
                if first_part is None:
                    part_ready(2)
                    gram(3, 2)
                    spread(3)
                    return
                gram_new(2, 0)
                part_ready(2)
                gram(3, 2)
                spread(2)
                spread(3)
                gram_new(4, 1)
                spread(4)
                gram_new(5, 2)
                spread(5)
                first_part(0)
                first_part(1)
                first_part(2)

            def chunk(g, j):
                return slice((3 * g + j) * CH, (3 * g + j + 1) * CH)

            def third(j):
                return slice(j * CH, (j + 1) * CH)

            def front_even(g, mlstm):
                if g == 0:
                    for c in range(3):
                        pe.wait_ge(pj_free[c], n.before(pj_free[c]))
                claim(0)
                for j in range(3):
                    last = nc.tensor.transpose(mb[0][:, third(j)], kT[:, chunk(g, j)], ident[:, :])
                last.then_inc(mb_full[0], 1)
                claim(1)
                for j in range(3):
                    last = nc.tensor.transpose(mb[1][:, third(j)], vT[:, chunk(g, j)], ident[:, :])
                last.then_inc(mb_full[1], 1)
                claim(2)
                for j in range(3):
                    last = mm(mb[2][:, third(j)], kT[:, chunk(g, j)], qT[:, chunk(g, j)])
                last.then_inc(mb_full[2], 1)
                if mlstm:
                    if g == 0:
                        pe.wait_ge(head_set, n.next(head_set))
                    for d in range(2):
                        claim(3 + d)
                        mm(mb[3 + d][:, 0:TG], sel[:, d, :], crow[:, g * TG:(g + 1) * TG]).then_inc(mb_full[3 + d], 1)

            def update_even(t, w):
                i = t % 2
                if t == 0:
                    pe.wait_ge(front_done, n.next(front_done, 3))
                    pe.wait_ge(mb_free[1], n.before(mb_free[1]))
                claim(i)
                for d, c in enumerate((t, NC - t if t else 0)):
                    last = mm(mb[i][:, 129 * d:129 * d + w], kw[d][:, c, :], v1[:, c, 0:w])
                last.then_inc(mb_full[i], 1)

            def read_mlstm(c):
                if c == 0:
                    for i in range(2):
                        pe.wait_ge(mb_free[i], n.before(mb_free[i]))
                i = 2 + c % 2
                claim(i)
                for d in range(2):
                    out = mb[i][:, 129 * d:129 * d + 129]
                    last = mm(out, pr[d][:, c, :], v1[:, c, :], True, c == 0)
                    if c:
                        last = mm(out, qw[d][:, c, :], st[d][:, c, :], False, True)
                last.then_inc(mb_full[i], 1)

            def read_ret(c):
                if c == 0:
                    for i in range(2):
                        pe.wait_ge(mb_free[i], n.before(mb_free[i]))
                i = 2 + c % 2
                claim(i)
                out = mb[i][:, 0:128]
                last = mm(out, pr[0][:, c, :], v1[:, c, 0:128], True, c == 0)
                if c:
                    mm(out, qw[0][:, c, :], st[0][:, c, 0:128], False, False)
                    last = mm(out, qw[1][:, c, :], st[1][:, c, 0:128], False, True)
                last.then_inc(mb_full[i], 1)

            def out_even():
                pe.wait_ge(o_ready, n.next(o_ready))
                for g, i in enumerate((4, 0, 1)):
                    pe.wait_ge(mb_free[i], n.before(mb_free[i]))
                    n.next(hout_ready)
                    for j in range(3):
                        last = nc.tensor.transpose(mb[i][:, third(j)], num[:, 3 * g + j, 0, 0:128], ident[:, :])
                    last.then_inc(mb_full[i], 1)

            def head_even(mlstm, first=False, follows=True):
                read = read_mlstm if mlstm else read_ret
                w = 129 if mlstm else 128
                s = slot()
                project(s, 0)
                if not first:
                    out_even()
                project(s, 1)
                if not first:
                    outputs_taken()
                front_even(0, mlstm)
                project(s, 2)
                front_even(1, mlstm)
                if not follows:
                    front_even(2, mlstm)
                    for j in range(4):
                        ada(j)
                    for t in range(8):
                        update_even(t, w)
                    for c in range(NC):
                        read(c)
                    return
                s = slot()
                project(s, 0)
                front_even(2, mlstm)
                project(s, 1)
                ada(0)
                update_even(0, w)
                update_even(1, w)
                project(s, 2)
                update_even(2, w)
                update_even(3, w)
                ada(1)
                s = slot()
                project(s, 0)
                update_even(4, w)
                update_even(5, w)
                project(s, 1)
                update_even(6, w)
                update_even(7, w)
                project(s, 2)
                for c in range(3):
                    read(c)
                ada(2)
                s = slot()
                for g in range(2):
                    project(s, g)
                    for c in range(3 * g + 3, 3 * g + 6):
                        read(c)
                project(s, 2)
                ada(3)

            def gate_logits(d):
                if d == 0:
                    pe.wait_ge(w2_set, n.next(w2_set))
                for g in range(3):
                    claim(4)
                    mm(mb[4][:, 0:TG], w2s[32 * d:32 * d + RANK, :], glr[32 * d:32 * d + RANK, g * TG:(g + 1) * TG])\
                        .then_inc(mb_full[4], 1)

            def front_odd(g):
                if g == 0:
                    for c in range(3):
                        pe.wait_ge(pj_free[c], n.before(pj_free[c]))
                for i in range(2):
                    claim(2 + i)
                    for j in range(3):
                        last = nc.tensor.transpose(mb[2 + i][:, third(j)], ov[:, i, chunk(g, j)], ident[:, :])
                    last.then_inc(mb_full[2 + i], 1)
                pe.wait_ge(ke_ready, n.next(ke_ready))
                for d in range(2):
                    claim(d)
                    for j in range(3):
                        last = nc.tensor.transpose(mb[d][:, third(j)], ke[d][:, j, :], ident[:, :])
                    last.then_inc(mb_full[d], 1)
                for d in range(2):
                    i = 4 if d == 0 else 0
                    claim(i)
                    for j in range(3):
                        last = mm(mb[i][:, third(j)], ke[d][:, j, :], qe[d][:, 3 * g + j, :])
                    last.then_inc(mb_full[i], 1)

            def step_odd(t):
                if t == 0:
                    pe.wait_ge(front_done, n.next(front_done, 3))
                    for i in range(4):
                        pe.wait_ge(mb_free[i], n.before(mb_free[i]))
                back = NC - t if t else 0
                if t < 8:
                    for d, c in enumerate((t, back)):
                        claim(d)
                        mm(mb[d][:, 0:DVG], kt[:, d, c, :], vt[:, c, :]).then_inc(mb_full[d], 1)
                claim(2)
                last = mm(mb[2][:, 0:DVG], pg[:, t, :], vt[:, t, :], True, t == 0)
                if t:
                    pe.wait_ge(sd_ready, n.next(sd_ready, 2))
                    last = mm(mb[2][:, 0:DVG], qe[0][:, t, :], sgs[0][:, :], False, True)
                last.then_inc(mb_full[2], 1)
                if t:
                    claim(3)
                    mm(mb[3][:, 0:DVG], qe[1][:, back, :], sgs[1][:, :]).then_inc(mb_full[3], 1)

            def out_odd():
                pe.wait_ge(o_ready, n.next(o_ready))
                for m, b in enumerate((4, 0, 1, 2, 3, 4)):
                    i, g = m // 3, m % 3
                    if m < 5:
                        pe.wait_ge(mb_free[b], n.before(mb_free[b]))
                    else:
                        pe.wait_ge(hout_ready, n.before(hout_ready) - 4)
                    n.next(hout_ready)
                    for j in range(3):
                        last = nc.tensor.transpose(mb[b][:, third(j)], og[:, 3 * g + j, 128 * i:128 * i + 128], ident[:, :])
                    last.then_inc(mb_full[b], 1)

            def head_odd(first=False, follows=True):
                s = slot()
                project(s, 0)
                if not first:
                    out_odd()
                project(s, 1)
                if not first:
                    outputs_taken()
                front_odd(0)
                project(s, 2)
                s = slot()
                project(s, 0)
                front_odd(1)
                project(s, 1)
                front_odd(2)
                project(s, 2)
                if not follows:
                    for t in range(NC):
                        step_odd(t)
                else:
                    for b in range(4):
                        s = slot()
                        for c in range(3):
                            project(s, c)
                            t = 3 * b + c
                            if t < NC:
                                step_odd(t)
                            if t < 2:
                                gate_logits(t)

            def project_out():
                project_heads(slot())
                with n.loop(pe, "pe.out", 3):
                    project_all(slot())
                    project_all(slot())
                s = slot()
                return lambda c: project(s, c), lambda c: pe.wait_ge(pj_free[c], n.before(pj_free[c]))

            def down():
                pe.wait_ge(hl_ready, n.next(hl_ready, 2))
                for half in range(2):
                    s = slot()
                    pe.wait_ge(w_ready[s], n.next(w_ready[s]))
                    for m in range(4):
                        for c in range(3):
                            j = 12 * half + 3 * m + c
                            i = j % 4
                            pe.wait_ge(mb_free[i], n.before(mb_free[i]))
                            n.next(mb_free[i])
                            g = slice(c * TG, (c + 1) * TG)
                            for t in range(2):
                                w = slice(t * 512 + m * 128, t * 512 + m * 128 + 128)
                                ins = exact(mb[i][:, 0:TG], wh[s][:, w], wl[s][:, w], hh[:, t, g], hl[:, t, g], t == 0, t == 1)
                            ins.then_inc(w_used[s] if m == 3 and c == 2 else mb_full[i], 1)

            def down_last():
                slots = (slot(), slot())

                def part(c):
                    if c == 0:
                        pe.wait_ge(hl_ready, n.next(hl_ready, 2))
                    for half, s in enumerate(slots):
                        if c == 0:
                            pe.wait_ge(w_ready[s], n.next(w_ready[s]))
                        for m in range(4):
                            j = 8 * c + 4 * half + m
                            i = j % 2
                            if j < 2:
                                pe.wait_ge(mb_free[i], n.before(mb_free[i]))
                            else:
                                pe.wait_ge(y_new, n.next(y_new))
                            g = slice(c * TG, (c + 1) * TG)
                            for t in range(2):
                                w = slice(t * 512 + m * 128, t * 512 + m * 128 + 128)
                                ins = exact(mb[i][:, 0:TG], wh[s][:, w], wl[s][:, w], hh[:, t, g], hl[:, t, g], t == 0, t == 1)
                            ins.then_inc(w_used[s] if m == 3 and c == 2 else mb_full[i], 1)

                def part_ready(c):
                    if c == 2:
                        pe.wait_ge(y_new, n.next(y_new, 2))
                return part, part_ready

            def ffn(layer):
                with_ada = layer == 0
                if with_ada:
                    ada(0)
                for j in range(1, 4):
                    project_all(slot())
                    if with_ada:
                        ada(j)
                with n.loop(pe, f"pe.ffn{layer}", FP - 1):
                    project_all(slot())
                    if with_ada:
                        ada(0)
                    down()
                    for j in range(1, 4):
                        project_all(slot())
                        if with_ada:
                            ada(j)
                return down_last()

            def ada_front(blocks_):
                for b in blocks_:
                    s = b % 8
                    pe.wait_ge(front_loaded[s], n.next(front_loaded[s], 16))
                    for k in range(KT):
                        last = mm(mb[4][:, 2 * b:2 * b + 2], front[:, s, k * 128:(k + 1) * 128], cond[:, k, :], k == 0, k == KT - 1)
                    last.then_inc(front_used, 1)

            pe.wait_ge(consts_made, 1)
            pe.wait_ge(cond_ready, 1)
            ada_front(range(8))
            pe.wait_ge(x_loaded, 16)
            for b, (norm, g) in enumerate(((2, 0), (4, 1), (5, 2))):
                gram(norm, g)
                ada_front((8 + b,))
                spread(norm)
            ada_front(range(11, ADA_FRONT))
            n.next(mb_free[4])
            gates = project_first(slot())
            for g in range(3):
                gates(g)
            for j in range(3):
                project_all(slot())
                ada(j)
            ada(3)
            pe.wait_ge(gates_exp, 1)
            for i, rows in enumerate((gr, ur, lf)):
                claim(i)
                for c in range(NC):
                    last = nc.tensor.transpose(mb[i][:, 36 * c:36 * c + 36], rows[:, c * CH:(c + 1) * CH], ident[0:36, 0:36])
                last.then_inc(mb_full[i], 1)
            claim(3)
            for r in range(8):
                row = 32 * (r // 4) + r % 4
                last = mm(mb[3][:, 18 * r:18 * r + 18], ident[0:36, row:row + 1].broadcast_to([36, 128]),
                          ms[:, :, :].rearrange("p a c -> p (a c)"))
            last.then_inc(mb_full[3], 1)
            head_even(True, first=True)
            with n.loop(pe, "pe.mlstm", 3):
                head_even(True)
            with n.loop(pe, "pe.ret", 3):
                head_even(False)
            head_even(False, follows=False)
            out_even()
            out = project_out()
            boundary(out, project_first(slot()))
            out = ffn(0)
            boundary(out, project_first(slot()))
            for b in range(4):
                project_all(slot())
                if b < 2:
                    gate_logits(b)
            head_odd(first=True)
            with n.loop(pe, "pe.odd", 2):
                head_odd()
            head_odd(follows=False)
            out_odd()
            out = project_out()
            boundary(out, project_first(slot()))
            boundary(ffn(1), None)

        @block.scalar
        def _(act):
            n = Tally()
            blocks = {"n": 0}
            COPY, EXP, IDENT = ACT.Copy, ACT.Exp, ACT.Identity
            fn = nc.scalar.activation

            def link(ins, done=act_order):
                ins.then_inc(done, 1)
                act.wait_ge(done, n.next(done))

            def settle():
                link(fn(tick[:, :], eps[:, :], COPY))

            def slot():
                blocks["n"] += 1
                return (blocks["n"] - 1) % 2

            def full(i):
                act.wait_ge(mb_full[i], n.next(mb_full[i]))

            def dves(i, uses):
                n.next(mb_full[i], uses)

            def job(s, c):
                full_ = w_used[s] if c == 2 else pj_full[c]
                act.wait_ge(full_, n.next(full_))

            def evacuate(s, c, out, scale=1.0):
                job(s, c)
                fn(out, pj[c][0:out.shape[0], 0:TG], COPY, scale=scale).then_inc(pj_free[c], 1)
                n.next(pj_free[c])

            def tg(c):
                return slice(c * TG, (c + 1) * TG)

            def rms(norm):
                act.wait_ge(sum_ready, n.next(sum_ready))
                fn(std[:, norm, :], sumsq[:, norm, :], ACT.Sqrt, bias=eps[:, :], scale=1.0 / D).then_inc(std_ready, 1)

            def load_group(g, source):
                act.dma_start(xg[g][:, :, :], source[:, :, tg(g)]).then_inc(xg_loaded[g], 16)

            def pre(layer, part, g):
                if g == 0:
                    act.wait_ge(coef_ready, n.next(coef_ready))
                shift = mod_column(layer, 3 * part, 0)
                act.wait_ge(t_ready, n.next(t_ready))
                for q in range(4):
                    for k in range(2 * q, 2 * q + 2):
                        for col, lo, hi in ((0, 0, CTX), (1, CTX, TG)) if g == 0 else ((1, 0, TG),):
                            tile = xt[:, k, g * TG + lo:g * TG + hi]
                            fn(tile, tile, IDENT, bias=mod[:, k + shift, col:col + 1],
                               scale=coef_in[:, k, col:col + 1]).then_inc(act_order, 1)
                            n.next(act_order)
                    act.wait_ge(act_order, n.before(act_order))
                    two = slice(2 * q, 2 * q + 2)
                    fn(xh[:, two, tg(g)], xt[:, two, tg(g)], COPY).then_inc(xh_ready, 1)
                n.next(xl_ready, 4)

            def save(g):
                act.dma_start(x_saved_dram[:, :, tg(g)], y[:, :, tg(g)]).then_inc(x_saved, 16)
                n.next(x_saved, 16)

            def boundary(evacuate_last, source, layer, part):
                act.wait_ge(x_saved, n.before(x_saved))
                load_group(0, source)
                load_group(1, source)
                for g in range(3):
                    evacuate_last(g)
                    if g:
                        rms(g - 1)
                act.wait_ge(x_new, n.next(x_new))
                load_group(2, source)
                if layer is None:
                    act.dma_start(a["out_x"][:, :, tg(0)], y[:, :, tg(0)]).then_inc(out_stored, 16)
                    rms(3)
                    for g in (1, 2):
                        act.wait_ge(x_new, n.next(x_new))
                        act.dma_start(a["out_x"][:, :, tg(g)], y[:, :, tg(g)]).then_inc(out_stored, 16)
                    return
                save(0)
                rms(2)
                rms(3)
                act.wait_ge(x_new, n.next(x_new))
                save(1)
                pre(layer, part, 0)
                rms(4)
                act.wait_ge(x_new, n.next(x_new))
                save(2)
                rms(5)
                pre(layer, part, 1)
                pre(layer, part, 2)

            def load_states_even(mlstm, h):
                for d in range(2):
                    c = 1 if d == 0 else NC - 1
                    source = a["st_mlstm"][d] if mlstm else a["st_ret"][d]
                    act.dma_start(st[d][:, c, 0:(129 if mlstm else 128)], source[h]).then_inc(st_loaded, 16)

            def store_states_even(mlstm, h):
                act.wait_ge(so_ready, n.next(so_ready, 2))
                for d in range(2):
                    dest = a["new_mlstm"][d] if mlstm else a["new_ret"][d]
                    act.dma_start(dest[h], st[d][:, 0, 0:(129 if mlstm else 128)]).then_inc(so_stored, 16)

            def front_even(g, mlstm):
                full(1)
                fn(v1[:, 3 * g:3 * g + 3, 0:CH], g3(mb[1][:, 0:TG]), COPY).then_inc(mb_free[1], 1)
                if not mlstm:
                    return
                for d in range(2):
                    full(3 + d)
                    fn(cb[d][:, :, :], g3(mb[3 + d][:, 0:TG]), COPY).then_inc(mb_free[3 + d], 1)
                settle()
                if g == 0:
                    act.wait_ge(head_set, n.next(head_set))
                for d in range(2):
                    for j in range(3):
                        c = 3 * g + j
                        fn(qw[d][:, c, :], cb[d][:, j, :], EXP, bias=hsc[:, d, 0, c:c + 1], scale=-1.0).then_inc(q_decay, 1)
                act.wait_ge(e_masked, n.next(e_masked, 2))
                for d in range(2):
                    for j in range(3):
                        c = 3 * g + j
                        fn(pr[d][:, c, :], tm[d][:, j, :], EXP, bias=hcol[:, 0, d, c:c + 1], scale=-1.0).then_inc(e_ready, 1)

            def read_even(mlstm, c):
                i = 2 + c % 2
                full(i)
                if mlstm:
                    fn(num[:, c, :, :], mb[i][:, 0:258].rearrange("p (d n) -> p d n", d=2), COPY).then_inc(mb_free[i], 1)
                else:
                    fn(num[:, c, 0, 0:CH], mb[i][:, 0:CH], COPY).then_inc(mb_free[i], 1)

            def tail_even(mlstm, h):
                act.wait_ge(pj_free[2], n.before(pj_free[2]))
                fn(gT[:, :], gT[:, :], ACT.Sigmoid if mlstm else ACT.Silu).then_inc(gate_ready, 1)
                act.wait_ge(ss_ready, n.next(ss_ready))
                fn(hstd[:, :], hss[:, :], ACT.Sqrt, bias=eps[:, :], scale=1.0 / CH).then_inc(hstd_ready, 1)
                for g in range(3):
                    act.wait_ge(hout_ready, n.next(hout_ready))
                    act.dma_start(h_dram[h + (0 if mlstm else 4)][:, tg(g)], hout[g][:, :]).then_inc(h_stored[g], 16)
                    n.next(h_stored[g], 16)

            def head_even(mlstm, h, follows):
                load_states_even(mlstm, h)
                if not mlstm:
                    act.wait_ge(head_set, n.next(head_set))
                    for i in range(4):
                        fn(rt[:, i, :], pos[:, i, :], EXP, scale=rlg[:, i % 2:i % 2 + 1]).then_inc(act_order, 1)
                    for d in range(2):
                        fn(rw[:, 0, d:d + 1], pcol[:, d:d + 1], EXP, scale=rlg[:, d:d + 1]).then_inc(act_order, 1)
                    n.next(act_order, 6)
                    fn(rw[:, 1, :], rlg[:, :], EXP, scale=float(CH)).then_inc(ret_rows, 1)
                s = slot()
                evacuate(s, 0, gT[:, tg(0)])
                evacuate(s, 1, gT[:, tg(1)])
                front_even(0, mlstm)
                evacuate(s, 2, gT[:, tg(2)])
                front_even(1, mlstm)
                front_even(2, mlstm)
                dves(0, 3)
                dves(2, 3)
                dves(0, 4)
                dves(1, 4)
                if not follows:
                    n.next(front_done, 3)
                    store_states_even(mlstm, h)
                    for c in range(NC):
                        read_even(mlstm, c)
                else:
                    s = slot()
                    act.wait_ge(front_done, n.next(front_done, 3))
                    evacuate(s, 0, qT[:, tg(0)])
                    evacuate(s, 1, qT[:, tg(1)])
                    store_states_even(mlstm, h)
                    evacuate(s, 2, qT[:, tg(2)])
                    s = slot()
                    for g in range(3):
                        evacuate(s, g, kT[:, tg(g)], DK ** -0.5)
                    for c in range(3):
                        read_even(mlstm, c)
                    s = slot()
                    for g in range(2):
                        evacuate(s, g, vT[:, tg(g)])
                        for c in range(3 * g + 3, 3 * g + 6):
                            read_even(mlstm, c)
                    evacuate(s, 2, vT[:, tg(2)])
                for i in (4, 0, 1):
                    dves(i, 1)
                tail_even(mlstm, h)

            def gate_logits(d):
                if d == 0:
                    act.wait_ge(w2_set, n.next(w2_set))
                for g in range(3):
                    full(4)
                    fn(bb[d][:, tg(g)], mb[4][:, 0:TG], IDENT, bias=b2s[:, d:d + 1]).then_inc(mb_free[4], 1)
                settle()

            def gate_logs(d):
                for part in range(3):
                    gate_log(d, part)

            def gate_log(d, part):
                if part == 0:
                    link(fn(la[d][:, :], bb[d][:, :], ACT.Abs))
                elif part == 1:
                    link(fn(la[d][:, :], la[d][:, :], EXP, scale=-1.0))
                else:
                    link(fn(la[d][:, :], la[d][:, :], ACT.Ln, bias=1.0), z_logs)

            def decays_odd(g):
                if g:
                    act.wait_ge(front_done, n.next(front_done))
                for d in range(2):
                    fn(qe[d][:, 3 * g:3 * g + 3, :], g3(bb[d][:, tg(g)]), EXP, scale=1.0 / GLA_TAU).then_inc(eg_ready, 1)
                    fn(ke[d][:, :, :], g3(bb[d][:, tg(g)]), EXP, scale=-1.0 / GLA_TAU).then_inc(eg_ready, 1)

            def keys_odd(g):
                dves(2, 1)
                dves(3, 1)
                for d in range(2):
                    full(d)
                    fn(kt[:, d, 3 * g:3 * g + 3, :], g3(mb[d][:, 0:TG]), COPY).then_inc(mb_free[d], 1)
                dves(4, 1)
                dves(0, 1)
                if g == 2:
                    act.wait_ge(front_done, n.next(front_done))

            def step_odd(t):
                if t:
                    act.wait_ge(sg_new, n.next(sg_new))
                    for d, c in enumerate((t, NC - t)):
                        fn(sgs[d][:, :], sg[d][t % 2][:, :], COPY, scale=dc[:, d, 2, c:c + 1]).then_inc(sd_ready, 1)
                if t < 8:
                    dves(0, 1)
                    dves(1, 1)
                full(2)
                if t <= 4:
                    fn(og[:, t, :], mb[2][:, 0:DVG], COPY).then_inc(mb_free[2], 1)
                if t:
                    full(3)
                    if t <= 4:
                        fn(og[:, NC - t, :], mb[3][:, 0:DVG], COPY).then_inc(mb_free[3], 1)

            def silu_gate():
                act.wait_ge(pj_free[2], n.before(pj_free[2]))
                fn(ogate[:, :, :].rearrange("p i n -> p (i n)"), ogate[:, :, :].rearrange("p i n -> p (i n)"), ACT.Silu).then_inc(gate_ready, 1)

            def tail_odd_std():
                act.wait_ge(ss_ready, n.next(ss_ready))
                fn(hstd[:, :], hss[:, :], ACT.Sqrt, bias=eps[:, :], scale=1.0 / DVG).then_inc(hstd_ready, 1)

            def tail_odd(h):
                for i in range(2):
                    for g in range(3):
                        act.wait_ge(hout_ready, n.next(hout_ready))
                        act.dma_start(h_dram[2 * h + i][:, tg(g)], oh[g][:, :]).then_inc(h_stored[g], 16)
                        n.next(h_stored[g], 16)

            def head_odd(h, follows):
                act.wait_ge(bb_ready, n.next(bb_ready, 2))
                for d in range(2):
                    act.dma_start(sg[d][1][:, :], a["st_gla"][d][h]).then_inc(st_loaded, 16)
                link(fn(dc[:, :, :, :].rearrange("p d i c -> p (d i c)"), bm[:, :, :, :].rearrange("p d i c -> p (d i c)"),
                        EXP, scale=1.0 / GLA_TAU), dc_ready)
                s = slot()
                evacuate(s, 0, ogate[:, 0, tg(0)])
                decays_odd(0)
                evacuate(s, 1, ogate[:, 0, tg(1)])
                keys_odd(0)
                decays_odd(1)
                evacuate(s, 2, ogate[:, 0, tg(2)])
                s = slot()
                evacuate(s, 0, ogate[:, 1, tg(0)])
                keys_odd(1)
                decays_odd(2)
                evacuate(s, 1, ogate[:, 1, tg(1)])
                keys_odd(2)
                evacuate(s, 2, ogate[:, 1, tg(2)])

                def store():
                    act.wait_ge(so_ready, n.next(so_ready, 2))
                    for d in range(2):
                        act.dma_start(a["new_gla"][d][h], sgo[d][:, :]).then_inc(so_stored, 16)
                if not follows:
                    for t in range(NC):
                        step_odd(t)
                        if t == 1:
                            store()
                    silu_gate()
                    tail_odd_std()
                else:
                    for b in range(4):
                        s = slot()
                        for c in range(3):
                            out, scale = ((oq[:, tg(c)], DK ** -0.5), (ok[:, tg(c)], 1.0),
                                          (ov[:, 0, tg(c)], 1.0), (ov[:, 1, tg(c)], 1.0))[b]
                            if b >= 2 and c == 0:
                                act.wait_ge(la_free, n.next(la_free))
                            evacuate(s, c, out, scale)
                            t = 3 * b + c
                            if t < NC:
                                step_odd(t)
                                if t == 1:
                                    store()
                            if t < 2:
                                gate_logits(t)
                            if 1 <= t < 7:
                                gate_log((t - 1) // 3, (t - 1) % 3)
                            if t == NC - 1:
                                silu_gate()
                            if t == NC:
                                tail_odd_std()
                for i in range(5):
                    dves(i, 2 if i == 4 else 1)
                tail_odd(h)

            def project_out():
                for g in range(3):
                    act.wait_ge(h_stored[g], n.before(h_stored[g]))

                def load(k):
                    act.dma_start(xr[k % 2][:, :], h_dram[k]).then_inc(xr_loaded[k % 2], 16)
                load(0)
                load(1)
                for k in range(KT):
                    act.wait_ge(xr_loaded[k % 2], n.next(xr_loaded[k % 2], 16))
                    fn(xh[:, k, :], xr[k % 2][:, :], COPY).then_inc(xh_ready, 1)
                    act.wait_ge(xl_ready, n.next(xl_ready))
                    if k + 2 < KT:
                        load(k + 2)

                def evacuate_tile(m, s, c):
                    job(s, c)
                    fn(y[:, m, tg(c)], pj[c][:, 0:TG], COPY).then_inc(pj_free[c], 1)
                    n.next(pj_free[c])
                for c in range(3):
                    s = slot() if c == 0 else s
                    evacuate_tile(0, s, c)
                with n.loop(act, "act.out", 3) as turn:
                    for m in range(2):
                        s = slot()
                        for c in range(3):
                            evacuate_tile(turn * 2 + (m + 1), s, c)
                s = slot()

                def last_block(c):
                    evacuate_tile(7, s, c)
                return last_block

            def pads(t, s):
                for c in range(3):
                    job(s, c)
                    if c == 0:
                        fn(padc[t][:, 1:1 + CTX], pj[0][:, 0:CTX], COPY).then_inc(act_order, 1)
                        n.next(act_order)
                    lo = 0 if c == 0 else (c * TG - CTX) // GRID_W
                    hi = ((c + 1) * TG - CTX) // GRID_W
                    off = CTX if c == 0 else 0
                    fn(pad[t][:, 1 + lo:1 + hi, 1:1 + GRID_W],
                       pj[c][:, off:TG].rearrange("p (r w) -> p r w", w=GRID_W), COPY).then_inc(pj_free[c], 1)
                    n.next(pj_free[c])
                fn(tick[:, :], eps[:, :], COPY).then_inc(a_padded, 1)
                act.wait_ge(a_padded, n.next(a_padded))

            def dve_takes(s):
                for c in range(2):
                    n.next(pj_full[c])
                    n.next(pj_free[c])
                n.next(w_used[s])
                n.next(pj_free[2])

            def gelu(t):
                act.wait_ge(conv_done, n.next(conv_done))
                fn(cc[t][:, :], cc[t][:, :], ACT.Gelu_apprx_tanh, bias=cw[:, t, 9:10]).then_inc(gelu_done, 1)

            def upper(t):
                act.wait_ge(pj_free[2], n.before(pj_free[2]))
                fn(hh[:, t, :], cc[t][:, :], COPY).then_inc(hh_ready, 1)

            def pair(with_down):
                pads(0, slot())
                if with_down:
                    for _ in range(2):
                        n.next(w_used[slot()])
                gelu(0)
                dve_takes(slot())
                upper(0)
                pads(1, slot())
                gelu(1)
                dve_takes(slot())
                upper(1)

            def ffn(layer):
                act.dma_start(conv[:, :, :], a["conv"][layer]).then_inc(conv_loaded, 16)
                act.wait_ge(pads_clear, n.next(pads_clear))
                pair(False)
                with n.loop(act, f"act.ffn{layer}", FP - 1):
                    pair(True)
                for half in range(2):
                    n.next(w_used[slot()])
                for i, last in enumerate((12, 10, 0, 0)):
                    dves(i, (FP - 1) * (6 if i < 3 else 4) + last)
                act.wait_ge(hl_ready, n.next(hl_ready, FT))
                return lambda c: None

            act.wait_ge(small_loaded, 48)
            link(fn(cond[:, :, :], cond[:, :, :], ACT.Silu), cond_ready)
            act.wait_ge(x_loaded, 16)
            act.wait_ge(consts_made, 1)
            for norm in (2, 4, 5):
                rms(norm)
            for g in range(3):
                pre(0, 0, g)

            act.wait_ge(xl_ready, n.before(xl_ready))
            act.dma_start(gbias[:, :], a["gbias"]).then_inc(mix_loaded, 16)
            act.dma_start(m0[:, :], a["m0"]).then_inc(mix_loaded, 16)
            act.dma_start(lg[:, :], a["ret_logit"]).then_inc(mix_loaded, 16)
            act.wait_ge(mix_loaded, n.next(mix_loaded, 48))
            s = slot()
            for c in range(3):
                job(s, c)
                link(fn(ig[:, tg(c)], pj[c][0:36, 0:TG], IDENT, bias=gbias[0:36, 0:1]))
                fn(fz[64:100, tg(c)], pj[c][64:100, 0:TG], IDENT, bias=gbias[64:100, 1:2]).then_inc(pj_free[c], 1)
                n.next(pj_free[c])
            act.wait_ge(pj_free[2], n.before(pj_free[2]))
            link(fn(fa[64:100, :], fz[64:100, :], ACT.Abs))
            link(fn(fa[64:100, :], fa[64:100, :], EXP, scale=-1.0))
            link(fn(lgt[:, :], lg[:, :], ACT.Abs))
            link(fn(lgt[:, :], lgt[:, :], EXP, scale=-1.0))
            link(fn(lgt[:, :], lgt[:, :], ACT.Ln, bias=1.0))
            link(fn(fa[64:100, :], fa[64:100, :], ACT.Ln, bias=1.0), gates_logs)
            s = slot()
            for c in range(3):
                evacuate(s, c, qT[:, tg(c)])
            act.wait_ge(gates_rows, 1)
            act.dma_start(a["new_m"][0], mr[0:4, CTX - 1:CTX]).then_inc(m_stored, 16)
            act.dma_start(a["new_m"][1], mr[32:36, 0:1]).then_inc(m_stored, 16)
            link(fn(ur, ur, EXP))
            link(fn(lf, mr, EXP, scale=-1.0))
            link(fn(ms[:, 1, :], ms[:, 1, :], EXP), gates_exp)
            for dest, scale in ((kT, DK ** -0.5), (vT, 1.0)):
                s = slot()
                for c in range(3):
                    evacuate(s, c, dest[:, tg(c)], scale)
            for i in range(3):
                full(i)
                fn(cols[i][:, :, :].rearrange("p c r -> p (c r)"), mb[i][:, 0:36 * NC], COPY).then_inc(mb_free[i], 1)
            full(3)
            fn(scb[:, :, :, :].rearrange("p r a c -> p (r a c)"), mb[3][:, 0:8 * 18], COPY).then_inc(mb_free[3], 1)
            act.wait_ge(m_stored, 32)
            link(fn(tick[:, :], eps[:, :], COPY), cols_ready)
            head_even(True, 0, True)
            with n.loop(act, "act.mlstm", 3) as turn:
                head_even(True, turn + 1, True)
            with n.loop(act, "act.ret", 3) as turn:
                head_even(False, turn, True)
            head_even(False, 3, False)
            boundary(project_out(), a["x"], 0, 1)
            boundary(ffn(0), x_saved_dram, 1, 0)
            act.wait_ge(xl_ready, n.before(xl_ready))
            act.dma_start(w2, a["w2"]).then_inc(mix_loaded, 16)
            act.dma_start(b2[:, :, :], a["b2"]).then_inc(mix_loaded, 16)
            act.wait_ge(x_saved, n.before(x_saved))
            s = slot()
            for c in range(3):
                evacuate(s, c, glr[:, tg(c)])
            for b in range(4):
                s = slot()
                if b >= 2:
                    act.wait_ge(la_free, n.next(la_free))
                for c in range(3):
                    out, scale = ((oq[:, tg(c)], DK ** -0.5), (ok[:, tg(c)], 1.0),
                                  (ov[:, 0, tg(c)], 1.0), (ov[:, 1, tg(c)], 1.0))[b]
                    evacuate(s, c, out, scale)
                if b < 2:
                    gate_logits(b)
                    gate_logs(b)
            head_odd(0, True)
            with n.loop(act, "act.odd", 2) as turn:
                head_odd(turn + 1, True)
            head_odd(3, False)
            boundary(project_out(), x_saved_dram, 1, 1)
            boundary(ffn(1), x_saved_dram, None, None)
            act.wait_ge(out_stored, 48)
            act.wait_ge(so_stored, 16 * 2 * 12)
            for g in range(3):
                act.wait_ge(h_stored[g], n.before(h_stored[g]))
            act.wait_ge(x_saved, n.before(x_saved))

        @block.vector
        def _(dve):
            n = Tally()
            blocks = {"n": 0}
            v = nc.vector

            def link(ins, done=dve_order):
                ins.then_inc(done, 1)
                dve.wait_ge(done, n.next(done))

            def give(ins, free):
                ins.then_inc(free, 1)
                n.next(free)

            def settle(done=dve_order):
                link(v.tensor_copy(tickv[:, :], eps[:, :]), done)

            def slot():
                blocks["n"] += 1
                return (blocks["n"] - 1) % 2

            def passes(count):
                for _ in range(count):
                    n.next(w_used[slot()])
                    n.next(pj_full[0])
                    n.next(pj_full[1])

            def full(i):
                dve.wait_ge(mb_full[i], n.next(mb_full[i]))

            def acts(i, uses=1):
                n.next(mb_full[i], uses)

            def tg(c):
                return slice(c * TG, (c + 1) * TG)

            def sum_squares(norm):
                dve.wait_ge(gram_full, n.next(gram_full))
                link(v.tensor_tensor(diag[:, :, :], g3(mb[GRAM_BANK[norm]][:, 0:TG]), chunk_row(ident[:, :], 3), ALU.mult))
                link(v.tensor_reduce(sumsq[:, norm, :], diag[:, :, :], AX.X, ALU.add), sum_ready)

            def inverse_rms(norm):
                dve.wait_ge(std_ready, n.next(std_ready))
                link(v.reciprocal(rstd[:, norm, :], std[:, norm, :]), rstd_ready)

            def over_tiles(norm):
                dve.wait_ge(rb_full, n.next(rb_full))
                return mb[NORM_BANK[norm]][:, 0:TG].rearrange("p (o i) -> p o i", o=1).broadcast_to([128, KT, TG])

            def coefs_in(layer, part):
                c0 = mod_column(layer, 3 * part + 1, 0)
                link(v.scalar_tensor_tensor(coef_in[:, :, :], mod[:, c0:c0 + KT, :], 1.0, b3(gains[:, 2 * part, layer, :], 2),
                                            ALU.add, ALU.mult), coef_ready)

            def coefs_out(layer, part):
                g = gains[:, 2 * part + 1, layer, :]
                for k0, k1 in ((0, 4), (4, 8)):
                    c0 = mod_column(layer, 3 * part + 2, k0)
                    link(v.tensor_tensor(coef_out[:, k0:k1, :], mod[:, c0:c0 + 4, :], b3(g[:, k0:k1], 2), ALU.mult))

            def normed(norm, g):
                link(v.tensor_tensor(xt[:, :, tg(g)], y[:, :, tg(g)], over_tiles(norm), ALU.mult), t_ready)

            def lower(g):
                for q in range(4):
                    dve.wait_ge(xh_ready, n.next(xh_ready))
                    two = slice(2 * q, 2 * q + 2)
                    link(v.tensor_tensor(xl[:, two, tg(g)], xt[:, two, tg(g)], xh[:, two, tg(g)].bitcast(f32),
                                         ALU.subtract), xl_ready)

            def post(norm, g):
                link(v.tensor_tensor(y[:, :, tg(g)], y[:, :, tg(g)], over_tiles(norm), ALU.mult))
                dve.wait_ge(xg_loaded[g], n.next(xg_loaded[g], 16))
                at = g * TG
                for col, lo, hi in ((0, 0, CTX), (1, CTX, TG)) if g == 0 else ((1, 0, TG),):
                    for k in range(KT):
                        v.scalar_tensor_tensor(y[:, k, at + lo:at + hi], y[:, k, at + lo:at + hi], coef_out[:, k, col:col + 1],
                                               xg[g][:, k, lo:hi], ALU.mult, ALU.add)
                settle(x_new)

            def boundary(last_part, layer, part, following):
                coefs_out(layer, part)
                if following is not None:
                    coefs_in(*following)
                last_part(0)
                last_part(1)
                sum_squares(0)
                inverse_rms(0)
                post(0, 0)
                last_part(2)
                sum_squares(1)
                inverse_rms(1)
                post(1, 1)
                if following is None:
                    sum_squares(3)
                    inverse_rms(3)
                    post(3, 2)
                    return
                sum_squares(2)
                sum_squares(3)
                inverse_rms(2)
                inverse_rms(3)
                normed(2, 0)
                post(3, 2)
                sum_squares(4)
                inverse_rms(4)
                lower(0)
                normed(4, 1)
                sum_squares(5)
                inverse_rms(5)
                normed(5, 2)
                lower(1)
                lower(2)

            def conditioning(column):
                dve.wait_ge(ada_used, n.next(ada_used, 4))
                give(v.tensor_tensor(mod[:, bass.ds(column, 4), :], mb[4][:, 0:8].rearrange("p (c g) -> p c g", g=2),
                                     b3(ada_b[:, bass.ds(column, 4)], 2), ALU.add), mb_free[4])

            def bcast(col, g):
                return b3(col[:, 3 * g:3 * g + 3], CH)

            def set_head_mlstm(h):
                for d in range(2):
                    for i in range(3):
                        link(v.tensor_copy(hcol[:, i, d, :], cols[i][:, :, h + 32 * d]))
                    link(v.tensor_copy(hsc[:, d, :, :], scb[:, h + 4 * d, :, :]))
                    link(v.tensor_copy(sel[:, d, :], ident[0:36, bass.ds(h + 32 * d, 1)].broadcast_to([36, 128])),
                         head_set if d else dve_order)

            def set_head_ret(h):
                for d in range(2):
                    link(v.tensor_copy(rlg[:, d:d + 1], lg[:, bass.ds(h + 4 * d, 1)]), head_set if d else dve_order)
                dve.wait_ge(ret_rows, n.next(ret_rows))
                for d in range(2):
                    link(v.tensor_tensor(rt[:, 2 + d, :], rt[:, 2 + d, :], m01[:, d, :], ALU.mult))
                link(v.tensor_tensor(rt[:, 2, :], rt[:, 2, :], rt[:, 3, :], ALU.add))

            def front_mlstm(g):
                r = slice(3 * g, 3 * g + 3)
                full(0)
                for d, done in ((0, link), (1, give)):
                    done(v.tensor_tensor(kw[d][:, r, :], g3(mb[0][:, 0:TG]), bcast(hcol[:, 1, d, :], g), ALU.mult),
                         mb_free[0] if d else dve_order)
                acts(1)
                acts(3)
                acts(4)
                dve.wait_ge(q_decay, n.next(q_decay, 6))
                for d in range(2):
                    link(v.tensor_tensor(tm[d][:, :, :], cb[d][:, :, :], chunk_row(far[:, d, :], 3), ALU.add), e_masked)
                full(2)
                dve.wait_ge(e_ready, n.next(e_ready, 6))
                for d, done in ((0, link), (1, give)):
                    done(v.tensor_tensor(pr[d][:, r, :], pr[d][:, r, :], g3(mb[2][:, 0:TG]), ALU.mult), mb_free[2] if d else dve_order)
                for d in range(2):
                    link(v.tensor_tensor(qw[d][:, r, :], qw[d][:, r, :], g3(qT[:, tg(g)]), ALU.mult), front_done if d else dve_order)

            def front_ret(g):
                r = slice(3 * g, 3 * g + 3)
                full(0)
                for d, done in ((0, link), (1, give)):
                    done(v.tensor_scalar(kw[d][:, r, :], g3(mb[0][:, 0:TG]), rw[:, 0, d:d + 1], None, ALU.mult),
                         mb_free[0] if d else dve_order)
                acts(1)
                full(2)
                give(v.tensor_tensor(pr[0][:, r, :], chunk_row(rt[:, 2, :], 3), g3(mb[2][:, 0:TG]), ALU.mult), mb_free[2])
                for d in range(2):
                    link(v.tensor_tensor(qw[d][:, r, :], chunk_row(rt[:, d, :], 3), g3(qT[:, tg(g)]), ALU.mult), front_done if d else dve_order)

            def states_even(mlstm):
                w = 129 if mlstm else 128
                for t in range(8):
                    i = t % 2
                    full(i)
                    if t == 0:
                        dve.wait_ge(so_stored, n.before(so_stored))
                        n.next(so_stored, 32)
                        link(v.tensor_copy(st[0][:, 0, 0:w], mb[0][:, 0:w]), so_ready)
                        give(v.tensor_copy(st[1][:, 0, 0:w], mb[0][:, 129:129 + w]), mb_free[0])
                        continue
                    if t == 1:
                        dve.wait_ge(st_loaded, n.next(st_loaded, 32))
                    for d, (c, to) in enumerate(((t, t + 1), (NC - t, NC - t - 1))):
                        decay = hsc[:, d, 1, c:c + 1] if mlstm else rw[:, 1, d:d + 1]
                        done = mb_free[i] if d else so_ready if t == 1 else dve_order
                        (give if d else link)(v.scalar_tensor_tensor(st[d][:, to, 0:w], st[d][:, c, 0:w], decay, mb[i][:, 129 * d:129 * d + w],
                                                    ALU.mult, ALU.add), done)

            def head_norm(o, square, width):
                link(v.tensor_tensor(square, o, o, ALU.mult))
                link(v.tensor_reduce(hss[:, :], square, AX.X, ALU.add), ss_ready)
                dve.wait_ge(hstd_ready, n.next(hstd_ready))
                link(v.reciprocal(hrs[:, :], hstd[:, :]))
                link(v.tensor_tensor(o, o, b3(hrs[:, :], width), ALU.mult), o_ready)

            def gated(g, bank, gate, dest):
                full(bank)
                dve.wait_ge(h_stored[g], n.before(h_stored[g]))
                n.next(h_stored[g], 16)
                link(v.tensor_tensor(dest[g][:, :], mb[bank][:, 0:TG], gate, ALU.mult), hout_ready)

            def head_even(mlstm, h, ada_turn):
                if mlstm:
                    set_head_mlstm(h)
                else:
                    set_head_ret(h)
                for g in range(3):
                    (front_mlstm if mlstm else front_ret)(g)
                states_even(mlstm)
                acts(2, 5)
                acts(3, 4)
                n.next(mb_free[2], 5)
                dve.wait_ge(mb_free[2], n.before(mb_free[2]))
                o = num[:, :, 0, 0:CH]
                if mlstm:
                    link(v.scalar_tensor_tensor(den[:, :, :], num[:, :, :, 128], -1.0, num[:, :, :, 128], ALU.mult, ALU.max))
                    link(v.tensor_tensor(den[:, :, :], den[:, :, :], hcol[:, 2, :, :].rearrange("p d c -> p c d"), ALU.max))
                    link(v.reciprocal(rr[:, :, :], den[:, :, :]))
                    for d in range(2):
                        link(v.tensor_tensor(num[:, :, d, 0:CH], num[:, :, d, 0:CH], b3(rr[:, :, d], CH), ALU.mult))
                    link(v.tensor_tensor(o, o, num[:, :, 1, 0:CH], ALU.add))
                head_norm(o, num[:, :, 1, 0:CH], CH)
                conditioning(ada_turn)
                dve.wait_ge(gate_ready, n.next(gate_ready))
                for g, bank in enumerate((4, 0, 1)):
                    gated(g, bank, gT[:, tg(g)], hout)

            def set_gates_odd(h):
                link(v.tensor_copy(b2s[:, :], b2[:, :, h]))
                link(v.tensor_copy(w2s, ada_w[0:48, bass.ds(h * 128, 128)]), w2_set)

            def log_decay(d):
                sum_logs(d)
                center_logs(d)

            def sum_logs(d):
                dve.wait_ge(z_logs, n.next(z_logs))
                link(v.scalar_tensor_tensor(la[d][:, :], bb[d][:, :], 0.0, la[d][:, :], ALU.min, ALU.subtract))
                if d == 0:
                    link(v.tensor_tensor_scan(bb[0][:, :], rst[:, 0:T], la[0][:, :], 0.0, ALU.mult, ALU.add), la_free)
                else:
                    link(v.tensor_tensor_scan(bb[1][:, T - 1::-1], rst[:, T:0:-1], la[1][:, T - 1::-1], 0.0, ALU.mult, ALU.add), la_free)

            def center_logs(d):
                last, mid = (CH - 1, CH // 2 - 1) if d == 0 else (0, CH // 2)
                link(v.tensor_copy(bm[:, d, 0, :], bb[d][:, last::CH]))
                link(v.tensor_copy(bm[:, d, 2, :], bb[d][:, mid::CH]))
                link(v.tensor_tensor(bm[:, d, 1, :], bm[:, d, 0, :], bm[:, d, 2, :], ALU.subtract))
                link(v.tensor_tensor(g3(bb[d][:, :]), g3(bb[d][:, :]), b3(bm[:, d, 2, :], CH), ALU.subtract), bb_ready)

            def front_odd(g):
                r = slice(3 * g, 3 * g + 3)
                for i in range(2):
                    full(2 + i)
                    if g == 0 and i == 0:
                        for x in range(3):
                            dve.wait_ge(h_stored[x], n.before(h_stored[x]))
                    give(v.tensor_copy(vt[:, r, 128 * i:128 * i + 128], g3(mb[2 + i][:, 0:TG])), mb_free[2 + i])
                dve.wait_ge(eg_ready, n.next(eg_ready, 4))
                for d in range(2):
                    link(v.tensor_tensor(qe[d][:, r, :], qe[d][:, r, :], g3(oq[:, tg(g)]), ALU.mult))
                    link(v.tensor_tensor(ke[d][:, :, :], ke[d][:, :, :], g3(ok[:, tg(g)]), ALU.mult), ke_ready if d else dve_order)
                acts(0)
                acts(1)
                for d in range(2):
                    i = 4 if d == 0 else 0
                    full(i)
                    v.memset(after[:, d:d + 1], 0.0)
                    give(v.copy_predicated(tp[d][:, :, :], chunk_row(m8[:, d, :], 3), g3(mb[i][:, 0:TG])), mb_free[i])
                settle()
                link(v.tensor_tensor(pg[:, r, :], tp[0][:, :, :], tp[1][:, :, :], ALU.add), front_done)

            def step_odd(t):
                if t == 0:
                    dve.wait_ge(so_stored, n.before(so_stored))
                    n.next(so_stored, 32)
                    dve.wait_ge(dc_ready, n.next(dc_ready))
                    for d in range(2):
                        full(d)
                        give(v.tensor_scalar(sgo[d][:, :], mb[d][:, 0:DVG], dc[:, d, 1, 0:1], None, ALU.mult), mb_free[d])
                    acts(2)
                    return
                now, then = t % 2, (t + 1) % 2
                if t == 1:
                    dve.wait_ge(st_loaded, n.next(st_loaded, 32))
                settle(sg_new)
                if t == 1:
                    settle(so_ready)
                    settle(so_ready)
                if t < 8:
                    for d, c in enumerate((t, NC - t)):
                        link(v.tensor_scalar(sgt[d][:, :], sg[d][now][:, :], dc[:, d, 0, c:c + 1], None, ALU.mult))
                    if t > 1:
                        dve.wait_ge(sd_ready, n.next(sd_ready, 2))
                    for d, c in enumerate((t, NC - t)):
                        full(d)
                        give(v.scalar_tensor_tensor(sg[d][then][:, :], mb[d][:, 0:DVG], dc[:, d, 1, c:c + 1], sgt[d][:, :],
                                                    ALU.mult, ALU.add), mb_free[d])
                else:
                    n.next(sd_ready, 4)
                for i, c in ((2, t), (3, NC - t)):
                    if t <= 4:
                        acts(i)
                    else:
                        full(i)
                        give(v.tensor_tensor(og[:, c, :], og[:, c, :], mb[i][:, 0:DVG], ALU.add), mb_free[i])

            def head_odd(h, follows):
                for g in range(3):
                    front_odd(g)
                if follows:
                    set_gates_odd(h + 1)
                for t in range(NC):
                    step_odd(t)
                    if t == 1 and follows:
                        acts(4, 6)
                    if t in (4, 7) and follows:
                        sum_logs(t // 7)
                    if t == 5 and follows:
                        center_logs(0)
                settle()
                head_norm(og[:, :, :], kt[:, :, :, :].rearrange("p d c n -> p (d c n)").rearrange("p (c n) -> p c n", n=DVG), DVG)
                if follows:
                    center_logs(1)
                dve.wait_ge(gate_ready, n.next(gate_ready))
                for m, bank in enumerate((4, 0, 1, 2, 3, 4)):
                    gated(m % 3, bank, ogate[:, m // 3, tg(m % 3)], oh)

            def project_out():
                for g in range(3):
                    dve.wait_ge(h_stored[g], n.before(h_stored[g]))
                for k in range(KT):
                    s = k % 2
                    dve.wait_ge(xr_loaded[s], n.next(xr_loaded[s], 16))
                    dve.wait_ge(xh_ready, n.next(xh_ready))
                    link(v.tensor_tensor(xl[:, k, :], xr[s][:, :], xh[:, k, :].bitcast(f32), ALU.subtract), xl_ready)
                passes(KT)
                return lambda c: None

            def conv_tap(t, tap):
                grid = tap < 9
                i, j = (tap // 3, tap % 3) if grid else (1, tap - 9)
                first = tap in (0, 9)
                if grid:
                    src = pad[t][:, i:i + ROWS, j:j + GRID_W]
                    dst = cc[t][:, CTX:T].rearrange("p (r w) -> p r w", w=GRID_W)
                else:
                    src, dst = padc[t][:, j:j + CTX], cc[t][:, 0:CTX]
                w = cw[:, t, 3 * i + j:3 * i + j + 1]
                done = conv_done if tap == 11 else dve_order
                if tap == 0:
                    dve.wait_ge(a_padded, n.next(a_padded))
                if first:
                    link(v.tensor_scalar(dst, src, w, None, ALU.mult), done)
                else:
                    link(v.scalar_tensor_tensor(dst, src, w, dst, ALU.mult, ALU.add), done)

            def value(t, s):
                dve.wait_ge(gelu_done, n.next(gelu_done))
                for c in range(3):
                    full_ = w_used[s] if c == 2 else pj_full[c]
                    dve.wait_ge(full_, n.next(full_))
                    give(v.tensor_tensor(cc[t][:, tg(c)], cc[t][:, tg(c)], pj[c][:, 0:TG], ALU.mult), pj_free[c])
                dve.wait_ge(hh_ready, n.next(hh_ready))
                link(v.tensor_tensor(hl[:, t, :], cc[t][:, :], hh[:, t, :].bitcast(f32), ALU.subtract), hl_ready)

            def act_takes(s):
                n.next(w_used[s])
                for c in range(2):
                    n.next(pj_full[c])

            def down():
                for half in range(2):
                    s = slot()
                    for m in range(4):
                        for c in range(3):
                            j = 12 * half + 3 * m + c
                            i = j % 4
                            if m == 3 and c == 2:
                                dve.wait_ge(w_used[s], n.next(w_used[s]))
                            else:
                                full(i)
                            dst = y[:, 4 * half + m, tg(c)]
                            give(v.tensor_tensor(dst, dst, mb[i][:, 0:TG], ALU.add), mb_free[i])
                            if j % 2:
                                conv_tap(0, j // 2)

            def down_last():
                slots = (slot(), slot())

                def part(c):
                    for half, s in enumerate(slots):
                        for m in range(4):
                            i = m % 2
                            if m == 3 and c == 2:
                                dve.wait_ge(w_used[s], n.next(w_used[s]))
                            else:
                                full(i)
                            dst = y[:, 4 * half + m, tg(c)]
                            link(v.tensor_tensor(dst, dst, mb[i][:, 0:TG], ALU.add), y_new)
                return part

            def set_taps(p):
                link(v.tensor_copy(cw[:, :, :], conv[:, bass.ds(p * 2, 2), :]))

            def pair(turn, with_down, column, saved=0):
                set_taps(turn)
                act_takes(slot())
                if with_down:
                    down()
                else:
                    for tap in range(12):
                        conv_tap(0, tap)
                    dve.wait_ge(x_saved, saved)
                    link(v.memset(y[:, :, :], 0.0))
                value(0, slot())
                act_takes(slot())
                for tap in range(12):
                    conv_tap(1, tap)
                value(1, slot())
                if column is not None:
                    conditioning(column)

            def ffn(layer):
                for t in range(2):
                    link(v.memset(pad[t][:, :, :], 0.0))
                    link(v.memset(padc[t][:, :], 0.0), pads_clear if t else dve_order)
                dve.wait_ge(conv_loaded, n.next(conv_loaded, 16))
                column = 52 if layer == 0 else None
                pair(0, False, column, saved=48 if layer == 0 else 3 * 48)
                with n.loop(dve, f"dve.ffn{layer}", FP - 1) as turn:
                    pair(turn + 1, True, None if column is None else turn * 4 + 56)
                return down_last()

            dve.wait_ge(consts_made, 1)
            link(v.tensor_copy(m8[:, :, :], m01[:, :, :]))
            for norm, g in ((2, 0), (4, 1), (5, 2)):
                sum_squares(norm)
                inverse_rms(norm)
                normed(norm, g)
            dve.wait_ge(small_loaded, 48)
            dve.wait_ge(front_used, ADA_FRONT)
            give(v.tensor_tensor(mod[:, 0:ADA_FRONT, :], mb[4][:, 0:2 * ADA_FRONT].rearrange("p (c g) -> p c g", g=2),
                                 b3(ada_b[:, 0:ADA_FRONT], 2), ALU.add), mb_free[4])
            dve.wait_ge(mb_free[4], n.before(mb_free[4]))
            coefs_in(0, 0)
            for g in range(3):
                lower(g)

            dve.wait_ge(gates_logs, 1)
            link(v.scalar_tensor_tensor(lf, fz[64:100, :], 0.0, fa[64:100, :], ALU.min, ALU.subtract))
            link(v.scalar_tensor_tensor(lg[:, :], lg[:, :], 0.0, lgt[:, :], ALU.min, ALU.subtract))
            link(v.memset(jr, 0.0))
            link(v.tensor_tensor_scan(fc[0:32, :], rst[0:32, 0:T], lf[0:32, :], 0.0, ALU.mult, ALU.add))
            link(v.tensor_tensor_scan(fc[32:36, T - 1::-1], rst[32:36, T:0:-1], lf[32:36, T - 1::-1], 0.0, ALU.mult, ALU.add))
            link(v.tensor_tensor(gr, ig, fc, ALU.subtract))
            link(v.tensor_copy(jr[0:32, 2 * CH:T:CH], fc[0:32, 2 * CH - 1:T - 1:CH]))
            link(v.tensor_copy(jr[32:36, 2 * CH - 1:T - 1:CH], fc[32:36, 2 * CH:T:CH]))
            link(v.tensor_tensor_scan(crow[0:32, 0:CTX], jr[0:32, 0:CTX], gr[0:32, 0:CTX], 0.0, ALU.add, ALU.max))
            link(v.tensor_tensor_scan(crow[0:32, CTX:T], jr[0:32, CTX:T], gr[0:32, CTX:T], m0[0:32, :], ALU.add, ALU.max))
            link(v.tensor_tensor_scan(crow[32:36, CTX - 1::-1], jr[32:36, CTX - 1::-1], gr[32:36, CTX - 1::-1], 0.0, ALU.add, ALU.max))
            link(v.tensor_tensor_scan(crow[32:36, T - 1:CTX - 1:-1], jr[32:36, T - 1:CTX - 1:-1], gr[32:36, T - 1:CTX - 1:-1],
                                      m0[32:36, :], ALU.add, ALU.max))
            link(v.tensor_tensor(mr, fc, crow[:, :], ALU.add))
            link(v.memset(ms[:, :, :], 0.0))
            link(v.tensor_copy(ms[0:32, 0, 1:2], m0[0:32, :]))
            link(v.tensor_copy(ms[0:32, 0, 2:NC], mr[0:32, 2 * CH - 1:T - 1:CH]))
            link(v.tensor_copy(ms[32:36, 0, NC - 1:NC], m0[32:36, :]))
            link(v.tensor_copy(ms[32:36, 0, 1:NC - 1], mr[32:36, 2 * CH:T:CH]))
            link(v.tensor_copy(cl[0:32, :], crow[0:32, CH - 1:T:CH]))
            link(v.tensor_copy(cl[32:36, :], crow[32:36, 0:T:CH]))
            link(v.tensor_tensor(ms[:, 1, :], ms[:, 0, :], cl[:, :], ALU.subtract))
            link(v.tensor_tensor(g3(ur), g3(gr), b3(cl[:, :], CH), ALU.subtract), gates_rows)
            conditioning(ADA_FRONT)
            dve.wait_ge(cols_ready, 1)
            link(v.memset(v1[:, :, 128:129], 1.0))
            for i in range(4):
                acts(i)
            n.next(mb_free[2])
            head_even(True, 0, ADA_FRONT + 4)
            with n.loop(dve, "dve.mlstm", 3) as turn:
                head_even(True, turn + 1, turn * 4 + (ADA_FRONT + 8))
            with n.loop(dve, "dve.ret", 3) as turn:
                head_even(False, turn, turn * 4 + 36)
            head_even(False, 3, 48)
            passes(4 + 7 * 4 + 1)
            boundary(project_out(), 0, 0, (0, 1))
            boundary(ffn(0), 0, 1, (1, 0))
            dve.wait_ge(mix_loaded, 48 + 32)
            set_gates_odd(0)
            for d in range(2):
                link(v.memset(tp[d][:, :, :], 0.0))
            acts(4, 6)
            log_decay(0)
            log_decay(1)
            head_odd(0, True)
            with n.loop(dve, "dve.odd", 2) as turn:
                head_odd(turn + 1, True)
            head_odd(3, False)
            passes(5 + 3 * 6 + 2)
            boundary(project_out(), 1, 0, (1, 1))
            boundary(ffn(1), 1, 1, None)

def even_blocks(w_in):
    gates = np.zeros((D, 128), w_in.dtype)
    for to, off in ((0, 0), (32, 8), (64, 4), (96, 12)):
        gates[:, to:to + 4] = w_in[:, 2048 + off:2052 + off]

    def head(h, part):
        base = 512 * part + (0 if h < 4 else 2064)
        return w_in[:, base + 128 * (h % 4):base + 128 * (h % 4) + 128]
    blocks = [gates] + [head(0, p) for p in range(3)]
    for h in range(8):
        blocks.append(head(h, 3))
        if h < 7:
            blocks += [head(h + 1, p) for p in range(3)]
    return blocks


def odd_blocks(w_in):
    low = np.zeros((D, 128), w_in.dtype)
    low[:, 0:RANK] = w_in[:, 3072:3072 + RANK]
    low[:, 32:32 + RANK] = w_in[:, 3072 + RANK:3072 + 2 * RANK]

    def cols(at):
        return w_in[:, at:at + 128]

    def qkv(h):
        return [cols(128 * h), cols(512 + 128 * h), cols(1024 + 256 * h), cols(1024 + 256 * h + 128)]
    blocks = [low] + qkv(0)
    for h in range(4):
        blocks += [cols(2048 + 256 * h), cols(2048 + 256 * h + 128)]
        if h < 3:
            blocks += qkv(h + 1)
    return blocks


def by_features(w):
    return w.reshape(KT, 128, 128).transpose(1, 0, 2).reshape(128, 1024)


def ffn_blocks(w_in, w_out):
    def a_(t):
        return by_features(w_in[:, 128 * t:128 * t + 128])

    def v_(t):
        return by_features(w_in[:, D_FF + 128 * t:D_FF + 128 * t + 128])

    def down(p):
        pair = w_out[256 * p:256 * p + 256].reshape(2, 128, 2, 512)
        return [pair[:, :, half].transpose(1, 0, 2).reshape(128, 1024) for half in range(2)]
    blocks = []
    for p in range(FP):
        blocks.append(a_(2 * p))
        if p:
            blocks += down(p - 1)
        blocks += [v_(2 * p), a_(2 * p + 1), v_(2 * p + 1)]
    return blocks + down(FP - 1)


_OUTS = {"out_x": (128, KT, T), "new_mlstm": (2, 4, 128, 129), "new_m": (2, 4, 1),
         "new_ret": (2, 4, 128, 128), "new_gla": (2, 4, 128, DVG)}


def kernel(x_prompt, x_sample, c, c_ctx, state_mlstm_C, state_mlstm_n, state_mlstm_m, state_ret,
           state_gla, ada_w, ada_b, norm_mix_pre, norm_mix_post, norm_ffn_pre, norm_ffn_post,
           w_in_even, w_out_even, mlstm_igate_b, mlstm_fgate_b, ret_decay_logit,
           w_in_odd, gla_gate_w2, gla_gate_b, w_out_odd,
           ffn_w_in, ffn_conv_w, ffn_conv_b, ffn_w_out):
    import concourse.bacc as bacc
    from concourse.bass_utils import run_bass_kernel_spmd

    f = np.float32
    tokens = np.concatenate([np.asarray(x_prompt)[0], np.asarray(x_sample)[0]], 0)
    arrays = {"x": tokens.T.reshape(KT, 128, T).transpose(1, 0, 2)}
    arrays["cond"] = np.stack([np.asarray(c_ctx), np.asarray(c)[0]], 1).reshape(KT, 128, 2).transpose(1, 0, 2)
    ada_w, ada_b = np.asarray(ada_w), np.asarray(ada_b)
    ada = np.zeros((96, 128, 1024), ada_w.dtype)
    bias = np.zeros((128, 96), ada_b.dtype)
    for layer in range(2):
        for part in range(6):
            for k in range(KT):
                at, j = mod_column(layer, part, k), 8 * part + k
                ada[at] = by_features(ada_w[layer][:, 128 * j:128 * j + 128])
                bias[:, at] = ada_b[layer][128 * j:128 * j + 128]
    arrays["ada"], arrays["ada_b"] = ada, bias
    arrays["gains"] = np.stack([np.asarray(g).reshape(2, KT, 128) for g in
                                (norm_mix_pre, norm_mix_post, norm_ffn_pre, norm_ffn_post)]).transpose(3, 0, 1, 2)
    w_in, w_out = np.asarray(ffn_w_in), np.asarray(ffn_w_out)
    blocks = [by_features(w) for w in even_blocks(np.asarray(w_in_even)[0])]
    blocks += [by_features(np.asarray(w_out_even)[0][:, 128 * m:128 * m + 128]) for m in range(KT)]
    blocks += ffn_blocks(w_in[0], w_out[0])
    blocks += [by_features(w) for w in odd_blocks(np.asarray(w_in_odd)[0])]
    blocks += [by_features(np.asarray(w_out_odd)[0][:, 128 * m:128 * m + 128]) for m in range(KT)]
    blocks += ffn_blocks(w_in[1], w_out[1])
    arrays["w"] = np.stack(blocks)
    gbias = np.zeros((128, 2), f)
    m0 = np.zeros((36, 1), f)
    for d in range(2):
        gbias[32 * d:32 * d + 4, 0] = np.asarray(mlstm_igate_b)[0, d]
        gbias[64 + 32 * d:68 + 32 * d, 1] = np.asarray(mlstm_fgate_b)[0, d]
        m0[32 * d:32 * d + 4, 0] = np.asarray(state_mlstm_m)[0, 0, d]
    arrays["gbias"], arrays["m0"] = gbias, m0
    arrays["ret_logit"] = np.broadcast_to(np.asarray(ret_decay_logit)[0].reshape(1, 8), (128, 8))
    arrays["st_mlstm"] = np.concatenate([np.asarray(state_mlstm_C)[0, 0], np.asarray(state_mlstm_n)[0, 0][..., None]], -1)
    arrays["st_ret"] = np.asarray(state_ret)[0, 0]
    arrays["st_gla"] = np.asarray(state_gla)[0, 0]
    w2 = np.zeros((48, 512), f)
    w2[0:RANK], w2[32:32 + RANK] = np.asarray(gla_gate_w2)[0, 0], np.asarray(gla_gate_w2)[0, 1]
    arrays["w2"] = w2
    arrays["b2"] = np.asarray(gla_gate_b)[0].reshape(2, 4, 128).transpose(2, 0, 1)
    taps = np.concatenate([np.asarray(ffn_conv_w).reshape(2, 9, D_FF), np.asarray(ffn_conv_b)[:, None]], 1)
    arrays["conv"] = taps.reshape(2, 10, FT, 128).transpose(0, 3, 2, 1)

    nc = bacc.Bacc("TRN2", target_bir_lowering=False, num_devices=1)
    args, feed = {}, {}
    for name, array in arrays.items():
        array = np.ascontiguousarray(array)
        feed[f"in_{name}"] = array
        args[name] = nc.dram_tensor(f"in_{name}", array.shape, mybir.dt.from_np(array.dtype), kind="ExternalInput").ap()
    for name, shape in _OUTS.items():
        args[name] = nc.dram_tensor(f"res_{name}", shape, mybir.dt.float32, kind="ExternalOutput").ap()
    build(nc, args)
    r = run_bass_kernel_spmd(nc, [feed], core_ids=[0])
    got = {name: r.results[0][f"res_{name}"] for name in _OUTS}
    y = got["out_x"].transpose(1, 0, 2).reshape(D, T).T
    states = got["new_mlstm"]
    return (np.ascontiguousarray(y[None, 0:CTX]), np.ascontiguousarray(y[None, CTX:T]),
            np.ascontiguousarray(states[None, None, ..., 0:128]), np.ascontiguousarray(states[None, None, ..., 128]),
            np.ascontiguousarray(got["new_m"][None, None, ..., 0]), got["new_ret"][None, None], got["new_gla"][None, None])
```
